# Optimizing a Trainium2 kernel written in Bass

```python
import math
import jax, jax.numpy as jnp
from jax import lax
import numpy as np

D_MODEL = 1024
BATCH = 1
SEQ = 1024
DEPTH = 1

MEM_LEN = 256
HEAD_DIM = 64
SWA_HEADS = 8
SWA_KV_HEADS = 2
WINDOW = 128
BLOCK = 128
N_BUCKETS = 32
MAX_DISTANCE = 128
GLA_HEADS = 4
GLA_DK = 32
GLA_DV = 64
GLA_RANK = 16
GLA_TAU = 16.0
GLA_CHUNK = 32
MEM_HEADS = 4
D_FF = 2816
EPS = 1e-6

SWA_Q_W = SWA_HEADS * HEAD_DIM
SWA_KV_W = SWA_KV_HEADS * HEAD_DIM
GLA_QK_W = GLA_HEADS * GLA_DK
GLA_V_W = GLA_HEADS * GLA_DV
MEM_Q_W = MEM_HEADS * HEAD_DIM
MIX_W = SWA_Q_W + GLA_V_W + MEM_Q_W
IN_SIZES = (SWA_Q_W, SWA_KV_W, SWA_KV_W, GLA_QK_W, GLA_QK_W, GLA_V_W, GLA_V_W, GLA_RANK, MEM_Q_W)
IN_W = SWA_Q_W + 2 * SWA_KV_W + 2 * GLA_QK_W + 2 * GLA_V_W + GLA_RANK + MEM_Q_W

kernel_name = "hymba_swa_sink_gla_memxattn_macaron"

def _split_points():
    return [int(s) for s in np.cumsum(IN_SIZES)[:-1]]

def rmsnorm(x, g):
    x32 = x.astype(jnp.float32)
    y = x32 * lax.rsqrt(jnp.mean(x32 * x32, axis=-1, keepdims=True) + EPS)
    return (y * g.astype(jnp.float32)).astype(x.dtype)

def swiglu(x, w_gate, w_up, w_down):
    return (jax.nn.silu(x @ w_gate) * (x @ w_up)) @ w_down

def t5_bucket(dist):
    max_exact = N_BUCKETS // 2
    d = jnp.maximum(dist, 1).astype(jnp.float32)
    large = max_exact + (jnp.log(d / max_exact) / math.log(MAX_DISTANCE / max_exact)
                         * (N_BUCKETS - max_exact)).astype(jnp.int32)
    large = jnp.minimum(large, N_BUCKETS - 1)
    return jnp.where(dist < max_exact, dist, large)

def swa_attention(q, k, v, q_gain, k_gain, sinks, rel_bias):
    B, S = q.shape[0], q.shape[1]
    nb = S // BLOCK
    G = SWA_HEADS // SWA_KV_HEADS
    q = rmsnorm(q, q_gain)
    k = rmsnorm(k, k_gain)
    qb = q.reshape(B, nb, BLOCK, SWA_KV_HEADS, G, HEAD_DIM)
    pad = jnp.zeros((B, BLOCK, SWA_KV_HEADS, HEAD_DIM), k.dtype)

    def band(t):
        tp = jnp.concatenate([pad, t], axis=1).reshape(B, nb + 1, BLOCK, SWA_KV_HEADS, HEAD_DIM)
        return jnp.concatenate([tp[:, :-1], tp[:, 1:]], axis=2)

    kb, vb = band(k), band(v)
    scores = jnp.einsum('bnqhgd,bnkhd->bhgnqk', qb, kb).astype(jnp.float32) * (HEAD_DIM ** -0.5)

    qi = jnp.arange(BLOCK)[:, None]
    kj = jnp.arange(2 * BLOCK)[None, :]
    dist = qi + BLOCK - kj
    in_win = (dist >= 0) & (dist < WINDOW)
    key_pos = jnp.arange(nb)[:, None, None] * BLOCK - BLOCK + kj[None]
    valid = in_win[None] & (key_pos >= 0)

    bias = rel_bias[t5_bucket(jnp.maximum(dist, 0))].astype(jnp.float32)
    bias = bias.transpose(2, 0, 1).reshape(SWA_KV_HEADS, G, BLOCK, 2 * BLOCK)
    scores = scores + bias[:, :, None]
    scores = jnp.where(valid[None, None, None], scores, -jnp.inf)

    sink = sinks.astype(jnp.float32).reshape(SWA_KV_HEADS, G)[None, :, :, None, None, None]
    m = jnp.maximum(jnp.max(scores, axis=-1, keepdims=True), sink)
    p = jnp.exp(scores - m)
    p = p / (jnp.sum(p, axis=-1, keepdims=True) + jnp.exp(sink - m))
    out = jnp.einsum('bhgnqk,bnkhd->bnqhgd', p.astype(v.dtype), vb)
    return out.reshape(B, S, SWA_Q_W)

def gla(q, k, v, out_gate, gate_lr, w_gate_up, b_gate, norm_gain):
    B, S = q.shape[0], q.shape[1]
    N, C = S // GLA_CHUNK, GLA_CHUNK
    log_a = jax.nn.log_sigmoid((gate_lr @ w_gate_up + b_gate).astype(jnp.float32)) / GLA_TAU

    def chunked(t, d):
        return t.astype(jnp.float32).reshape(B, N, C, GLA_HEADS, d).transpose(0, 3, 1, 2, 4)

    qc = chunked(q, GLA_DK) * (GLA_DK ** -0.5)
    kc = chunked(k, GLA_DK)
    vc = chunked(v, GLA_DV)
    b = jnp.cumsum(chunked(log_a, GLA_DK), axis=3)

    causal = jnp.tril(jnp.ones((C, C), dtype=bool))
    diff = b[..., :, None, :] - b[..., None, :, :]
    decay = jnp.exp(jnp.where(causal[:, :, None], diff, -jnp.inf))
    A = jnp.sum(qc[..., :, None, :] * kc[..., None, :, :] * decay, axis=-1)
    o_intra = jnp.einsum('bhnij,bhnjd->bhnid', A, vc)

    b_last = b[..., -1:, :]
    chunk_kv = jnp.einsum('bhncd,bhnce->bhnde', kc * jnp.exp(b_last - b), vc)
    chunk_decay = jnp.exp(b_last[..., 0, :])

    def step(state, inp):
        dec, kv = inp
        return dec[..., None] * state + kv, state

    s0 = jnp.zeros((B, GLA_HEADS, GLA_DK, GLA_DV), jnp.float32)
    _, s_prev = lax.scan(step, s0, (jnp.moveaxis(chunk_decay, 2, 0), jnp.moveaxis(chunk_kv, 2, 0)))
    s_prev = jnp.moveaxis(s_prev, 0, 2)
    o_inter = jnp.einsum('bhncd,bhnde->bhnce', qc * jnp.exp(b), s_prev)

    o = (o_intra + o_inter).transpose(0, 2, 3, 1, 4).reshape(B, S, GLA_HEADS, GLA_DV)
    o = rmsnorm(o, norm_gain).reshape(B, S, GLA_V_W)
    return (o * jax.nn.silu(out_gate.astype(jnp.float32))).astype(q.dtype)

def memory_attention(q, k, v, q_gain, k_gain):
    B, S = q.shape[0], q.shape[1]
    q = rmsnorm(q, q_gain)
    k = rmsnorm(k, k_gain)
    s = jnp.einsum('bshd,bmhd->bhsm', q, k).astype(jnp.float32) * (HEAD_DIM ** -0.5)
    p = jax.nn.softmax(s, axis=-1)
    out = jnp.einsum('bhsm,bmhd->bshd', p.astype(v.dtype), v)
    return out.reshape(B, S, MEM_Q_W)

def _normal(k, shape, scale):
    return jax.random.normal(k, shape, jnp.float32) * scale

def _gain(k, shape):
    return 1.0 + 0.05 * jax.random.normal(k, shape, jnp.float32)

def setup_inputs(seed: int = 0) -> dict:
    key = jax.random.key(seed)
    ks = jax.random.split(key, 24)
    L, D = DEPTH, D_MODEL
    return {
        "x": _normal(ks[0], (BATCH, SEQ, D), 1.0),
        "mem": _normal(ks[1], (BATCH, MEM_LEN, D), 1.0),
        "ffn1_norm": _gain(ks[2], (L, D)),
        "ffn1_w_gate": _normal(ks[3], (L, D, D_FF), D ** -0.5),
        "ffn1_w_up": _normal(ks[4], (L, D, D_FF), D ** -0.5),
        "ffn1_w_down": _normal(ks[5], (L, D_FF, D), D_FF ** -0.5),
        "mix_norm": _gain(ks[6], (L, D)),
        "mem_norm": _gain(ks[7], (L, D)),
        "w_in": _normal(ks[8], (L, D, IN_W), D ** -0.5),
        "w_mem_kv": _normal(ks[9], (L, D, 2 * MEM_Q_W), D ** -0.5),
        "swa_q_norm": _gain(ks[10], (L, HEAD_DIM)),
        "swa_k_norm": _gain(ks[11], (L, HEAD_DIM)),
        "swa_sinks": _normal(ks[12], (L, SWA_HEADS), 0.5),
        "rel_bias": _normal(ks[13], (N_BUCKETS, SWA_HEADS), 0.2),
        "gla_w_gate_up": _normal(ks[14], (L, GLA_RANK, GLA_QK_W), GLA_RANK ** -0.5),
        "gla_b_gate": _normal(ks[15], (L, GLA_QK_W), 0.01),
        "gla_out_norm": _gain(ks[16], (L, GLA_DV)),
        "mem_q_norm": _gain(ks[17], (L, HEAD_DIM)),
        "mem_k_norm": _gain(ks[18], (L, HEAD_DIM)),
        "w_out": _normal(ks[19], (L, MIX_W, D), MIX_W ** -0.5),
        "ffn2_norm": _gain(ks[20], (L, D)),
        "ffn2_w_gate": _normal(ks[21], (L, D, D_FF), D ** -0.5),
        "ffn2_w_up": _normal(ks[22], (L, D, D_FF), D ** -0.5),
        "ffn2_w_down": _normal(ks[23], (L, D_FF, D), D_FF ** -0.5),
    }

def reference(x, mem, ffn1_norm, ffn1_w_gate, ffn1_w_up, ffn1_w_down, mix_norm, mem_norm,
              w_in, w_mem_kv, swa_q_norm, swa_k_norm, swa_sinks, rel_bias, gla_w_gate_up,
              gla_b_gate, gla_out_norm, mem_q_norm, mem_k_norm, w_out, ffn2_norm,
              ffn2_w_gate, ffn2_w_up, ffn2_w_down):
    B, S, _ = x.shape
    M = mem.shape[1]
    splits = _split_points()
    for l in range(DEPTH):
        x = x + 0.5 * swiglu(rmsnorm(x, ffn1_norm[l]), ffn1_w_gate[l], ffn1_w_up[l], ffn1_w_down[l])

        h = rmsnorm(x, mix_norm[l])
        sq, sk, sv, gq, gk, gv, gg, glr, mq = jnp.split(h @ w_in[l], splits, axis=-1)

        y_swa = swa_attention(sq.reshape(B, S, SWA_HEADS, HEAD_DIM),
                              sk.reshape(B, S, SWA_KV_HEADS, HEAD_DIM),
                              sv.reshape(B, S, SWA_KV_HEADS, HEAD_DIM),
                              swa_q_norm[l], swa_k_norm[l], swa_sinks[l], rel_bias)
        y_gla = gla(gq, gk, gv, gg, glr, gla_w_gate_up[l], gla_b_gate[l], gla_out_norm[l])
        mk, mv = jnp.split(rmsnorm(mem, mem_norm[l]) @ w_mem_kv[l], 2, axis=-1)
        y_mem = memory_attention(mq.reshape(B, S, MEM_HEADS, HEAD_DIM),
                                 mk.reshape(B, M, MEM_HEADS, HEAD_DIM),
                                 mv.reshape(B, M, MEM_HEADS, HEAD_DIM),
                                 mem_q_norm[l], mem_k_norm[l])
        x = x + jnp.concatenate([y_swa, y_gla, y_mem], axis=-1) @ w_out[l]

        x = x + 0.5 * swiglu(rmsnorm(x, ffn2_norm[l]), ffn2_w_gate[l], ffn2_w_up[l], ffn2_w_down[l])
    return x


_drawn_inputs = setup_inputs


def setup_inputs(seed=0):
    import zlib

    import numpy as np

    out = dict(_drawn_inputs(seed))
    spreads = {}
    factors = {'mem_norm': 8.0,
     'swa_q_norm': 8.0,
     'swa_k_norm': 8.0,
     'swa_sinks': 64.0,
     'rel_bias': 13.095,
     'gla_b_gate': 43.909,
     'gla_out_norm': 11.306,
     'mem_q_norm': 8.0,
     'mem_k_norm': 8.0,
     'ffn2_norm': 3.103}
    for name, (base, spread) in spreads.items():
        noise = np.random.default_rng([zlib.crc32(name.encode()), seed]).standard_normal(out[name].shape)
        drawn = base * np.exp(spread * noise) if base else spread * noise
        out[name] = __import__('jax').numpy.asarray(drawn.astype(out[name].dtype))
    for name, factor in factors.items():
        out[name] = (out[name] * factor).astype(out[name].dtype)
    return out
```

```python
from contextlib import ExitStack

import numpy as np

import concourse.bass as bass
from concourse import mybir

F32 = mybir.dt.float32
F32R = mybir.dt.float32r
U8 = mybir.dt.uint8
ALU = mybir.AluOpType
ACT = mybir.ActivationFunctionType
AX = mybir.AxisListType

P = 128
D = 1024
T = 1024
KT = D // P
HALF = 512
NHALF = T // HALF
F = 2816
PAIRS = F // (2 * P)
EPS = 1e-6
MEM = 256
NB = T // P
HEAD = 64
SWA_HEADS = 8
N_BUCKETS = 32
MAX_DISTANCE = 128
ROW = 3 * P
GLA_DK, GLA_DV, GLA_RANK, GLA_TAU = 32, 64, 16, 16.0
LEVELS = 8
MASKED = -1e30
PROJ = ["v", "gv0", "gv1", "gk", "gq", "glr", "mv0", "mv1", "mk0", "mk1", "k",
        "q0", "q1", "q2", "q3", "mq0", "mq1", "gg0", "gg1"]
NSPLIT = 3


def split_product(nc, out, w_hi, w_lo, x_hi, x_lo, first, last):
    nc.tensor.matmul(out, w_hi, x_hi, start=first, stop=False)
    nc.tensor.matmul(out, w_hi, x_lo, start=False, stop=False)
    return nc.tensor.matmul(out, w_lo, x_hi, start=False, stop=last)


def build(nc, x_in, mem_in, w_gate1, w_up1, w_down1, w_proj, w_mem, w_out, w_gate2, w_up2, w_down2, gains_in,
          mem_gain_in, head_gains_in, sinks_in, rel_bias_in, bucket_of_in, gate_up_in, gate_bias_in, masks_in, ident_in, head_ones_in, out):
    ctx = ExitStack()
    with ctx:
        sb = lambda name, shape, dt=F32: ctx.enter_context(nc.sbuf_tensor(name, shape, dt))
        sem = lambda name: ctx.enter_context(nc.semaphore(name))

        def phase(*tensors):
            with ExitStack() as stack:
                return [stack.enter_context(nc.sbuf_tensor(name, shape, dt)) for name, shape, dt in tensors]

        xT = sb("xT", [P, KT, T])
        hT_hi = sb("hT_hi", [P, KT, T], F32R)
        hT_lo = sb("hT_lo", [P, KT, T], F32R)
        glu = sb("glu", [P, NHALF, HALF])
        rstd = sb("rstd", [P, T])
        ident = sb("ident", [P, P])
        ones = sb("ones", [P, P])
        head_ones = sb("head_ones", [P, P])
        eps = sb("eps", [P, 1])
        gains = sb("gains", [P, 3, KT])
        mem_gain = sb("mem_gain", [P, KT])
        head_gains = sb("head_gains", [P, 5])
        sinks = sb("sinks", [P, SWA_HEADS])
        gate_bias = sb("gate_bias", [P, 1])
        gate_up_w = sb("gate_up_w", [GLA_RANK, P])
        masks = sb("masks", [P, LEVELS, P], U8)
        rstd_tok = sb("rstd_tok", [P, KT + 2])

        rel_bias, bucket_of, rel_wide, bias_rows, masks_f = phase(
            ("rel_bias", [N_BUCKETS + 1, SWA_HEADS], F32), ("bucket_of", [N_BUCKETS + 1, ROW], F32),
            ("rel_wide", [N_BUCKETS + 1, SWA_HEADS, P], F32), ("bias_rows", [P, SWA_HEADS, ROW], F32),
            ("masks_f", [P, LEVELS, P], F32))
        bias_dram = nc.dram_tensor("bias_dram", (SWA_HEADS * P * ROW,), F32, kind="Internal").ap()

        act_hi, act_lo, w_hi, w_lo, w_raw = phase(
            ("act_hi", [P, 3, T], F32R), ("act_lo", [P, 3, T], F32R),
            ("w_hi", [P, 6, D], F32R), ("w_lo", [P, 6, D], F32R), ("w_raw", [P, 6, D], F32))

        memT, memT_hi, memT_lo = phase(
            ("memT", [P, KT, MEM], F32), ("memT_hi", [P, KT, MEM], F32R), ("memT_lo", [P, KT, MEM], F32R))
        with ExitStack() as mix:
            msb = lambda name, shape, dt=F32: mix.enter_context(nc.sbuf_tensor(name, shape, dt))
            qT = msb("qT", [P, 4, T])
            mqT = msb("mqT", [P, 2, T])
            kT = msb("kT", [P, T])
            mkT = msb("mkT", [P, 2, MEM])
            mv = msb("mv", [P, 2, 2 * P])
            vg = msb("vg", [P, NB, 3 * P])
            gqk = msb("gqk", [P, 2, T])
            bT = msb("bT", [P, T])
            ggT = msb("ggT", [P, 2, T])
            p_hi, p_lo, p_raw = phase(
                ("p_hi", [P, 3, D], F32R), ("p_lo", [P, 3, D], F32R), ("p_raw", [P, 3, D], F32))
            (bias, Pg0, Pg1, gk_lv, gq_lv, A_T, q_st, mq_st, k_st, v_st, gv_st, k_hat, k_hat_tok, q_hat,
             decay, state, row_max, shift, sink_shift, sink_exp, row_sum, row_inv) = phase(
                ("bias", [P, SWA_HEADS, 2 * P], F32),
                ("Pg0", [P, 4, 2 * P], F32), ("Pg1", [P, 4, 2 * P], F32),
                ("gk_lv", [P, LEVELS, P], F32), ("gq_lv", [P, LEVELS, P], F32),
                ("A_T", [P, 4, P], F32), 
                ("q_st", [P, 4, P], F32), ("mq_st", [P, 2, P], F32), ("k_st", [P, 2 * P], F32),
                ("v_st", [P, 2, P], F32), ("gv_st", [P, 2 * P], F32),
                ("k_hat", [P, P], F32), ("k_hat_tok", [P, P], F32), ("q_hat", [P, P], F32),
                ("decay", [P, P], F32), ("state", [P, 4 * GLA_DV], F32),
                ("row_max", [P, 8], F32), ("shift", [P, 12], F32), ("sink_shift", [P, 8], F32),
                ("sink_exp", [P, 8], F32), ("row_sum", [P, 12], F32), ("row_inv", [P, 12], F32))
        P_of = [Pg0[:], Pg1[:], rstd[:].rearrange("p (h k) -> p h k", h=4)]
        PT = glu

        ps = ctx.enter_context(nc.psum_tensor("ps", [P, 8, HALF], F32))
        BANK_GATE, BANK_UP, BANK_DOWN, BANK_NORM = 0, 2, 4, 6

        NPROJ = len(PROJ)
        MEM_UNITS = ["mk0", "mk1", "mv0", "mv1"]
        X_UNITS = [n for n in PROJ if n not in MEM_UNITS]
        gains_scaled, masks_ready = sem("gains_scaled"), sem("masks_ready")
        dve_passed, pool_passed = sem("dve_passed"), sem("pool_passed")
        mem_landed, bias_stored, bias_landed = sem("mem_landed"), sem("bias_stored"), sem("bias_landed")
        rel_wide_ready, bias_turned, bias_rows_ready = sem("rel_wide_ready"), sem("bias_turned"), sem("bias_rows_ready")
        p_landed = [sem(f"p_landed{i}") for i in range(3)]
        p_hi_ready = [sem(f"p_hi_ready{i}") for i in range(3)]
        p_ready = [sem(f"p_ready{i}") for i in range(3)]
        (proj_ready, proj_taken, mem_hi_ready, mem_lo_ready, mem_split, mem_summed, mem_rooted, mem_normed, gate_ready,
         gate_min, gate_log, gate_summed, gate_scanned, head_squared, head_summed, head_rooted, head_normed,
         out_gate_ready, out_added, gla_gated, gla_hi_ready, gla_lo_ready, mix_set, head_inverted) = [sem(n) for n in (
            "proj_ready proj_taken mem_hi_ready mem_lo_ready mem_split mem_summed mem_rooted mem_normed gate_ready "
            "gate_min gate_log gate_summed gate_scanned head_squared head_summed head_rooted head_normed "
            "out_gate_ready out_added gla_gated gla_hi_ready gla_lo_ready mix_set head_inverted").split()]
        (staged_q, staged_k, staged_mq, staged_v, staged_gv, scores_ready, biased, shift_ready, probs_ready, denom, scaled,
         turned, pt0_ready, pt1_ready, pv_done, y_hi_ready, y_lo_ready, level_ready, level_taken, gla_diff, gla_exp,
         gla_factor, k_hat_turned, k_hat_copied, kv_ready, state_ready, o_ready, o_copied) = [sem(n) for n in (
            "staged_q staged_k staged_mq staged_v staged_gv scores_ready biased shift_ready probs_ready denom scaled "
            "turned pt0_ready pt1_ready pv_done y_hi_ready y_lo_ready level_ready level_taken gla_diff gla_exp "
            "gla_factor k_hat_turned k_hat_copied kv_ready state_ready o_ready o_copied").split()]
        const_landed = sem("const_landed")
        const_set = sem("const_set")
        x_landed = [sem(f"x_landed{i}") for i in range(4)]
        consts = [(gains[:], gains_in), (mem_gain[:], mem_gain_in), (head_gains[:], head_gains_in),
                  (sinks[:], sinks_in.rearrange("(a n) -> a n", a=1).to_broadcast([P, SWA_HEADS])),
                  (gate_bias[:], gate_bias_in), (gate_up_w[:], gate_up_in), (bucket_of[:], bucket_of_in),
                  (ident[:], ident_in), (masks_f[:], masks_in), (head_ones[:], head_ones_in)]
        NCONST = len(consts) + 1
        h_hi_ready = sem("h_hi_ready")
        h_ready = sem("h_ready")
        squared = sem("squared")
        sumsq_added = sem("sumsq_added")
        norm_summed = sem("norm_summed")
        norm_rooted = sem("norm_rooted")
        rstd_ready = sem("rstd_ready")
        w_landed = [sem(f"w_landed{i}") for i in range(6)]
        w_hi_ready = [sem(f"w_hi_ready{i}") for i in range(6)]
        w_ready = [sem(f"w_ready{i}") for i in range(6)]
        gate_up_ready = sem("gate_up_ready")
        gate_scaled = sem("gate_scaled")
        gate_silu = sem("gate_silu")
        up_scaled = sem("up_scaled")
        glu_ready = sem("glu_ready")
        act_hi_ready = sem("act_hi_ready")
        act_ready = sem("act_ready")
        down_ready = sem("down_ready")
        down_added = sem("down_added")
        y_stored = sem("y_stored")

        SLOT = dict(ga=0, ua=1, da=2, db=3, gb=4, ub=5)

        def wait(eng, s, value):
            if isinstance(value, int) and value <= 0:
                return
            eng.wait_ge(s, value)

        ffn_weights = [(w_gate1, w_up1, w_down1), (w_gate2, w_up2, w_down2)]
        NFFN = 2

        class Base:
            def __init__(self, f):
                self.use = f * PAIRS
                self.gu = f * PAIRS * 4
                self.down = f * PAIRS * 2 * KT

        def load_slot(sp, f, name, k):
            b, s = Base(f), SLOT[name]
            wait(sp, w_ready[s], k + b.use)
            wg, wu, wd = ffn_weights[f]
            ab = 1 if name[1] == "b" else 0
            if name[0] == "d":
                src = wd[bass.ds((2 * k + ab) * P, P), :]
                dst = w_raw[:, s, :]
            else:
                w = wg if name[0] == "g" else wu
                src = w[bass.ds((2 * k + ab) * P, P), :]
                dst = w_raw[:, s, :]
            sp.dma_start(dst, src).then_inc(w_landed[s], 16)

        def each_pair(eng, body):
            body(0, 0, True, False)
            with eng.Fori(1, PAIRS - 2, 2) as i:
                body(i, 1, False, False)
                body(i + 1, 0, False, False)
            body(PAIRS - 2, 1, False, False)
            body(PAIRS - 1, 0, False, True)

        def ffn_sync(sp, f):
            def body(i, par, first, last):
                for name in ("ga", "ua"):
                    load_slot(sp, f, name, i)
                if not first:
                    for name in ("da", "db"):
                        load_slot(sp, f, name, i - 1)
                for name in ("gb", "ub"):
                    load_slot(sp, f, name, i)
            each_pair(sp, body)
            for name in ("da", "db"):
                load_slot(sp, f, name, PAIRS - 1)

        def freed(eng, f, name, k):
            b = Base(f)
            if name[0] == "d":
                wait(eng, down_ready, b.down + 2 * KT * k)
            else:
                wait(eng, gate_up_ready, b.gu + 4 * k - (2 if name[1] == "a" else 0))

        def weight_hi(act, f, name, k):
            b, s = Base(f), SLOT[name]
            wait(act, w_landed[s], 16 * (k + b.use) + 16)
            freed(act, f, name, k)
            nc.scalar.activation(w_hi[:, s, :], w_raw[:, s, :], ACT.Copy).then_inc(w_hi_ready[s], 1)

        def weight_lo(dve, f, name, k):
            b, s = Base(f), SLOT[name]
            wait(dve, w_hi_ready[s], k + b.use + 1)
            nc.vector.tensor_tensor(w_lo[:, s, :], w_raw[:, s, :], w_hi[:, s, :].bitcast(F32),
                                    ALU.subtract).then_inc(w_ready[s], 1)

        def ffn_scalar(act, f):
            b = Base(f)

            def act_slot(par, t):
                return 2 if t else par

            def glu_steps(i, par, t):
                for h in range(NHALF):
                    q = b.gu + 4 * i + 2 * t + h
                    wait(act, gate_scaled, q + 1)
                    nc.scalar.activation(ps[:, BANK_GATE + h, :], ps[:, BANK_GATE + h, :],
                                         ACT.Silu).then_inc(gate_silu, 1)
                    wait(act, glu_ready, q + 1)
                    wait(act, down_ready, b.down + 2 * KT * (i if t else i - 1))
                    nc.scalar.activation(act_hi[:, act_slot(par, t), h * HALF:(h + 1) * HALF], glu[:, h, :],
                                         ACT.Copy).then_inc(act_hi_ready, 1)

            def body(i, par, first, last):
                if first:
                    weight_hi(act, f, "ga", i)
                    weight_hi(act, f, "ua", i)
                weight_hi(act, f, "gb", i)
                weight_hi(act, f, "ub", i)
                if first:
                    norm_root(act, 2 * f)
                glu_steps(i, par, 0)
                if not last:
                    weight_hi(act, f, "ga", i + 1)
                    weight_hi(act, f, "ua", i + 1)
                weight_hi(act, f, "da", i)
                weight_hi(act, f, "db", i)
                glu_steps(i, par, 1)
            each_pair(act, body)

        def ffn_vector(dve, f):
            b = Base(f)

            def glu_steps(i, par, t):
                for h in range(NHALF):
                    q = b.gu + 4 * i + 2 * t + h
                    cols = slice(h * HALF, (h + 1) * HALF)
                    slot = 2 if t else par
                    wait(dve, gate_up_ready, q + 1)
                    nc.vector.tensor_tensor(ps[:, BANK_GATE + h, :], ps[:, BANK_GATE + h, :], rstd[:, cols],
                                            ALU.mult).then_inc(gate_scaled, 1)
                    nc.vector.tensor_tensor(glu[:, h, :], ps[:, BANK_UP + h, :], rstd[:, cols],
                                            ALU.mult).then_inc(up_scaled, 1)
                    wait(dve, up_scaled, q + 1)
                    wait(dve, gate_silu, q + 1)
                    nc.vector.tensor_tensor(glu[:, h, :], ps[:, BANK_GATE + h, :], glu[:, h, :],
                                            ALU.mult).then_inc(glu_ready, 1)
                    wait(dve, act_hi_ready, q + 1)
                    nc.vector.tensor_tensor(act_lo[:, slot, cols], glu[:, h, :],
                                            act_hi[:, slot, cols].bitcast(F32),
                                            ALU.subtract).then_inc(act_ready, 1)

            def body(i, par, first, last):
                if first:
                    weight_lo(dve, f, "ga", i)
                    weight_lo(dve, f, "ua", i)
                weight_lo(dve, f, "gb", i)
                weight_lo(dve, f, "ub", i)
                if first:
                    norm_recip(dve, 2 * f)
                glu_steps(i, par, 0)
                for g in range(2 * KT):
                    if not first:
                        down_add(dve, b.down, i - 1, g)
                    if g == 6 and not last:
                        weight_lo(dve, f, "ga", i + 1)
                    if g == 11 and not last:
                        weight_lo(dve, f, "ua", i + 1)
                weight_lo(dve, f, "da", i)
                weight_lo(dve, f, "db", i)
                glu_steps(i, par, 1)
            each_pair(dve, body)

        def down_add(dve, base, j, g):
            m, h = g // NHALF, g % NHALF
            r = base + 2 * KT * j + g
            dst = xT[:, m, h * HALF:(h + 1) * HALF]
            wait(dve, down_ready, r + 1)
            nc.vector.scalar_tensor_tensor(out=dst, in0=ps[:, BANK_DOWN + g % 4, :], scalar=0.5, in1=dst,
                                           op0=ALU.mult, op1=ALU.add).then_inc(down_added, 1)

        def ffn_tensor(pe, f):
            b = Base(f)

            def gate_up(i, t):
                g, u = (("ga", "ua"), ("gb", "ub"))[t]
                for h in range(NHALF):
                    q = b.gu + 4 * i + 2 * t + h
                    wait(pe, glu_ready, q - 1)
                    for name, bank in ((g, BANK_GATE + h), (u, BANK_UP + h)):
                        s = SLOT[name]
                        if h == 0:
                            wait(pe, w_ready[s], b.use + i + 1)
                        for k in range(KT):
                            if isinstance(i, int) and i == 0 and t == 0 and name[0] == "g":
                                pe.wait_ge(h_ready, split_count(2 * f, k, h))
                            cols, rows = slice(k * P, (k + 1) * P), slice(h * HALF, (h + 1) * HALF)
                            mm = split_product(nc, ps[:, bank, :], w_hi[:, s, cols], w_lo[:, s, cols],
                                               hT_hi[:, k, rows], hT_lo[:, k, rows], k == 0, k == KT - 1)
                    mm.then_inc(gate_up_ready, 1)
                    if isinstance(i, int) and i == 0 and t == 0 and h == 0:
                        norm_sum(pe, 2 * f)

            def down(j, par):
                wait(pe, act_ready, b.gu + 4 * j + 4)
                for s in (SLOT["da"], SLOT["db"]):
                    wait(pe, w_ready[s], b.use + j + 1)
                for g in range(2 * KT):
                    m, h = g // NHALF, g % NHALF
                    if g >= 4:
                        pe.wait_ge(down_added, b.down + 2 * KT * j + g - 3)
                    for t in range(2):
                        s, slot = SLOT[("da", "db")[t]], (par, 2)[t]
                        cols, rows = slice(m * P, (m + 1) * P), slice(h * HALF, (h + 1) * HALF)
                        mm = split_product(nc, ps[:, BANK_DOWN + g % 4, :], w_hi[:, s, cols], w_lo[:, s, cols],
                                           act_hi[:, slot, rows], act_lo[:, slot, rows], t == 0, t == 1)
                    mm.then_inc(down_ready, 1)

            def body(i, par, first, last):
                gate_up(i, 0)
                if not first:
                    down(i - 1, 1 - par)
                gate_up(i, 1)
            each_pair(pe, body)
            down(PAIRS - 1, 0)

        def norm_steps(n):
            if n != 1:
                return [(m, h) for h in range(NHALF) for m in range(KT)]
            return [(m, h) for m in range(KT) for h in range(NHALF)]

        def split_count(n, m, h):
            return 2 * KT * n + norm_steps(n).index((m, h)) + 1

        def norm_sum(pe, n):
            for h in range(NHALF):
                pe.wait_ge(sumsq_added, 2 * KT * (n + 1))
                nc.tensor.matmul(ps[:, BANK_NORM + h, :], ones[:, :], rstd[:, h * HALF:(h + 1) * HALF],
                                 start=True, stop=True).then_inc(norm_summed, 1)

        def norm_root(act, n):
            for h in range(NHALF):
                bank = ps[:, BANK_NORM + h, :]
                act.wait_ge(norm_summed, NHALF * n + h + 1)
                nc.scalar.activation(bank, bank, ACT.Sqrt, bias=eps[:, 0:1], scale=1.0 / D).then_inc(norm_rooted, 1)

        def norm_recip(dve, n):
            for h in range(NHALF):
                dve.wait_ge(norm_rooted, NHALF * n + h + 1)
                nc.vector.reciprocal(rstd[:, h * HALF:(h + 1) * HALF],
                                     ps[:, BANK_NORM + h, :]).then_inc(rstd_ready, 1)
            dve.wait_ge(rstd_ready, NHALF * (n + 1))

        def part(tensor, m, h):
            return tensor[:, m, h * HALF:(h + 1) * HALF]

        def norm_hi(act, n, m, h):
            if n == 0:
                act.wait_ge(x_landed[2 * h + m // 4], 16)
            elif n == 1:
                act.wait_ge(down_added, Base(1).down - 2 * KT + 2 * m + h + 1)
            else:
                act.wait_ge(out_added, 2 * m + h + 1)
                act.wait_ge(proj_ready, NG + 2 * KT)
            nc.scalar.activation(part(hT_hi, m, h), part(xT, m, h), ACT.Copy,
                                 scale=gains[:, n, m:m + 1]).then_inc(h_hi_ready, 1)

        def square_steps(n):
            return [(m, h) for m in range(KT) for h in range(NHALF)] if n else norm_steps(0)

        def square_count(n, m, h):
            return 2 * KT * n + square_steps(n).index((m, h)) + 1

        def norm_square(act, n, m, h):
            c = square_count(n, m, h)
            if n == 2:
                act.wait_ge(out_added, 2 * m + h + 1)
            wait(act, sumsq_added, c - 2)
            nc.scalar.activation(glu[:, c % 2, :], part(xT, m, h), ACT.Square).then_inc(squared, 1)

        def norm_vector(dve, n, m, h):
            dve.wait_ge(h_hi_ready, split_count(n, m, h))
            nc.vector.scalar_tensor_tensor(out=part(hT_lo, m, h), in0=part(xT, m, h), scalar=gains[:, n, m:m + 1],
                                           in1=part(hT_hi, m, h).bitcast(F32), op0=ALU.mult,
                                           op1=ALU.subtract).then_inc(h_ready, 1)

        def norm_pool(pool, n):
            for m, h in square_steps(n):
                c = square_count(n, m, h)
                acc = rstd[:, h * HALF:(h + 1) * HALF]
                pool.wait_ge(squared, c)
                if m == 0:
                    nc.gpsimd.tensor_scalar(acc, glu[:, c % 2, :], 1.0, 1.0, ALU.mult, ALU.mult).then_inc(sumsq_added, 1)
                else:
                    pool.wait_ge(sumsq_added, c - 1)
                    nc.gpsimd.tensor_tensor(acc, acc, glu[:, c % 2, :], ALU.add).then_inc(sumsq_added, 1)

        def unit_sync(sp, u):
            wait(sp, p_ready[u % 3], u // 3)
            n = PROJ[u] if u < NPROJ else None
            if n is None:
                src = w_out[(u - NPROJ) * P:(u - NPROJ + 1) * P, :]
            elif n in MEM_UNITS:
                i = MEM_UNITS.index(n)
                src = w_mem[i * P:(i + 1) * P, :]
            else:
                i = X_UNITS.index(n)
                src = w_proj[i * P:(i + 1) * P, :]
            sp.dma_start(p_raw[:, u % 3, :], src).then_inc(p_landed[u % 3], 16)

        def unit_free(u):
            return last_group[u - 3] if u >= 3 else 0

        def unit_scalar(act, u):
            s = u % 3
            act.wait_ge(p_landed[s], 16 * (u // 3 + 1))
            if u < 3:
                act.wait_ge(down_ready, Base(1).down)
            wait(act, proj_ready, unit_free(u))
            nc.scalar.activation(p_hi[:, s, :], p_raw[:, s, :], ACT.Copy).then_inc(p_hi_ready[s], 1)

        def unit_vector(dve, u):
            s = u % 3
            dve.wait_ge(p_hi_ready[s], u // 3 + 1)
            nc.vector.tensor_tensor(p_lo[:, s, :], p_raw[:, s, :], p_hi[:, s, :].bitcast(F32),
                                    ALU.subtract).then_inc(p_ready[s], 1)

        groups = [("v", t) for t in range(NB)]
        for n in PROJ[3:]:
            if n == "mv0":
                groups += [("mv", 0), ("mv", 1)]
            elif n == "mv1":
                pass
            elif n in ("mk0", "mk1"):
                groups += [(n, 0)]
            else:
                groups += [(n, h) for h in range(NHALF)]
        gi = {g: i for i, g in enumerate(groups)}
        NG = len(groups)

        def units_of(name):
            return {"v": [0, 1, 2], "mv": [6, 7]}.get(name) or [PROJ.index(name)]

        last_group = {}
        for i, (n, _) in enumerate(groups):
            for u in units_of(n):
                last_group[u] = i + 1
        for m in range(KT):
            last_group[NPROJ + m] = NG + 2 * (m + 1)

        normed = [("mk0", 0), ("mk1", 0)] + [(n, h) for n in ("k", "q0", "q1", "q2", "q3", "mq0", "mq1")
                                             for h in range(NHALF)]

        def normed_at(i):
            n, h = normed[i]
            cols = slice(h * HALF, (h + 1) * HALF)
            if n[:2] == "mk":
                return mkT[:, int(n[2]), :], head_gains[:, 3:4]
            if n[:2] == "mq":
                return mqT[:, int(n[2]), cols], head_gains[:, 2:3]
            if n[0] == "q":
                return qT[:, int(n[1]), cols], head_gains[:, 0:1]
            return kT[:, cols], head_gains[:, 1:2]

        def width(i):
            return MEM if normed[i][0][:2] == "mk" else HALF

        GLA_OUT = len(normed)

        def head_square(act, i, src, w):
            wait(act, head_summed, i - 1)
            nc.scalar.activation(glu[:, i % 2, 0:w], src, ACT.Square).then_inc(head_squared, 1)

        def head_sum(pe, i, w):
            pe.wait_ge(head_squared, i + 1)
            wait(pe, head_normed, i - 1)
            nc.tensor.matmul(ps[:, 4 + i % 2, 0:w], head_ones[:, :], glu[:, i % 2, 0:w], start=True,
                             stop=True).then_inc(head_summed, 1)

        def head_root(act, i, w):
            act.wait_ge(head_summed, i + 1)
            nc.scalar.activation(ps[:, 4 + i % 2, 0:w], ps[:, 4 + i % 2, 0:w], ACT.Sqrt, bias=eps[:, 0:1],
                                 scale=1.0 / HEAD).then_inc(head_rooted, 1)

        def head_norm(dve, i, at, gain, w):
            dve.wait_ge(head_rooted, i + 1)
            bank = ps[:, 4 + i % 2, 0:w]
            nc.vector.reciprocal(bank, bank).then_inc(head_inverted, 1)
            dve.wait_ge(head_inverted, i + 1)
            nc.vector.scalar_tensor_tensor(out=at, in0=at, scalar=gain, in1=bank, op0=ALU.mult, op1=ALU.mult
                                           ).then_inc(head_normed, 1)

        DELAY = 2

        def delayed(i):
            if i - DELAY < 0:
                return None
            n, h = groups[i - DELAY]
            if n == "glr":
                return ("gate", h)
            if (n, h) in normed:
                return ("norm", normed.index((n, h)))
            return None

        def proj_tensor(pe):
            for i, (n, h) in enumerate(groups):
                us = units_of(n)
                for u in us:
                    pe.wait_ge(p_ready[u % 3], u // 3 + 1)
                wait(pe, proj_taken, i - 3)
                if i < 4:
                    pe.wait_ge(down_added, Base(1).down)
                if n in ("mv", "mk0", "mk1"):
                    pe.wait_ge(mem_split, 2)
                for k in range(KT):
                    kc = slice(k * P, (k + 1) * P)
                    if n == "v":
                        pe.wait_ge(h_ready, split_count(1, k, h // 4))
                        tok = slice(h * P, (h + 1) * P)
                        mm = split_product(nc, ps[:, i % 4, 0:3 * P], hT_hi[:, k, tok], hT_lo[:, k, tok],
                                           p_hi[:, 0:3, kc], p_lo[:, 0:3, kc], k == 0, k == KT - 1)
                    elif n == "mv":
                        tok = slice(h * P, (h + 1) * P)
                        mm = split_product(nc, ps[:, i % 4, 0:2 * P], memT_hi[:, k, tok], memT_lo[:, k, tok],
                                           p_hi[:, 0:2, kc], p_lo[:, 0:2, kc], k == 0, k == KT - 1)
                    elif n in ("mk0", "mk1"):
                        s = us[0] % 3
                        mm = split_product(nc, ps[:, i % 4, 0:MEM], p_hi[:, s, kc], p_lo[:, s, kc],
                                           memT_hi[:, k, :], memT_lo[:, k, :], k == 0, k == KT - 1)
                    else:
                        s = us[0] % 3
                        cols = slice(h * HALF, (h + 1) * HALF)
                        mm = split_product(nc, ps[:, i % 4, :], p_hi[:, s, kc], p_lo[:, s, kc],
                                           hT_hi[:, k, cols], hT_lo[:, k, cols], k == 0, k == KT - 1)
                mm.then_inc(proj_ready, 1)
                if i == 1:
                    pe.wait_ge(sumsq_added, 2 * KT * 2)
                    for t in range(NB):
                        nc.tensor.matmul(ps[:, 5, t:t + 1], rstd[:, t * P:(t + 1) * P], ones[:, 0:1],
                                         start=True, stop=True)
                    pe.wait_ge(mem_split, 3)
                    for t in range(2):
                        for k in range(KT):
                            nc.tensor.matmul(ps[:, 5, KT + t:KT + t + 1], memT[:, k, t * P:(t + 1) * P],
                                             ones[:, 0:1], start=(k == 0), stop=(k == KT - 1))
                    for k in range(KT):
                        mm = nc.tensor.matmul(ps[:, 4, 0:MEM], ones[:, :], memT[:, k, :], start=(k == 0),
                                              stop=(k == KT - 1))
                    mm.then_inc(mem_summed, 1)
                    norm_sum(pe, 1)
                small = delayed(i)
                if small and small[0] == "gate":
                    g = small[1]
                    pe.wait_ge(proj_taken, gi[("glr", g)] + 1)
                    pe.wait_ge(mem_normed, 2)
                    nc.tensor.matmul(ps[:, 4 + g, :], gate_up_w[:, :], glu[0:GLA_RANK, g, :], start=True,
                                     stop=True).then_inc(gate_ready, 1)
                elif small:
                    j = small[1]
                    if j < 2:
                        pe.wait_ge(gate_summed, 2)
                    head_sum(pe, j, width(j))

        def mem_split_scalar(act):
            act.wait_ge(mem_landed, 16)
            for k in range(KT):
                nc.scalar.activation(memT_hi[:, k, :], memT[:, k, :], ACT.Copy,
                                     scale=mem_gain[:, k:k + 1]).then_inc(mem_hi_ready, 1)
            act.wait_ge(mem_lo_ready, KT)
            nc.scalar.activation(memT[:], memT[:], ACT.Square).then_inc(mem_split, 3)

        def mem_split_vector(dve):
            for k in range(KT):
                dve.wait_ge(mem_hi_ready, k + 1)
                nc.vector.scalar_tensor_tensor(out=memT_lo[:, k, :], in0=memT[:, k, :], scalar=mem_gain[:, k:k + 1],
                                               in1=memT_hi[:, k, :].bitcast(F32), op0=ALU.mult,
                                               op1=ALU.subtract).then_inc(mem_lo_ready, 1)

        def proj_scalar(act):
            for u in range(3):
                unit_scalar(act, u)
            mem_split_scalar(act)
            act.wait_ge(mem_summed, 1)
            nc.scalar.activation(ps[:, 5, 0:KT + 2], ps[:, 5, 0:KT + 2], ACT.Sqrt, bias=eps[:, 0:1],
                                 scale=1.0 / D).then_inc(mem_rooted, 1)
            nc.scalar.activation(ps[:, 4, 0:MEM], ps[:, 4, 0:MEM], ACT.Sqrt, bias=eps[:, 0:1],
                                 scale=1.0 / D).then_inc(mem_rooted, 1)
            norm_root(act, 1)
            for i, (n, h) in enumerate(groups):
                if i >= NB - 1 and i % 1 == 0:
                    for u in prefetch.get(i, []):
                        unit_scalar(act, u)
                if n == "gg":
                    pass
                if n[:2] == "gg":
                    at = ggT[:, int(n[2]), h * HALF:(h + 1) * HALF]
                    act.wait_ge(proj_taken, i + 1)
                    nc.scalar.activation(at, at, ACT.Silu).then_inc(out_gate_ready, 1)
                if (n, h) in normed:
                    j = normed.index((n, h))
                    act.wait_ge(proj_taken, i + 1)
                    if j == 0:
                        act.wait_ge(gate_ready, 2)
                    head_square(act, j, normed_at(j)[0], width(j))
                small = delayed(i)
                if small and small[0] == "gate":
                    g = small[1]
                    bank = ps[:, 4 + g, :]
                    act.wait_ge(gate_min, g + 1)
                    nc.scalar.activation(bank, bank, ACT.Abs, bias=gate_bias[:, 0:1]).then_inc(gate_log, 1)
                    act.wait_ge(gate_log, 3 * g + 1)
                    nc.scalar.activation(bank, bank, ACT.Exp, scale=-1.0).then_inc(gate_log, 1)
                    act.wait_ge(gate_log, 3 * g + 2)
                    nc.scalar.activation(bank, bank, ACT.Ln, bias=ones[:, 0:1]).then_inc(gate_log, 1)
                elif small:
                    head_root(act, small[1], width(small[1]))

        def proj_vector(dve):
            for u in range(3):
                unit_vector(dve, u)
            mem_split_vector(dve)
            dve.wait_ge(mem_rooted, 1)
            nc.vector.reciprocal(rstd_tok[:], ps[:, 5, 0:KT + 2]).then_inc(mem_normed, 1)
            dve.wait_ge(mem_rooted, 2)
            nc.vector.reciprocal(memT[:, 0, :], ps[:, 4, 0:MEM]).then_inc(mem_normed, 1)
            dve.wait_ge(mem_normed, 2)
            norm_recip(dve, 1)
            for i, (n, h) in enumerate(groups):
                if i >= NB - 1:
                    for u in prefetch.get(i, []):
                        unit_vector(dve, u)
                dve.wait_ge(proj_ready, i + 1)
                bank = ps[:, i % 4, :]
                cols = slice(h * HALF, (h + 1) * HALF)
                if n == "v":
                    ins = nc.vector.tensor_scalar(vg[:, h, :], bank[:, 0:3 * P], rstd_tok[:, h:h + 1], None, ALU.mult)
                elif n == "mv":
                    ins = nc.vector.tensor_scalar(mv[:, h, :], bank[:, 0:2 * P], rstd_tok[:, KT + h:KT + h + 1], None,
                                                  ALU.mult)
                elif n in ("mk0", "mk1"):
                    ins = nc.vector.tensor_tensor(mkT[:, int(n[2]), :], bank[:, 0:MEM], memT[:, 0, :], ALU.mult)
                elif n == "gq":
                    ins = nc.vector.scalar_tensor_tensor(out=gqk[:, 0, cols], in0=bank, scalar=float(GLA_DK) ** -0.5,
                                                         in1=rstd[:, cols], op0=ALU.mult, op1=ALU.mult)
                elif n == "glr":
                    ins = nc.vector.tensor_tensor(glu[0:GLA_RANK, h, :], bank[0:GLA_RANK, :],
                                                  rstd[0:GLA_RANK, cols], ALU.mult)
                else:
                    at = {"gk": lambda: gqk[:, 1, cols], "k": lambda: kT[:, cols],
                          "g": lambda: ggT[:, int(n[2]), cols], "m": lambda: mqT[:, int(n[2]), cols],
                          "q": lambda: qT[:, int(n[1]), cols]}
                    dst = at[n if n in at else n[0]]()
                    ins = nc.vector.tensor_tensor(dst, bank, rstd[:, cols], ALU.mult)
                ins.then_inc(proj_taken, 1)
                small = delayed(i)
                if small and small[0] == "gate":
                    g = small[1]
                    c = slice(g * HALF, (g + 1) * HALF)
                    dve.wait_ge(gate_ready, g + 1)
                    nc.vector.tensor_scalar(bT[:, c], ps[:, 4 + g, :], gate_bias[:, 0:1], 0.0, ALU.add,
                                            ALU.min).then_inc(gate_min, 1)
                    dve.wait_ge(gate_log, 3 * g + 3)
                    dve.wait_ge(gate_min, g + 1)
                    nc.vector.tensor_tensor(bT[:, c], bT[:, c], ps[:, 4 + g, :], ALU.subtract).then_inc(gate_summed, 1)
                    dve.wait_ge(gate_summed, g + 1)
                    for t in range(4 * g, 4 * g + 4):
                        blk = bT[:, t * P:(t + 1) * P]
                        nc.vector.tensor_tensor_scan(blk, ones[:, :], blk, 0.0, ALU.mult, ALU.add
                                                     ).then_inc(gate_scanned, 1)
                elif small:
                    at, gain = normed_at(small[1])
                    head_norm(dve, small[1], at, gain, width(small[1]))

        prefetch = {}
        for u in range(3, NPROJ):
            prefetch.setdefault(last_group[u - 3] - 1 + (0), []).append(u)

        def mem_slot(h):
            return h % 2 * 2 + h // 2

        def stand_alone(eng, passed):
            eng.sem_inc(passed, 1)

        def blk(n):
            return bass.ds(n * P, P)

        def each_block(eng, body):
            body(0, True, False)
            with eng.Fori(1, NB - 1) as n:
                body(n, False, False)
            body(NB - 1, False, True)

        def mix_tensor(pe, n, first, last):
            band = slice(P, 2 * P) if first else slice(0, 2 * P)

            def scores(g):
                for j in range(4):
                    mm = nc.tensor.matmul(ps[:, 2 * g + j // 2, (j % 2) * 2 * P + band.start:(j % 2) * 2 * P + 2 * P],
                                          q_st[g * HEAD:(g + 1) * HEAD, j, :], k_st[g * HEAD:(g + 1) * HEAD, band],
                                          start=True, stop=True)
                mm.then_inc(scores_ready, 1)

            def mem_scores():
                wait(pe, staged_mq, 16 * n + 16)
                wait(pe, biased, 8 * n + 4)
                for h in range(4):
                    r = slice(h % 2 * HEAD, (h % 2 + 1) * HEAD)
                    mm = nc.tensor.matmul(ps[:, h % 2, (h // 2) * MEM:(h // 2 + 1) * MEM], mq_st[r, h // 2, :],
                                          mkT[r, h // 2, :], start=True, stop=True)
                mm.then_inc(scores_ready, 1)

            def levels(part):
                if part:
                    wait(pe, level_taken, LEVELS * n + 4)
                else:
                    wait(pe, pt0_ready, 3 * n)
                    wait(pe, pt1_ready, 3 * n)
                    wait(pe, state_ready, 4 * n)
                    wait(pe, o_copied, n)
                for l in range(4 * part, 4 * part + 4):
                    for h in range(4):
                        r = slice(h * GLA_DK, (h + 1) * GLA_DK)
                        mm = nc.tensor.matmul(ps[:, 4 + h, l % 4 * P:(l % 4 + 1) * P], gk_lv[r, l, :],
                                              gq_lv[r, l, :], start=True, stop=True, tile_position=(h * GLA_DK, 0))
                mm.then_inc(level_ready, 1)

            def turn(u):
                wait(pe, scaled, 12 * n + 4 * u + 4)
                for kt in range(2):
                    wait(pe, (pt0_ready, pt1_ready)[kt], 3 * n + u)
                    for j in range(4):
                        tr = nc.tensor.transpose(ps[:, 4 + kt, j * P:(j + 1) * P],
                                                 P_of[u][:, j, kt * P:(kt + 1) * P], ident[:, :])
                    tr.then_inc(turned, 1)

            def values(g):
                wait(pe, pt0_ready, 3 * n + g + 1)
                wait(pe, pt1_ready, 3 * n + g + 1)
                for kt in range(2):
                    mm = nc.tensor.matmul(ps[g * HEAD:(g + 1) * HEAD, 2, :], v_st[:, kt, g * HEAD:(g + 1) * HEAD],
                                          PT[:, kt, :], start=(kt == 0), stop=(kt == 1))
                mm.then_inc(pv_done, 1)

            wait(pe, staged_q, 16 * n + 16)
            wait(pe, staged_k, 16 * n + 16)
            wait(pe, probs_ready, 14 * n)
            scores(0)
            wait(pe, gla_factor, 4 * n + 2)
            levels(0)
            wait(pe, y_hi_ready, 2 * n)
            wait(pe, y_lo_ready, 2 * n)
            scores(1)
            mem_scores()
            levels(1)
            wait(pe, gla_factor, 4 * n + 4)
            wait(pe, level_taken, LEVELS * (n + 1))
            nc.tensor.transpose(ps[:, 6, 0:P], k_hat[:, :], ident[:, :]).then_inc(k_hat_turned, 1)
            turn(0)
            wait(pe, staged_gv, 16 * n + 16)
            wait(pe, state_ready, 4 * n)
            for h in range(4):
                o = ps[h % 2 * GLA_DV:(h % 2 + 1) * GLA_DV, 7, (h // 2) * P:(h // 2 + 1) * P]
                nc.tensor.matmul(o, gv_st[:, h * GLA_DV:(h + 1) * GLA_DV], A_T[:, h, :], start=True, stop=False)
                mm = nc.tensor.matmul(o, state[:, h * GLA_DV:(h + 1) * GLA_DV], q_hat[:, :], start=False, stop=True)
            mm.then_inc(o_ready, 1)
            wait(pe, staged_v, 16 * n + 16)
            wait(pe, biased, 8 * n + 8)
            values(0)
            turn(1)
            wait(pe, k_hat_copied, n + 1)
            nc.tensor.matmul(ps[:, 6, 0:2 * P], k_hat_tok[:, :], gv_st[:, :], start=True, stop=True
                             ).then_inc(kv_ready, 1)
            values(1)
            turn(2)
            wait(pe, pt0_ready, 3 * n + 3)
            wait(pe, pt1_ready, 3 * n + 3)
            for h in range(4):
                for kt in range(2):
                    mm = nc.tensor.matmul(ps[h % 2 * HEAD:(h % 2 + 1) * HEAD, 3, (h // 2) * P:(h // 2 + 1) * P],
                                          mv[:, kt, h * HEAD:(h + 1) * HEAD],
                                          PT[:, kt, mem_slot(h) * P:(mem_slot(h) + 1) * P],
                                          start=(kt == 0), stop=(kt == 1))
            mm.then_inc(pv_done, 1)

        def gla_exps(act, n):
            wait(act, gla_diff, 9 * n + 8)
            nc.scalar.activation(gq_lv[:], gq_lv[:], ACT.Abs).then_inc(gla_exp, 1)
            wait(act, gla_exp, 4 * n + 1)
            nc.scalar.activation(gq_lv[:], gq_lv[:], ACT.Exp, scale=-1.0 / GLA_TAU).then_inc(gla_exp, 1)
            wait(act, gla_diff, 9 * n + 9)
            nc.scalar.activation(k_hat[:], k_hat[:], ACT.Exp, scale=-1.0 / GLA_TAU).then_inc(gla_exp, 1)
            wait(act, state_ready, 4 * n)
            wait(act, gla_factor, 4 * n)
            nc.scalar.activation(decay[:], bT[:, blk(n)], ACT.Exp, scale=1.0 / GLA_TAU).then_inc(gla_exp, 1)

        def gla_diffs(dve, n):
            wait(dve, level_ready, 2 * n)
            b = bT[:, blk(n)]
            for l in range(LEVELS):
                s = P >> (l + 1)
                if s:
                    pairs = b.rearrange("p (a c) -> p a c", c=2 * s)
                    nc.vector.tensor_tensor(gq_lv[:, l, :].rearrange("p (a c) -> p a c", c=2 * s), pairs,
                                            pairs[:, :, s - 1:s].to_broadcast([P, P // (2 * s), 2 * s]),
                                            ALU.subtract).then_inc(gla_diff, 1)
                else:
                    nc.vector.tensor_tensor(gq_lv[:, l, :], b, b, ALU.subtract).then_inc(gla_diff, 1)
            wait(dve, k_hat_turned, n)
            nc.vector.tensor_tensor(k_hat[:], b, bT[:, bass.ds(n * P + P - 1, 1)].to_broadcast([P, P]),
                                    ALU.subtract).then_inc(gla_diff, 1)

        def gla_factors(dve, n):
            q, k = gqk[:, 0, blk(n)], gqk[:, 1, blk(n)]
            wait(dve, gla_exp, 4 * n + 2)
            nc.vector.tensor_tensor(gk_lv[:], gq_lv[:], k.unsqueeze(1).to_broadcast([P, LEVELS, P]),
                                    ALU.mult).then_inc(gla_factor, 1)
            nc.vector.tensor_tensor(gq_lv[:], gq_lv[:], q.unsqueeze(1).to_broadcast([P, LEVELS, P]),
                                    ALU.mult).then_inc(gla_factor, 1)
            wait(dve, gla_exp, 4 * n + 4)
            nc.vector.tensor_tensor(k_hat[:], k_hat[:], k, ALU.mult).then_inc(gla_factor, 1)
            wait(dve, o_ready, n)
            nc.vector.tensor_tensor(q_hat[:], decay[:], q, ALU.mult).then_inc(gla_factor, 1)

        def mix_scalar(act, n, first, last):
            band = slice(P, 2 * P) if first else slice(0, 2 * P)

            def exps(g):
                wait(act, shift_ready, 5 * n + 2 * g + 1)
                wait(act, scaled, 12 * n - 8 + 4 * g) if first else None
                for j in range(4):
                    p = P_of[g][:, j, band]
                    nc.scalar.activation(p, p, ACT.Exp, bias=shift[:, 4 * g + j:4 * g + j + 1],
                                         accum_out=row_sum[:, 4 * g + j:4 * g + j + 1]).then_inc(probs_ready, 1)
                wait(act, shift_ready, 5 * n + 2 * g + 2)
                nc.scalar.activation(sink_exp[:, 4 * g:4 * g + 4], sink_shift[:, 4 * g:4 * g + 4], ACT.Exp
                                     ).then_inc(probs_ready, 1)

            def pt_copy(u):
                wait(act, turned, 6 * n + 2 * u + 1)
                wait(act, pv_done, 3 * n + u)
                nc.scalar.activation(PT[:, 0, :], ps[:, 4, :], ACT.Copy).then_inc(pt0_ready, 1)

            exps(0)
            exps(1)
            wait(act, shift_ready, 5 * n + 5)
            wait(act, turned, 6 * n)
            for h in range(4):
                nc.scalar.activation(P_of[2][:, h, :], ps[:, h // 2, (h % 2) * MEM:(h % 2 + 1) * MEM], ACT.Exp,
                                     bias=shift[:, 8 + h:9 + h], accum_out=row_sum[:, 8 + h:9 + h]
                                     ).then_inc(probs_ready, 1)
            wait(act, k_hat_turned, n + 1)
            wait(act, kv_ready, n)
            nc.scalar.activation(k_hat_tok[:], ps[:, 6, 0:P], ACT.Copy).then_inc(k_hat_copied, 1)
            pt_copy(0)
            wait(act, o_ready, n + 1)
            nc.scalar.activation(gqk[:, :, blk(n)], ps[:, 7, 0:2 * P].rearrange("p (j t) -> p j t", j=2), ACT.Copy
                                 ).then_inc(o_copied, 1)
            pt_copy(1)
            wait(act, pv_done, 3 * n + 2)
            nc.scalar.activation(hT_hi[:, 0:4, blk(n)], ps[:, 2, :].rearrange("p (j t) -> p j t", j=4), ACT.Copy
                                 ).then_inc(y_hi_ready, 1)
            pt_copy(2)
            if not last:
                gla_exps(act, n + 1)
            wait(act, pv_done, 3 * n + 3)
            nc.scalar.activation(hT_hi[:, 6:8, blk(n)], ps[:, 3, 0:2 * P].rearrange("p (j t) -> p j t", j=2), ACT.Copy
                                 ).then_inc(y_hi_ready, 1)

        def mix_vector(dve, n, first, last):
            band = slice(P, 2 * P) if first else slice(0, 2 * P)

            def bias_max(g):
                wait(dve, scores_ready, 3 * n + g + 1)
                wait(dve, turned, 6 * n - 4 + 2 * g)
                stand_alone(dve, dve_passed)
                for j in range(4):
                    h = 4 * g + j
                    s = ps[:, 2 * g + j // 2, (j % 2) * 2 * P + band.start:(j % 2) * 2 * P + 2 * P]
                    nc.vector.tensor_tensor_reduce(out=P_of[g][:, j, band], in0=s, in1=bias[:, h, band], scale=1.0,
                                                   scalar=sinks[:, h:h + 1], op0=ALU.add, op1=ALU.max,
                                                   accum_out=row_max[:, h:h + 1]).then_inc(biased, 1)
                wait(dve, biased, 8 * n + 4 * g + 4)
                hs = slice(4 * g, 4 * g + 4)
                nc.vector.tensor_scalar(shift[:, hs], row_max[:, hs], -1.0, None, ALU.mult).then_inc(shift_ready, 1)
                nc.vector.tensor_tensor(sink_shift[:, hs], sinks[:, hs], row_max[:, hs], ALU.subtract
                                        ).then_inc(shift_ready, 1)

            def take(l):
                wait(dve, level_ready, 2 * n + l // 4 + 1)
                if l:
                    wait(dve, level_taken, LEVELS * n + l)
                stand_alone(dve, dve_passed)
                nc.vector.copy_predicated(A_T[:], masks[:, l, :].unsqueeze(1).to_broadcast([P, 4, P]),
                                          ps[:, 4:8, l % 4 * P:(l % 4 + 1) * P]
                                          ).then_inc(level_taken, 1)

            def denominators(g):
                hs = slice(4 * g, 4 * g + 4)
                wait(dve, probs_ready, 14 * n + 5 * g + 5)
                nc.vector.tensor_tensor(row_sum[:, hs], row_sum[:, hs], sink_exp[:, hs], ALU.add).then_inc(denom, 1)
                wait(dve, denom, 5 * n + 2 * g + 1)
                wait(dve, scaled, 12 * n - 8 + 4 * g)
                nc.vector.reciprocal(row_inv[:, hs], row_sum[:, hs]).then_inc(denom, 1)

            def pt_copy(u):
                wait(dve, turned, 6 * n + 2 * u + 2)
                wait(dve, pv_done, 3 * n + u)
                nc.vector.tensor_copy(PT[:, 1, :], ps[:, 5, :]).then_inc(pt1_ready, 1)

            def y_lo(tiles, bank, c):
                wait(dve, pv_done, 3 * n + (2, 3)[c])
                wait(dve, y_hi_ready, 2 * n + c + 1)
                w = tiles.stop - tiles.start
                nc.vector.tensor_tensor(hT_lo[:, tiles, blk(n)], ps[:, bank, 0:w * P].rearrange("p (j t) -> p j t", j=w),
                                        hT_hi[:, tiles, blk(n)].bitcast(F32), ALU.subtract).then_inc(y_lo_ready, 1)

            bias_max(0)
            bias_max(1)
            wait(dve, o_ready, n)
            for l in range(4):
                take(l)
                if l == 1:
                    denominators(0)
            wait(dve, scores_ready, 3 * n + 3)
            nc.vector.tensor_reduce(shift[:, 8:12], ps[:, 0:2, :].rearrange("p a (b k) -> p (a b) k", k=MEM), AX.X,
                                    ALU.max, negate=True).then_inc(shift_ready, 1)
            denominators(1)
            for l in range(4, LEVELS):
                take(l)
            wait(dve, probs_ready, 14 * n + 14)
            wait(dve, scaled, 12 * n)
            nc.vector.reciprocal(row_inv[:, 8:12], row_sum[:, 8:12]).then_inc(denom, 1)
            pt_copy(0)
            if not last:
                gla_diffs(dve, n + 1)
            pt_copy(1)
            wait(dve, kv_ready, n + 1)
            wait(dve, o_ready, n + 1)
            for h in range(4):
                r = slice(h * GLA_DK, (h + 1) * GLA_DK)
                at = state[r, h * GLA_DV:(h + 1) * GLA_DV]
                nc.vector.scalar_tensor_tensor(out=at, in0=at, scalar=decay[r, P - 1:P],
                                               in1=ps[r, 6, h * GLA_DV:(h + 1) * GLA_DV], op0=ALU.mult,
                                               op1=ALU.add).then_inc(state_ready, 1)
            y_lo(slice(0, 4), 2, 0)
            pt_copy(2)
            if not last:
                gla_factors(dve, n + 1)
            y_lo(slice(6, 8), 3, 1)

        def stage_qk(sp, n, first):
            sp.dma_start(q_st[:], qT[:, :, blk(n)]).then_inc(staged_q, 16)
            if first:
                sp.dma_start(k_st[:, P:2 * P], kT[:, 0:P]).then_inc(staged_k, 16)
            else:
                sp.dma_start(k_st[:], kT[:, bass.ds(n * P - P, 2 * P)]).then_inc(staged_k, 16)
            sp.dma_start(mq_st[:], mqT[:, :, blk(n)]).then_inc(staged_mq, 16)

        def stage_v(sp, n, first):
            if first:
                sp.dma_start(v_st[:, 1, :], vg[:, 0, 0:P]).then_inc(staged_v, 16)
            else:
                sp.dma_start(v_st[:], vg[:, bass.ds(n - 1, 2), 0:P]).then_inc(staged_v, 16)
            sp.dma_start(gv_st[:].unsqueeze(1), vg[:, bass.ds(n, 1), P:3 * P]).then_inc(staged_gv, 16)

        def mix_sync(sp, n, first, last):
            if not last:
                wait(sp, scores_ready, 3 * n + 3)
                stage_qk(sp, n + 1, False)
                wait(sp, pv_done, 3 * n + 2)
                wait(sp, kv_ready, n + 1)
                stage_v(sp, n + 1, False)

        def mix_pool(pool, n, first, last):
            def scale(u):
                wait(pool, denom, 5 * n + (2, 4, 5)[u])
                stand_alone(pool, pool_passed)
                for j in range(4):
                    p = P_of[u][:, j, :]
                    nc.gpsimd.tensor_scalar(p, p, row_inv[:, 4 * u + j:4 * u + j + 1], 1.0, ALU.mult, ALU.mult
                                            ).then_inc(scaled, 1)
            scale(0)
            scale(1)
            scale(2)

        def mix_start_pool(pool):
            pool.wait_ge(proj_ready, NG)
            pool.wait_ge(proj_taken, NG)
            pool.wait_ge(head_normed, len(normed))
            for t, v in ((A_T, 0.0), (state, 0.0), (Pg0, 0.0), (Pg1, 0.0), (v_st, 0.0)):
                nc.gpsimd.memset(t[:], v).then_inc(mix_set, 1)

        def gla_item(c):
            j, h = c // 2, c % 2
            cols = slice(h * HALF, (h + 1) * HALF)
            return j, cols, gqk[:, j, cols]

        def gla_norm_scalar(act):
            for c in range(4):
                head_square(act, GLA_OUT + c, gla_item(c)[2], HALF)
            for c in range(4):
                head_root(act, GLA_OUT + c, HALF)
            for c in range(4):
                j, cols, at = gla_item(c)
                act.wait_ge(gla_gated, c + 1)
                nc.scalar.activation(hT_hi[:, 4 + j, cols], at, ACT.Copy).then_inc(gla_hi_ready, 1)

        def gla_norm_vector(dve):
            for c in range(4):
                j, cols, at = gla_item(c)
                head_norm(dve, GLA_OUT + c, at, head_gains[:, 4:5], HALF)
                dve.wait_ge(head_normed, GLA_OUT + c + 1)
                nc.vector.tensor_tensor(at, at, ggT[:, j, cols], ALU.mult).then_inc(gla_gated, 1)
            for c in range(4):
                j, cols, at = gla_item(c)
                dve.wait_ge(gla_hi_ready, c + 1)
                nc.vector.tensor_tensor(hT_lo[:, 4 + j, cols], at, hT_hi[:, 4 + j, cols].bitcast(F32),
                                        ALU.subtract).then_inc(gla_lo_ready, 1)

        def out_tensor(pe):
            for c in range(4):
                head_sum(pe, GLA_OUT + c, HALF)
            pe.wait_ge(y_lo_ready, 2 * NB)
            for g in range(2 * KT):
                m, h = g // 2, g % 2
                s = (NPROJ + m) % 3
                cols = slice(h * HALF, (h + 1) * HALF)
                pe.wait_ge(p_ready[s], (NPROJ + m) // 3 + 1)
                wait(pe, out_added, g - 3)
                for i, k in enumerate((0, 1, 2, 3, 6, 7, 4, 5)):
                    if k in (4, 5):
                        pe.wait_ge(gla_lo_ready, 2 * (k - 4) + h + 1)
                    kc = slice(k * P, (k + 1) * P)
                    mm = split_product(nc, ps[:, g % 4, :], p_hi[:, s, kc], p_lo[:, s, kc],
                                       hT_hi[:, k, cols], hT_lo[:, k, cols], i == 0, i == KT - 1)
                mm.then_inc(proj_ready, 1)

        def out_unit_scalar(act, u):
            unit_scalar(act, u)

        def out_scalar(act):
            for u in range(NPROJ, NPROJ + 3):
                unit_scalar(act, u)
            gla_norm_scalar(act)
            for m in range(KT):
                if m + 3 < KT:
                    unit_scalar(act, NPROJ + m + 3)
                for h in range(NHALF):
                    norm_square(act, 2, m, h)

        def out_vector(dve):
            for u in range(NPROJ, NPROJ + 3):
                unit_vector(dve, u)
            gla_norm_vector(dve)
            for g in range(2 * KT):
                m, h = g // 2, g % 2
                dve.wait_ge(proj_ready, NG + g + 1)
                nc.vector.tensor_tensor(part(xT, m, h), ps[:, g % 4, :], part(xT, m, h), ALU.add
                                        ).then_inc(out_added, 1)
                if h == 1 and m + 3 < KT:
                    unit_vector(dve, NPROJ + m + 3)

        def x_sync(sp):
            for c in range(4):
                h, ms = c // 2, slice(4 * (c % 2), 4 * (c % 2) + 4)
                sp.dma_start(xT[:, ms, h * HALF:(h + 1) * HALF],
                             x_in.rearrange("(m p) t -> p m t", p=P)[:, ms, h * HALF:(h + 1) * HALF]
                             ).then_inc(x_landed[c], 16)

        def y_sync(sp):
            for g in range(2 * KT):
                m, h = g // NHALF, g % NHALF
                sp.wait_ge(down_added, Base(NFFN).down - 2 * KT + g + 1)
                sp.dma_start(out[m * P:(m + 1) * P, h * HALF:(h + 1) * HALF], part(xT, m, h)).then_inc(y_stored, 16)
            sp.wait_ge(y_stored, 16 * 2 * KT)

        block = ctx.enter_context(nc.Block())

        @block.sync
        def _(sp):
            x_sync(sp)
            ffn_sync(sp, 0)
            sp.wait_ge(w_ready[SLOT["db"]], PAIRS)
            sp.wait_ge(down_ready, Base(1).down)
            sp.dma_start(memT[:], mem_in.rearrange("(k p) t -> p k t", p=P)).then_inc(mem_landed, 16)
            for u in range(NPROJ):
                unit_sync(sp, u)
            sp.wait_ge(proj_ready, NG)
            sp.wait_ge(bias_stored, 16)
            skewed = bias_dram.rearrange("(h x) -> h x", h=SWA_HEADS)[:, P - 1:P - 1 + P * (ROW - 1)]
            sp.dma_start(bias[:], skewed.rearrange("h (p u) -> p h u", u=ROW - 1)[:, :, 0:2 * P]).then_inc(bias_landed, 16)
            sp.wait_ge(head_normed, len(normed))
            sp.wait_ge(mix_set, 5)
            stage_qk(sp, 0, True)
            stage_v(sp, 0, True)
            each_block(sp, lambda n, first, last: mix_sync(sp, n, first, last))
            sp.wait_ge(y_lo_ready, 2 * NB)
            sp.wait_ge(state_ready, 4 * NB)
            for u in range(NPROJ, NPROJ + KT):
                unit_sync(sp, u)
            sp.wait_ge(proj_ready, NG + 2 * KT)
            ffn_sync(sp, 1)
            y_sync(sp)

        @block.gpsimd
        def _(pool):
            nc.gpsimd.memset(eps[:], EPS).then_inc(const_set, 1)
            nc.gpsimd.memset(ones[:], 1.0).then_inc(const_set, 1)
            nc.gpsimd.memset(rel_bias[:], MASKED).then_inc(const_set, 1)
            for dst, src in consts:
                pool.dma_start(dst, src).then_inc(const_landed, 16)
            pool.wait_ge(const_set, 3)
            pool.dma_start(rel_bias[0:N_BUCKETS, :], rel_bias_in).then_inc(const_landed, 16)
            pool.wait_ge(bias_rows_ready, SWA_HEADS)
            pool.dma_start(bias_dram.rearrange("(h p u) -> p h u", h=SWA_HEADS, p=P), bias_rows[:]).then_inc(bias_stored, 16)
            norm_pool(pool, 0)
            norm_pool(pool, 1)
            mix_start_pool(pool)
            each_block(pool, lambda n, first, last: mix_pool(pool, n, first, last))
            norm_pool(pool, 2)

        @block.scalar
        def _(act):
            act.wait_ge(const_landed, 16 * NCONST)
            act.wait_ge(const_set, 3)
            for m, h in norm_steps(0):
                norm_hi(act, 0, m, h)
                norm_square(act, 0, m, h)
            act.wait_ge(masks_ready, 1)
            act.wait_ge(bias_stored, 16)
            ffn_scalar(act, 0)
            for m, h in norm_steps(1):
                norm_hi(act, 1, m, h)
                norm_square(act, 1, m, h)
            proj_scalar(act)
            act.wait_ge(gate_scanned, NB)
            act.wait_ge(mix_set, 5)
            gla_exps(act, 0)
            each_block(act, lambda n, first, last: mix_scalar(act, n, first, last))
            out_scalar(act)
            for m, h in norm_steps(2):
                norm_hi(act, 2, m, h)
            ffn_scalar(act, 1)

        @block.vector
        def _(dve):
            dve.wait_ge(const_landed, 16 * NCONST)
            for c in (0, 2):
                nc.vector.tensor_scalar(head_gains[:, c:c + 1], head_gains[:, c:c + 1], float(HEAD) ** -0.5, None,
                                        ALU.mult).then_inc(gains_scaled, 1)
            dve.wait_ge(gains_scaled, 2)
            for h in range(SWA_HEADS):
                nc.vector.tensor_scalar(rel_wide[:, h, :], ones[0:N_BUCKETS + 1, :], rel_bias[:, h:h + 1], None,
                                        ALU.mult).then_inc(rel_wide_ready, 1)
            nc.vector.tensor_copy(masks[:], masks_f[:]).then_inc(masks_ready, 1)
            for h in range(SWA_HEADS):
                dve.wait_ge(bias_turned, h + 1)
                nc.vector.tensor_copy(bias_rows[:, h, :], ps[:, h, 0:ROW]).then_inc(bias_rows_ready, 1)
            for m, h in norm_steps(0):
                norm_vector(dve, 0, m, h)
            ffn_vector(dve, 0)
            for g in range(2 * KT):
                down_add(dve, 0, PAIRS - 1, g)
                if g >= 2:
                    norm_vector(dve, 1, *norm_steps(1)[g - 2])
            for g in (2 * KT - 2, 2 * KT - 1):
                norm_vector(dve, 1, *norm_steps(1)[g])
            proj_vector(dve)
            dve.wait_ge(gate_scanned, NB)
            dve.wait_ge(mix_set, 5)
            gla_diffs(dve, 0)
            gla_factors(dve, 0)
            dve.wait_ge(bias_landed, 16)
            each_block(dve, lambda n, first, last: mix_vector(dve, n, first, last))
            out_vector(dve)
            for m, h in norm_steps(2):
                norm_vector(dve, 2, m, h)
            ffn_vector(dve, 1)
            for g in range(2 * KT):
                down_add(dve, Base(1).down, PAIRS - 1, g)

        @block.tensor
        def _(pe):
            pe.wait_ge(const_landed, 16 * NCONST)
            pe.wait_ge(rel_wide_ready, SWA_HEADS)
            for h in range(SWA_HEADS):
                nc.tensor.matmul(ps[:, h, 0:ROW], rel_wide[:, h, :], bucket_of[:, :], start=True, stop=True
                                 ).then_inc(bias_turned, 1)
            pe.wait_ge(bias_rows_ready, SWA_HEADS)
            ffn_tensor(pe, 0)
            proj_tensor(pe)
            each_block(pe, lambda n, first, last: mix_tensor(pe, n, first, last))
            out_tensor(pe)
            ffn_tensor(pe, 1)


def _columns(w):
    return np.ascontiguousarray(w.reshape(KT, P, -1, P).transpose(2, 1, 0, 3)).reshape(-1, D)


def _bucket_of():
    exact = N_BUCKETS // 2
    hot = np.zeros((N_BUCKETS + 1, ROW), np.float32)
    for u in range(ROW):
        dist = 2 * P - 1 - u
        if not 0 <= dist < P:
            hot[N_BUCKETS, u] = 1
            continue
        large = exact + int(np.float32(np.log(np.float32(max(dist, 1) / exact))) / np.float32(np.log(MAX_DISTANCE / exact))
                            * (N_BUCKETS - exact))
        hot[dist if dist < exact else min(large, N_BUCKETS - 1), u] = 1
    return hot


def _masks():
    i, j = np.arange(P)[None, :], np.arange(P)[:, None]
    out = np.zeros((P, LEVELS, P), np.float32)
    for l in range(LEVELS):
        s = P >> (l + 1)
        out[:, l, :] = (i // (2 * s) == j // (2 * s)) & (i % (2 * s) >= s) & (j % (2 * s) < s) if s else i == j
    return out


def kernel(**inputs):
    import concourse.bacc as _bacc
    from concourse.bass_utils import run_bass_kernel_spmd as _run

    a = {n: np.asarray(v) for n, v in inputs.items()}
    w_in = a["w_in"][0]
    at = {"q": 0, "k": 512, "v": 640, "gq": 768, "gk": 896, "gv": 1024, "gg": 1280, "glr": 1536, "mq": 1552}

    def columns_of(n):
        if n[0] == "q":
            j = int(n[1])
            return np.r_[HEAD * j:HEAD * (j + 1), 4 * HEAD + HEAD * j:4 * HEAD + HEAD * (j + 1)]
        base = n.rstrip("0123")
        start = at[base] + P * int(n[len(base):] or 0)
        return np.arange(start, start + P)

    picked = np.concatenate([columns_of(n) for n in PROJ if n[:2] not in ("mk", "mv")])
    w_out = a["w_out"][0]
    swa_rows = w_out[:SWA_HEADS * HEAD].reshape(2, 4, HEAD, D).transpose(1, 0, 2, 3).reshape(-1, D)
    per_tile = lambda g: g.reshape(-1, KT, P).transpose(2, 0, 1)
    twice = lambda g: np.concatenate([g, g])
    arrays = {
        "x": a["x"][0].T,
        "mem": a["mem"][0].T,
        "w_gate1": _columns(a["ffn1_w_gate"][0]), "w_up1": _columns(a["ffn1_w_up"][0]), "w_down1": a["ffn1_w_down"][0],
        "w_proj": _columns(w_in[:, picked]),
        "w_mem": _columns(a["w_mem_kv"][0]),
        "w_out": _columns(np.concatenate([swa_rows, w_out[SWA_HEADS * HEAD:]])),
        "w_gate2": _columns(a["ffn2_w_gate"][0]), "w_up2": _columns(a["ffn2_w_up"][0]), "w_down2": a["ffn2_w_down"][0],
        "gains": per_tile(np.stack([a["ffn1_norm"][0], a["mix_norm"][0], a["ffn2_norm"][0]])),
        "mem_gain": per_tile(a["mem_norm"][0])[:, 0],
        "head_gains": np.stack([twice(a[n][0]) for n in ("swa_q_norm", "swa_k_norm", "mem_q_norm", "mem_k_norm",
                                                         "gla_out_norm")], axis=1),
        "sinks": a["swa_sinks"][0],
        "rel_bias": a["rel_bias"],
        "bucket_of": _bucket_of(),
        "gate_up": a["gla_w_gate_up"][0],
        "gate_bias": a["gla_b_gate"][0][:, None],
        "masks": _masks(),
        "ident": np.eye(P, dtype=np.float32),
        "head_ones": np.kron(np.eye(2, dtype=np.float32), np.ones((HEAD, HEAD), np.float32)),
    }
    nc = _bacc.Bacc("TRN2", target_bir_lowering=False, num_devices=1)
    feeds, args = {}, []
    for name, v in arrays.items():
        v = np.ascontiguousarray(v)
        feeds[f"in_{name}"] = v
        args.append(nc.dram_tensor(f"in_{name}", v.shape, mybir.dt.from_np(v.dtype), kind="ExternalInput").ap())
    args.append(nc.dram_tensor("out_y", (D, T), F32, kind="ExternalOutput").ap())
    build(nc, *args)
    r = _run(nc, [feeds], core_ids=[0])
    return np.ascontiguousarray(r.results[0]["out_y"].T)[None]
```

```python
from contextlib import ExitStack

import numpy as np

import concourse.bass as bass
from concourse import mybir

F32 = mybir.dt.float32
F32R = mybir.dt.float32r
U8 = mybir.dt.uint8
ALU = mybir.AluOpType
ACT = mybir.ActivationFunctionType
AX = mybir.AxisListType

P = 128
D = 1024
T = 1024
KT = D // P
HALF = 512
NHALF = T // HALF
F = 2816
PAIRS = F // (2 * P)
EPS = 1e-6
MEM = 256
NB = T // P
HEAD = 64
SWA_HEADS = 8
N_BUCKETS = 32
MAX_DISTANCE = 128
ROW = 3 * P
GLA_DK, GLA_DV, GLA_RANK, GLA_TAU = 32, 64, 16, 16.0
LEVELS = 8
MASKED = -1e30
PROJ = ["v", "gv0", "gv1", "gk", "gq", "glr", "mv0", "mv1", "mk0", "mk1", "k",
        "q0", "q1", "q2", "q3", "mq0", "mq1", "gg0", "gg1"]
NSPLIT = 3


def split_product(nc, out, w_hi, w_lo, x_hi, x_lo, first, last):
    nc.tensor.matmul(out, w_hi, x_hi, start=first, stop=False)
    nc.tensor.matmul(out, w_hi, x_lo, start=False, stop=False)
    return nc.tensor.matmul(out, w_lo, x_hi, start=False, stop=last)


def build(nc, x_in, mem_in, w_gate1, w_up1, w_down1, w_proj, w_mem, w_out, w_gate2, w_up2, w_down2, gains_in,
          mem_gain_in, head_gains_in, sinks_in, rel_bias_in, bucket_of_in, gate_up_in, gate_bias_in, masks_in, ident_in, head_ones_in, out):
    ctx = ExitStack()
    with ctx:
        sb = lambda name, shape, dt=F32: ctx.enter_context(nc.sbuf_tensor(name, shape, dt))
        sem = lambda name: ctx.enter_context(nc.semaphore(name))

        def phase(*tensors):
            with ExitStack() as stack:
                return [stack.enter_context(nc.sbuf_tensor(name, shape, dt)) for name, shape, dt in tensors]

        xT = sb("xT", [P, KT, T])
        hT_hi = sb("hT_hi", [P, KT, T], F32R)
        hT_lo = sb("hT_lo", [P, KT, T], F32R)
        glu = sb("glu", [P, NHALF, HALF])
        rstd = sb("rstd", [P, T])
        ident = sb("ident", [P, P])
        ones = sb("ones", [P, P])
        head_ones = sb("head_ones", [P, P])
        eps = sb("eps", [P, 1])
        gains = sb("gains", [P, 3, KT])
        mem_gain = sb("mem_gain", [P, KT])
        head_gains = sb("head_gains", [P, 5])
        sinks = sb("sinks", [P, SWA_HEADS])
        gate_bias = sb("gate_bias", [P, 1])
        gate_up_w = sb("gate_up_w", [GLA_RANK, P])
        masks = sb("masks", [P, LEVELS, P], U8)
        rstd_tok = sb("rstd_tok", [P, KT + 2])

        bias_dram = nc.dram_tensor("bias_dram", (SWA_HEADS * P * ROW,), F32, kind="Internal").ap()

        (raw_a, hi_a, lo_a, act_hi, act_lo, hi_d, lo_d, hi_b, lo_b, raw_d, raw_b) = phase(
            ("raw_a", [P, 2, D], F32), ("hi_a", [P, 2, D], F32R), ("lo_a", [P, 2, D], F32R),
            ("act_hi", [P, 3, T], F32R), ("act_lo", [P, 3, T], F32R),
            ("hi_d", [P, 2, D], F32R), ("lo_d", [P, 2, D], F32R), ("hi_b", [P, 2, D], F32R),
            ("lo_b", [P, 2, D], F32R), ("raw_d", [P, 2, D], F32), ("raw_b", [P, 2, D], F32))
        w_raw = [t[:, i, :] for t in (raw_a, raw_d, raw_b) for i in range(2)]
        w_hi = [t[:, i, :] for t in (hi_a, hi_d, hi_b) for i in range(2)]
        w_lo = [t[:, i, :] for t in (lo_a, lo_d, lo_b) for i in range(2)]

        _, rel_bias, bucket_of, bias_row, masks_f = phase(
            ("start_skip", [P, 6, D], F32), ("rel_bias", [N_BUCKETS + 1, SWA_HEADS], F32),
            ("bucket_of", [N_BUCKETS + 1, ROW], F32), ("bias_row", [SWA_HEADS, ROW], F32),
            ("masks_f", [P, LEVELS, P], F32))

        memT, memT_hi, memT_lo = phase(
            ("memT", [P, KT, MEM], F32), ("memT_hi", [P, KT, MEM], F32R), ("memT_lo", [P, KT, MEM], F32R))
        with ExitStack() as mix:
            msb = lambda name, shape, dt=F32: mix.enter_context(nc.sbuf_tensor(name, shape, dt))
            qT = msb("qT", [P, 4, T])
            mqT = msb("mqT", [P, 2, T])
            kT = msb("kT", [P, T])
            mkT = msb("mkT", [P, 2, MEM])
            mv = msb("mv", [P, 2, 2 * P])
            vg = msb("vg", [P, NB, 3 * P])
            gqk = msb("gqk", [P, 2, T])
            bT = msb("bT", [P, T])
            ggT = msb("ggT", [P, 2, T])
            p_hi, p_lo, p_raw = phase(
                ("p_hi", [P, 3, D], F32R), ("p_lo", [P, 3, D], F32R), ("p_raw", [P, 3, D], F32))
            (gk_lv, gq_lv, q_st, mq_st, k_st, Pg1, A_T, v_st, gv_st, k_hat, k_hat_tok, q_hat,
             decay, state, row_max, shift, sink_shift, sink_exp, row_sum, row_inv) = phase(
                ("gk_lv", [P, LEVELS, P], F32), ("gq_lv", [P, LEVELS, P], F32),
                ("q_st", [P, 4, P], F32), ("mq_st", [P, 2, P], F32), ("k_st", [P, 2 * P], F32),
                ("Pg1", [P, 4, 2 * P], F32), ("A_T", [P, 4, P], F32),
                ("v_st", [P, 2, P], F32), ("gv_st", [P, 2 * P], F32),
                ("k_hat", [P, P], F32), ("k_hat_tok", [P, P], F32), ("q_hat", [P, P], F32),
                ("decay", [P, P], F32), ("state", [P, 4 * GLA_DV], F32),
                ("row_max", [P, 8], F32), ("shift", [P, 12], F32), ("sink_shift", [P, 8], F32),
                ("sink_exp", [P, 8], F32), ("row_sum", [P, 12], F32), ("row_inv", [P, 12], F32))
            _, bias, Pg0 = phase(
                ("mix_skip", [P, 6, D], F32),
                ("bias", [P, SWA_HEADS, 2 * P], F32),
                ("Pg0", [P, 4, 2 * P], F32))
        P_of = [Pg0[:], Pg1[:], rstd[:].rearrange("p (h k) -> p h k", h=4)]
        PT = glu

        ps = ctx.enter_context(nc.psum_tensor("ps", [P, 8, HALF], F32))
        BANK_GATE, BANK_UP, BANK_DOWN, BANK_NORM = 0, 2, 4, 6

        NPROJ = len(PROJ)
        MEM_UNITS = ["mk0", "mk1", "mv0", "mv1"]
        X_UNITS = [n for n in PROJ if n not in MEM_UNITS]
        gains_scaled, masks_ready = sem("gains_scaled"), sem("masks_ready")
        dve_passed, pool_passed = sem("dve_passed"), sem("pool_passed")
        mem_landed, bias_stored, bias_landed = sem("mem_landed"), sem("bias_stored"), sem("bias_landed")
        gains_landed, rel_bias_landed = sem("gains_landed"), sem("rel_bias_landed")
        bias_row_summed, bias_row_ready = sem("bias_row_summed"), sem("bias_row_ready")
        p_landed = [sem(f"p_landed{i}") for i in range(3)]
        p_hi_ready = [sem(f"p_hi_ready{i}") for i in range(3)]
        p_ready = [sem(f"p_ready{i}") for i in range(3)]
        (tok_summed, proj_ready, proj_taken, mem_hi_ready, mem_lo_ready, mem_split, mem_summed, mem_rooted, mem_normed, gate_ready,
         gate_min, gate_log, gate_summed, gate_scanned, head_squared, head_summed, head_rooted, head_normed,
         out_gate_ready, out_added, gla_gated, gla_hi_ready, gla_lo_ready, mix_set, head_inverted) = [sem(n) for n in (
            "tok_summed proj_ready proj_taken mem_hi_ready mem_lo_ready mem_split mem_summed mem_rooted mem_normed gate_ready "
            "gate_min gate_log gate_summed gate_scanned head_squared head_summed head_rooted head_normed "
            "out_gate_ready out_added gla_gated gla_hi_ready gla_lo_ready mix_set head_inverted").split()]
        (staged_q, staged_k, staged_mq, staged_v, staged_gv, scores_ready, biased, shift_ready, probs_ready, denom, scaled,
         turned, pt0_ready, pt1_ready, pv_done, y_hi_ready, y_lo_ready, level_ready, level_taken, gla_diff, gla_exp,
         gla_factor, k_hat_turned, k_hat_copied, kv_ready, state_ready, o_ready, o_copied) = [sem(n) for n in (
            "staged_q staged_k staged_mq staged_v staged_gv scores_ready biased shift_ready probs_ready denom scaled "
            "turned pt0_ready pt1_ready pv_done y_hi_ready y_lo_ready level_ready level_taken gla_diff gla_exp "
            "gla_factor k_hat_turned k_hat_copied kv_ready state_ready o_ready o_copied").split()]
        const_landed = sem("const_landed")
        const_set = sem("const_set")
        x_landed = [sem(f"x_landed{i}") for i in range(4)]
        consts = [(mem_gain[:], mem_gain_in), (head_gains[:], head_gains_in),
                  (sinks[:], sinks_in.rearrange("(a n) -> a n", a=1).to_broadcast([P, SWA_HEADS])),
                  (gate_bias[:], gate_bias_in), (gate_up_w[:], gate_up_in),
                  (ident[:], ident_in), (masks_f[:], masks_in), (head_ones[:], head_ones_in)]
        NCONST = len(consts)
        h_hi_ready = sem("h_hi_ready")
        h_ready = sem("h_ready")
        squared = sem("squared")
        sumsq_added = sem("sumsq_added")
        sumsq0_added = sem("sumsq0_added")
        norm_summed = sem("norm_summed")
        norm_rooted = sem("norm_rooted")
        rstd_ready = sem("rstd_ready")
        w_landed = [sem(f"w_landed{i}") for i in range(6)]
        w_hi_ready = [sem(f"w_hi_ready{i}") for i in range(6)]
        w_ready = [sem(f"w_ready{i}") for i in range(6)]
        gate_up_ready = sem("gate_up_ready")
        gate_scaled = sem("gate_scaled")
        gate_silu = sem("gate_silu")
        up_scaled = sem("up_scaled")
        glu_ready = sem("glu_ready")
        act_hi_ready = sem("act_hi_ready")
        act_ready = sem("act_ready")
        down_ready = sem("down_ready")
        down_added = sem("down_added")
        y_stored = sem("y_stored")

        SLOT = dict(ga=0, ua=1, da=2, db=3, gb=4, ub=5)

        def wait(eng, s, value):
            if isinstance(value, int) and value <= 0:
                return
            eng.wait_ge(s, value)

        ffn_weights = [(w_gate1, w_up1, w_down1), (w_gate2, w_up2, w_down2)]
        NFFN = 2

        class Base:
            def __init__(self, f):
                self.use = f * PAIRS
                self.gu = f * PAIRS * 4
                self.down = f * PAIRS * 2 * KT

        def load_slot(sp, f, name, k):
            b, s = Base(f), SLOT[name]
            wait(sp, w_ready[s], k + b.use)
            wg, wu, wd = ffn_weights[f]
            ab = 1 if name[1] == "b" else 0
            if name[0] == "d":
                src = wd[bass.ds((2 * k + ab) * P, P), :]
                dst = w_raw[s]
            else:
                w = wg if name[0] == "g" else wu
                src = w[bass.ds((2 * k + ab) * P, P), :]
                dst = w_raw[s]
            sp.dma_start(dst, src).then_inc(w_landed[s], 16)

        def each_pair(eng, body):
            body(0, 0, True, False)
            with eng.Fori(1, PAIRS - 2, 2) as i:
                body(i, 1, False, False)
                body(i + 1, 0, False, False)
            body(PAIRS - 2, 1, False, False)
            body(PAIRS - 1, 0, False, True)

        def ffn_sync(sp, f):
            def body(i, par, first, last):
                if not first:
                    for name in ("ga", "ua"):
                        load_slot(sp, f, name, i)
                    for name in ("da", "db"):
                        load_slot(sp, f, name, i - 1)
                    for name in ("gb", "ub"):
                        load_slot(sp, f, name, i)
            each_pair(sp, body)
            for name in ("da", "db"):
                load_slot(sp, f, name, PAIRS - 1)

        def freed(eng, f, name, k):
            b = Base(f)
            if name[0] == "d":
                wait(eng, down_ready, b.down + 2 * KT * k)
            else:
                wait(eng, gate_up_ready, b.gu + 4 * k - (2 if name[1] == "a" else 0))

        def weight_hi(act, f, name, k):
            b, s = Base(f), SLOT[name]
            wait(act, w_landed[s], 16 * (k + b.use) + 16)
            freed(act, f, name, k)
            nc.scalar.activation(w_hi[s], w_raw[s], ACT.Copy).then_inc(w_hi_ready[s], 1)

        def weight_lo(dve, f, name, k):
            b, s = Base(f), SLOT[name]
            wait(dve, w_hi_ready[s], k + b.use + 1)
            nc.vector.tensor_tensor(w_lo[s], w_raw[s], w_hi[s].bitcast(F32),
                                    ALU.subtract).then_inc(w_ready[s], 1)

        def ffn_scalar(act, f):
            b = Base(f)

            def act_slot(par, t):
                return 2 if t else par

            def glu_steps(i, par, t):
                for h in range(NHALF):
                    q = b.gu + 4 * i + 2 * t + h
                    wait(act, gate_scaled, q + 1)
                    nc.scalar.activation(ps[:, BANK_GATE + h, :], ps[:, BANK_GATE + h, :],
                                         ACT.Silu).then_inc(gate_silu, 1)
                    wait(act, glu_ready, q + 1)
                    wait(act, down_ready, b.down + 2 * KT * (i if t else i - 1))
                    nc.scalar.activation(act_hi[:, act_slot(par, t), h * HALF:(h + 1) * HALF], glu[:, h, :],
                                         ACT.Copy).then_inc(act_hi_ready, 1)

            def body(i, par, first, last):
                weight_hi(act, f, "gb", i)
                weight_hi(act, f, "ub", i)
                if first:
                    norm_root(act, 2 * f)
                glu_steps(i, par, 0)
                if not last:
                    weight_hi(act, f, "ga", i + 1)
                    weight_hi(act, f, "ua", i + 1)
                weight_hi(act, f, "da", i)
                weight_hi(act, f, "db", i)
                glu_steps(i, par, 1)
                if f == 0 and last:
                    for u in range(3):
                        unit_scalar(act, u)
            each_pair(act, body)

        def ffn_vector(dve, f):
            b = Base(f)

            def glu_steps(i, par, t):
                for h in range(NHALF):
                    q = b.gu + 4 * i + 2 * t + h
                    cols = slice(h * HALF, (h + 1) * HALF)
                    slot = 2 if t else par
                    wait(dve, gate_up_ready, q + 1)
                    nc.vector.tensor_tensor(ps[:, BANK_GATE + h, :], ps[:, BANK_GATE + h, :], rstd[:, cols],
                                            ALU.mult).then_inc(gate_scaled, 1)
                    nc.vector.tensor_tensor(glu[:, h, :], ps[:, BANK_UP + h, :], rstd[:, cols],
                                            ALU.mult).then_inc(up_scaled, 1)
                    wait(dve, up_scaled, q + 1)
                    wait(dve, gate_silu, q + 1)
                    nc.vector.tensor_tensor(glu[:, h, :], ps[:, BANK_GATE + h, :], glu[:, h, :],
                                            ALU.mult).then_inc(glu_ready, 1)
                    wait(dve, act_hi_ready, q + 1)
                    nc.vector.tensor_tensor(act_lo[:, slot, cols], glu[:, h, :],
                                            act_hi[:, slot, cols].bitcast(F32),
                                            ALU.subtract).then_inc(act_ready, 1)

            def body(i, par, first, last):
                weight_lo(dve, f, "gb", i)
                weight_lo(dve, f, "ub", i)
                if first:
                    norm_recip(dve, 2 * f)
                glu_steps(i, par, 0)
                for g in range(2 * KT):
                    if not first:
                        down_add(dve, b.down, i - 1, g)
                    if g == 6 and not last:
                        weight_lo(dve, f, "ga", i + 1)
                    if g == 11 and not last:
                        weight_lo(dve, f, "ua", i + 1)
                weight_lo(dve, f, "da", i)
                weight_lo(dve, f, "db", i)
                glu_steps(i, par, 1)
            each_pair(dve, body)

        def down_add(dve, base, j, g):
            m, h = g // NHALF, g % NHALF
            r = base + 2 * KT * j + g
            dst = xT[:, m, h * HALF:(h + 1) * HALF]
            wait(dve, down_ready, r + 1)
            nc.vector.scalar_tensor_tensor(out=dst, in0=ps[:, BANK_DOWN + g % 4, :], scalar=0.5, in1=dst,
                                           op0=ALU.mult, op1=ALU.add).then_inc(down_added, 1)

        def ffn_tensor(pe, f):
            b = Base(f)

            def gate_up(i, t):
                g, u = (("ga", "ua"), ("gb", "ub"))[t]
                for h in range(NHALF):
                    q = b.gu + 4 * i + 2 * t + h
                    wait(pe, glu_ready, q - 1)
                    for name, bank in ((g, BANK_GATE + h), (u, BANK_UP + h)):
                        s = SLOT[name]
                        if h == 0:
                            wait(pe, w_ready[s], b.use + i + 1)
                        for k in range(KT):
                            if isinstance(i, int) and i == 0 and t == 0 and name[0] == "g":
                                pe.wait_ge(h_ready, split_count(2 * f, k, h))
                            cols, rows = slice(k * P, (k + 1) * P), slice(h * HALF, (h + 1) * HALF)
                            mm = split_product(nc, ps[:, bank, :], w_hi[s][:, cols], w_lo[s][:, cols],
                                               hT_hi[:, k, rows], hT_lo[:, k, rows], k == 0, k == KT - 1)
                    mm.then_inc(gate_up_ready, 1)
                    if isinstance(i, int) and i == 0 and t == 0 and h == 0:
                        norm_sum(pe, 2 * f)

            def down(j, par):
                wait(pe, act_ready, b.gu + 4 * j + 4)
                for s in (SLOT["da"], SLOT["db"]):
                    wait(pe, w_ready[s], b.use + j + 1)
                for g in range(2 * KT):
                    m, h = g // NHALF, g % NHALF
                    if g >= 4:
                        pe.wait_ge(down_added, b.down + 2 * KT * j + g - 3)
                    for t in range(2):
                        s, slot = SLOT[("da", "db")[t]], (par, 2)[t]
                        cols, rows = slice(m * P, (m + 1) * P), slice(h * HALF, (h + 1) * HALF)
                        mm = split_product(nc, ps[:, BANK_DOWN + g % 4, :], w_hi[s][:, cols], w_lo[s][:, cols],
                                           act_hi[:, slot, rows], act_lo[:, slot, rows], t == 0, t == 1)
                    mm.then_inc(down_ready, 1)

            def body(i, par, first, last):
                gate_up(i, 0)
                if not first:
                    down(i - 1, 1 - par)
                gate_up(i, 1)
            each_pair(pe, body)
            down(PAIRS - 1, 0)

        def norm_steps(n):
            if n != 1:
                return [(m, h) for h in range(NHALF) for m in range(KT)]
            return [(m, h) for m in range(KT) for h in range(NHALF)]

        def split_count(n, m, h):
            return 2 * KT * n + norm_steps(n).index((m, h)) + 1

        def norm_sum(pe, n):
            if n == 0:
                pe.wait_ge(sumsq0_added, KT)
            for h in range(NHALF):
                pe.wait_ge(sumsq_added, sumsq_count(n))
                nc.tensor.matmul(ps[:, BANK_NORM + h, :], ones[:, :], rstd[:, h * HALF:(h + 1) * HALF],
                                 start=True, stop=True).then_inc(norm_summed, 1)

        def norm_root(act, n):
            for h in range(NHALF):
                bank = ps[:, BANK_NORM + h, :]
                act.wait_ge(norm_summed, NHALF * n + h + 1)
                nc.scalar.activation(bank, bank, ACT.Sqrt, bias=eps[:, 0:1], scale=1.0 / D).then_inc(norm_rooted, 1)

        def norm_recip(dve, n):
            for h in range(NHALF):
                dve.wait_ge(norm_rooted, NHALF * n + h + 1)
                nc.vector.reciprocal(rstd[:, h * HALF:(h + 1) * HALF],
                                     ps[:, BANK_NORM + h, :]).then_inc(rstd_ready, 1)
            dve.wait_ge(rstd_ready, NHALF * (n + 1))

        def part(tensor, m, h):
            return tensor[:, m, h * HALF:(h + 1) * HALF]

        def norm_hi(act, n, m, h):
            if n == 0:
                act.wait_ge(x_landed[2 * h + m // 4], 16)
            elif n == 1:
                act.wait_ge(down_added, Base(1).down - 2 * KT + 2 * m + h + 1)
            else:
                act.wait_ge(out_added, 2 * KT)
                act.wait_ge(proj_ready, NG + 2 * KT)
            nc.scalar.activation(part(hT_hi, m, h), part(xT, m, h), ACT.Copy,
                                 scale=gains[:, n, m:m + 1]).then_inc(h_hi_ready, 1)

        def square_steps(n):
            return [(m, h) for m in range(KT) for h in range(NHALF)] if n else norm_steps(0)

        def square_count(n, m, h):
            return 2 * KT * n + square_steps(n).index((m, h)) + 1

        def sumsq_count(n):
            return KT + 2 * KT * n

        def norm_square(act, n, m, h):
            c = square_count(n, m, h)
            if n == 2:
                act.wait_ge(out_added, max(out_count(2 * m), out_count(2 * m + 1)))
            if n == 0 and c - 2 > KT:
                act.wait_ge(sumsq0_added, c - 2 - KT)
            else:
                wait(act, sumsq_added, c - 2 - (KT if n else 0))
                if n == 1 and m == 0:
                    act.wait_ge(sumsq0_added, KT)
            nc.scalar.activation(glu[:, c % 2, :], part(xT, m, h), ACT.Square).then_inc(squared, 1)

        def norm_vector(dve, n, m, h):
            dve.wait_ge(h_hi_ready, split_count(n, m, h))
            nc.vector.scalar_tensor_tensor(out=part(hT_lo, m, h), in0=part(xT, m, h), scalar=gains[:, n, m:m + 1],
                                           in1=part(hT_hi, m, h).bitcast(F32), op0=ALU.mult,
                                           op1=ALU.subtract).then_inc(h_ready, 1)

        def sumsq0_vector(dve):
            acc = rstd[:, HALF:T]
            for m in range(KT):
                dve.wait_ge(squared, KT + m + 1)
                sq = glu[:, (KT + m + 1) % 2, :]
                if m == 0:
                    nc.vector.tensor_copy(acc, sq).then_inc(sumsq0_added, 1)
                else:
                    dve.wait_ge(sumsq0_added, m)
                    nc.vector.tensor_tensor(acc, acc, sq, ALU.add).then_inc(sumsq0_added, 1)

        def norm_pool(pool, n):
            for m, h in square_steps(n):
                if n == 0 and h == 1:
                    continue
                c = square_count(n, m, h)
                acc = rstd[:, h * HALF:(h + 1) * HALF]
                pool.wait_ge(squared, c)
                if m == 0:
                    nc.gpsimd.tensor_scalar(acc, glu[:, c % 2, :], 1.0, 1.0, ALU.mult, ALU.mult).then_inc(sumsq_added, 1)
                else:
                    pool.wait_ge(sumsq_added, c - 1 - (KT if n else 0))
                    nc.gpsimd.tensor_tensor(acc, acc, glu[:, c % 2, :], ALU.add).then_inc(sumsq_added, 1)

        def unit_sync(sp, u):
            wait(sp, p_ready[u % 3], u // 3)
            n = PROJ[u] if u < NPROJ else None
            if n is None:
                src = w_out[(u - NPROJ) * P:(u - NPROJ + 1) * P, :]
            elif n in MEM_UNITS:
                i = MEM_UNITS.index(n)
                src = w_mem[i * P:(i + 1) * P, :]
            else:
                i = X_UNITS.index(n)
                src = w_proj[i * P:(i + 1) * P, :]
            sp.dma_start(p_raw[:, u % 3, :], src).then_inc(p_landed[u % 3], 16)

        def unit_free(u):
            return last_group[u - 3] if u >= 3 else 0

        def unit_scalar(act, u):
            s = u % 3
            act.wait_ge(p_landed[s], 16 * (u // 3 + 1))
            if u < 3:
                act.wait_ge(gate_up_ready, Base(1).gu)
            if NPROJ <= u < NPROJ + 3:
                act.wait_ge(level_ready, 2 * NB)
                act.wait_ge(scores_ready, 3 * NB)
            wait(act, proj_ready, unit_free(u))
            nc.scalar.activation(p_hi[:, s, :], p_raw[:, s, :], ACT.Copy).then_inc(p_hi_ready[s], 1)

        def unit_vector(dve, u, engine=None):
            s = u % 3
            dve.wait_ge(p_hi_ready[s], u // 3 + 1)
            (engine or nc.vector).tensor_tensor(p_lo[:, s, :], p_raw[:, s, :], p_hi[:, s, :].bitcast(F32),
                                    ALU.subtract).then_inc(p_ready[s], 1)

        groups = [("v", t) for t in range(NB)]
        for n in PROJ[3:]:
            if n == "mv0":
                groups += [("mv", 0), ("mv", 1)]
            elif n == "mv1":
                pass
            elif n in ("mk0", "mk1"):
                groups += [(n, 0)]
            else:
                groups += [(n, h) for h in range(NHALF)]
        gi = {g: i for i, g in enumerate(groups)}
        NG = len(groups)

        def units_of(name):
            return {"v": [0, 1, 2], "mv": [6, 7]}.get(name) or [PROJ.index(name)]

        OUT_ORDER = [0, 2, 1, 3] + list(range(4, 2 * KT))

        def out_count(g):
            return OUT_ORDER.index(g) + 1

        last_group = {}
        for i, (n, _) in enumerate(groups):
            for u in units_of(n):
                last_group[u] = i + 1
        for m in range(KT):
            last_group[NPROJ + m] = NG + max(out_count(2 * m), out_count(2 * m + 1))

        normed = [("mk0", 0), ("mk1", 0)] + [(n, h) for n in ("k", "q0", "q1", "q2", "q3", "mq0", "mq1")
                                             for h in range(NHALF)]

        def normed_at(i):
            n, h = normed[i]
            cols = slice(h * HALF, (h + 1) * HALF)
            if n[:2] == "mk":
                return mkT[:, int(n[2]), :], head_gains[:, 3:4]
            if n[:2] == "mq":
                return mqT[:, int(n[2]), cols], head_gains[:, 2:3]
            if n[0] == "q":
                return qT[:, int(n[1]), cols], head_gains[:, 0:1]
            return kT[:, cols], head_gains[:, 1:2]

        def width(i):
            return MEM if normed[i][0][:2] == "mk" else HALF

        GLA_OUT = len(normed)

        def head_square(act, i, src, w):
            wait(act, head_summed, i - 1)
            nc.scalar.activation(glu[:, i % 2, 0:w], src, ACT.Square).then_inc(head_squared, 1)

        def head_sum(pe, i, w):
            pe.wait_ge(head_squared, i + 1)
            wait(pe, head_normed, i - 1)
            nc.tensor.matmul(ps[:, 4 + i % 2, 0:w], head_ones[:, :], glu[:, i % 2, 0:w], start=True,
                             stop=True).then_inc(head_summed, 1)

        def head_root(act, i, w):
            act.wait_ge(head_summed, i + 1)
            nc.scalar.activation(ps[:, 4 + i % 2, 0:w], ps[:, 4 + i % 2, 0:w], ACT.Sqrt, bias=eps[:, 0:1],
                                 scale=1.0 / HEAD).then_inc(head_rooted, 1)

        def head_norm(dve, i, at, gain, w):
            dve.wait_ge(head_rooted, i + 1)
            bank = ps[:, 4 + i % 2, 0:w]
            nc.vector.reciprocal(bank, bank).then_inc(head_inverted, 1)
            dve.wait_ge(head_inverted, i + 1)
            nc.vector.scalar_tensor_tensor(out=at, in0=at, scalar=gain, in1=bank, op0=ALU.mult, op1=ALU.mult
                                           ).then_inc(head_normed, 1)

        DELAY = 2

        def delayed(i):
            if i - DELAY < 0:
                return None
            n, h = groups[i - DELAY]
            if n == "glr":
                return ("gate", h)
            if (n, h) in normed:
                return ("norm", normed.index((n, h)))
            return None

        def proj_tensor(pe):
            for i, (n, h) in enumerate(groups):
                us = units_of(n)
                for u in us:
                    pe.wait_ge(p_ready[u % 3], u // 3 + 1)
                wait(pe, proj_taken, i - 3)
                if n in ("mv", "mk0", "mk1"):
                    pe.wait_ge(mem_split, 2)
                for k in range(KT):
                    kc = slice(k * P, (k + 1) * P)
                    if n == "v":
                        pe.wait_ge(h_ready, split_count(1, k, h // 4))
                        tok = slice(h * P, (h + 1) * P)
                        mm = split_product(nc, ps[:, i % 4, 0:3 * P], hT_hi[:, k, tok], hT_lo[:, k, tok],
                                           p_hi[:, 0:3, kc], p_lo[:, 0:3, kc], k == 0, k == KT - 1)
                    elif n == "mv":
                        tok = slice(h * P, (h + 1) * P)
                        mm = split_product(nc, ps[:, i % 4, 0:2 * P], memT_hi[:, k, tok], memT_lo[:, k, tok],
                                           p_hi[:, 0:2, kc], p_lo[:, 0:2, kc], k == 0, k == KT - 1)
                    elif n in ("mk0", "mk1"):
                        s = us[0] % 3
                        mm = split_product(nc, ps[:, i % 4, 0:MEM], p_hi[:, s, kc], p_lo[:, s, kc],
                                           memT_hi[:, k, :], memT_lo[:, k, :], k == 0, k == KT - 1)
                    else:
                        s = us[0] % 3
                        cols = slice(h * HALF, (h + 1) * HALF)
                        mm = split_product(nc, ps[:, i % 4, :], p_hi[:, s, kc], p_lo[:, s, kc],
                                           hT_hi[:, k, cols], hT_lo[:, k, cols], k == 0, k == KT - 1)
                mm.then_inc(proj_ready, 1)
                if i == 1:
                    pe.wait_ge(sumsq_added, sumsq_count(1))
                    pe.wait_ge(down_added, Base(1).down)
                    for t in range(NB):
                        mm = nc.tensor.matmul(ps[:, 5, t:t + 1], rstd[:, t * P:(t + 1) * P], ones[:, 0:1],
                                              start=True, stop=True)
                    mm.then_inc(tok_summed, 1)
                    norm_sum(pe, 1)
                if i == 5:
                    pe.wait_ge(mem_split, 3)
                    pe.wait_ge(mem_normed, 1)
                    for t in range(2):
                        for k in range(KT):
                            nc.tensor.matmul(ps[:, 5, KT + t:KT + t + 1], memT[:, k, t * P:(t + 1) * P],
                                             ones[:, 0:1], start=(k == 0), stop=(k == KT - 1))
                    for k in range(KT):
                        mm = nc.tensor.matmul(ps[:, 4, 0:MEM], ones[:, :], memT[:, k, :], start=(k == 0),
                                              stop=(k == KT - 1))
                    mm.then_inc(mem_summed, 1)
                small = delayed(i)
                if small and small[0] == "gate":
                    g = small[1]
                    pe.wait_ge(proj_taken, gi[("glr", g)] + 1)
                    pe.wait_ge(mem_normed, 3)
                    nc.tensor.matmul(ps[:, 4 + g, :], gate_up_w[:, :], glu[0:GLA_RANK, g, :], start=True,
                                     stop=True).then_inc(gate_ready, 1)
                elif small:
                    j = small[1]
                    if j < 2:
                        pe.wait_ge(gate_summed, 2)
                    head_sum(pe, j, width(j))

        def mem_split_scalar(act):
            act.wait_ge(mem_landed, 16)
            for k in range(KT):
                nc.scalar.activation(memT_hi[:, k, :], memT[:, k, :], ACT.Copy,
                                     scale=mem_gain[:, k:k + 1]).then_inc(mem_hi_ready, 1)

        def mem_split_vector(dve):
            for k in range(KT):
                dve.wait_ge(mem_hi_ready, k + 1)
                nc.vector.scalar_tensor_tensor(out=memT_lo[:, k, :], in0=memT[:, k, :], scalar=mem_gain[:, k:k + 1],
                                               in1=memT_hi[:, k, :].bitcast(F32), op0=ALU.mult,
                                               op1=ALU.subtract).then_inc(mem_lo_ready, 1)

        def proj_scalar(act):
            mem_split_scalar(act)
            act.wait_ge(tok_summed, 1)
            nc.scalar.activation(ps[:, 5, 0:KT], ps[:, 5, 0:KT], ACT.Sqrt, bias=eps[:, 0:1],
                                 scale=1.0 / D).then_inc(mem_rooted, 1)
            norm_root(act, 1)
            act.wait_ge(mem_lo_ready, KT)
            nc.scalar.activation(memT[:], memT[:], ACT.Square).then_inc(mem_split, 3)
            act.wait_ge(mem_summed, 1)
            nc.scalar.activation(ps[:, 5, KT:KT + 2], ps[:, 5, KT:KT + 2], ACT.Sqrt, bias=eps[:, 0:1],
                                 scale=1.0 / D).then_inc(mem_rooted, 1)
            nc.scalar.activation(ps[:, 4, 0:MEM], ps[:, 4, 0:MEM], ACT.Sqrt, bias=eps[:, 0:1],
                                 scale=1.0 / D).then_inc(mem_rooted, 1)
            for i, (n, h) in enumerate(groups):
                for u in prefetch.get(i, []):
                    unit_scalar(act, u)
                if n[:2] == "gg":
                    at = ggT[:, int(n[2]), h * HALF:(h + 1) * HALF]
                    act.wait_ge(proj_taken, i + 1)
                    nc.scalar.activation(at, at, ACT.Silu).then_inc(out_gate_ready, 1)
                if (n, h) in normed:
                    j = normed.index((n, h))
                    act.wait_ge(proj_taken, i + 1)
                    if j == 0:
                        act.wait_ge(gate_ready, 2)
                    head_square(act, j, normed_at(j)[0], width(j))
                small = delayed(i)
                if small and small[0] == "gate":
                    g = small[1]
                    bank = ps[:, 4 + g, :]
                    act.wait_ge(gate_min, g + 1)
                    nc.scalar.activation(bank, bank, ACT.Abs, bias=gate_bias[:, 0:1]).then_inc(gate_log, 1)
                    act.wait_ge(gate_log, 3 * g + 1)
                    nc.scalar.activation(bank, bank, ACT.Exp, scale=-1.0).then_inc(gate_log, 1)
                    act.wait_ge(gate_log, 3 * g + 2)
                    nc.scalar.activation(bank, bank, ACT.Ln, bias=ones[:, 0:1]).then_inc(gate_log, 1)
                elif small:
                    head_root(act, small[1], width(small[1]))

        def proj_vector(dve):
            mem_split_vector(dve)
            dve.wait_ge(mem_rooted, 1)
            nc.vector.reciprocal(rstd_tok[:, 0:KT], ps[:, 5, 0:KT]).then_inc(mem_normed, 1)
            dve.wait_ge(mem_normed, 1)
            for i, (n, h) in enumerate(groups):
                if i == 3:
                    norm_recip(dve, 1)
                if i == NB - 1:
                    dve.wait_ge(mem_rooted, 3)
                    nc.vector.reciprocal(rstd_tok[:, KT:KT + 2], ps[:, 5, KT:KT + 2]).then_inc(mem_normed, 1)
                    nc.vector.reciprocal(memT[:, 0, :], ps[:, 4, 0:MEM]).then_inc(mem_normed, 1)
                    dve.wait_ge(mem_normed, 3)
                for u in prefetch.get(i, []):
                    unit_vector(dve, u)
                dve.wait_ge(proj_ready, i + 1)
                bank = ps[:, i % 4, :]
                cols = slice(h * HALF, (h + 1) * HALF)
                if n == "v":
                    ins = nc.vector.tensor_scalar(vg[:, h, :], bank[:, 0:3 * P], rstd_tok[:, h:h + 1], None, ALU.mult)
                elif n == "mv":
                    ins = nc.vector.tensor_scalar(mv[:, h, :], bank[:, 0:2 * P], rstd_tok[:, KT + h:KT + h + 1], None,
                                                  ALU.mult)
                elif n in ("mk0", "mk1"):
                    ins = nc.vector.tensor_tensor(mkT[:, int(n[2]), :], bank[:, 0:MEM], memT[:, 0, :], ALU.mult)
                elif n == "gq":
                    ins = nc.vector.scalar_tensor_tensor(out=gqk[:, 0, cols], in0=bank, scalar=float(GLA_DK) ** -0.5,
                                                         in1=rstd[:, cols], op0=ALU.mult, op1=ALU.mult)
                elif n == "glr":
                    ins = nc.vector.tensor_tensor(glu[0:GLA_RANK, h, :], bank[0:GLA_RANK, :],
                                                  rstd[0:GLA_RANK, cols], ALU.mult)
                else:
                    at = {"gk": lambda: gqk[:, 1, cols], "k": lambda: kT[:, cols],
                          "g": lambda: ggT[:, int(n[2]), cols], "m": lambda: mqT[:, int(n[2]), cols],
                          "q": lambda: qT[:, int(n[1]), cols]}
                    dst = at[n if n in at else n[0]]()
                    ins = nc.vector.tensor_tensor(dst, bank, rstd[:, cols], ALU.mult)
                ins.then_inc(proj_taken, 1)
                small = delayed(i)
                if small and small[0] == "gate":
                    g = small[1]
                    c = slice(g * HALF, (g + 1) * HALF)
                    dve.wait_ge(gate_ready, g + 1)
                    nc.vector.tensor_scalar(bT[:, c], ps[:, 4 + g, :], gate_bias[:, 0:1], 0.0, ALU.add,
                                            ALU.min).then_inc(gate_min, 1)
                    dve.wait_ge(gate_log, 3 * g + 3)
                    dve.wait_ge(gate_min, g + 1)
                    nc.vector.tensor_tensor(bT[:, c], bT[:, c], ps[:, 4 + g, :], ALU.subtract).then_inc(gate_summed, 1)
                    dve.wait_ge(gate_summed, g + 1)
                    for t in range(4 * g, 4 * g + 4):
                        blk = bT[:, t * P:(t + 1) * P]
                        nc.vector.tensor_tensor_scan(blk, ones[:, :], blk, 0.0, ALU.mult, ALU.add
                                                     ).then_inc(gate_scanned, 1)
                elif small:
                    at, gain = normed_at(small[1])
                    head_norm(dve, small[1], at, gain, width(small[1]))

        prefetch = {}
        for u in range(3, NPROJ):
            prefetch.setdefault(last_group[u - 3] - 1, []).append(u)

        def mem_slot(h):
            return h % 2 * 2 + h // 2

        def stand_alone(eng, passed):
            eng.sem_inc(passed, 1)

        def blk(n):
            return bass.ds(n * P, P)

        def each_block(eng, body):
            body(0, True, False)
            with eng.Fori(1, NB - 1) as n:
                body(n, False, False)
            body(NB - 1, False, True)

        def mix_tensor(pe, n, first, last):
            band = slice(P, 2 * P) if first else slice(0, 2 * P)

            def scores(g):
                for j in range(4):
                    mm = nc.tensor.matmul(ps[:, 2 * g + j // 2, (j % 2) * 2 * P + band.start:(j % 2) * 2 * P + 2 * P],
                                          q_st[g * HEAD:(g + 1) * HEAD, j, :], k_st[g * HEAD:(g + 1) * HEAD, band],
                                          start=True, stop=True)
                mm.then_inc(scores_ready, 1)

            def mem_scores():
                wait(pe, staged_mq, 16 * n + 16)
                wait(pe, biased, 8 * n + 4)
                for h in range(4):
                    r = slice(h % 2 * HEAD, (h % 2 + 1) * HEAD)
                    mm = nc.tensor.matmul(ps[:, h % 2, (h // 2) * MEM:(h // 2 + 1) * MEM], mq_st[r, h // 2, :],
                                          mkT[r, h // 2, :], start=True, stop=True)
                mm.then_inc(scores_ready, 1)

            def levels(part):
                if part:
                    wait(pe, level_taken, LEVELS * n + 4)
                else:
                    wait(pe, pt0_ready, 3 * n)
                    wait(pe, pt1_ready, 3 * n)
                    wait(pe, state_ready, 4 * n)
                    wait(pe, o_copied, n)
                for l in range(4 * part, 4 * part + 4):
                    for h in range(4):
                        r = slice(h * GLA_DK, (h + 1) * GLA_DK)
                        mm = nc.tensor.matmul(ps[:, 4 + h, l % 4 * P:(l % 4 + 1) * P], gk_lv[r, l, :],
                                              gq_lv[r, l, :], start=True, stop=True, tile_position=(h * GLA_DK, 0))
                mm.then_inc(level_ready, 1)

            def turn(u):
                wait(pe, scaled, 12 * n + 4 * u + 4)
                for kt in range(2):
                    wait(pe, (pt0_ready, pt1_ready)[kt], 3 * n + u)
                    for j in range(4):
                        tr = nc.tensor.transpose(ps[:, 4 + kt, j * P:(j + 1) * P],
                                                 P_of[u][:, j, kt * P:(kt + 1) * P], ident[:, :])
                    tr.then_inc(turned, 1)

            def values(g):
                wait(pe, pt0_ready, 3 * n + g + 1)
                wait(pe, pt1_ready, 3 * n + g + 1)
                for kt in range(2):
                    mm = nc.tensor.matmul(ps[g * HEAD:(g + 1) * HEAD, 2, :], v_st[:, kt, g * HEAD:(g + 1) * HEAD],
                                          PT[:, kt, :], start=(kt == 0), stop=(kt == 1))
                mm.then_inc(pv_done, 1)

            wait(pe, staged_q, 16 * n + 16)
            wait(pe, staged_k, 16 * n + 16)
            wait(pe, probs_ready, 14 * n)
            scores(0)
            wait(pe, gla_factor, 4 * n + 2)
            levels(0)
            wait(pe, y_hi_ready, 2 * n)
            wait(pe, y_lo_ready, 2 * n)
            scores(1)
            mem_scores()
            levels(1)
            wait(pe, gla_factor, 4 * n + 4)
            wait(pe, level_taken, LEVELS * (n + 1))
            nc.tensor.transpose(ps[:, 6, 0:P], k_hat[:, :], ident[:, :]).then_inc(k_hat_turned, 1)
            turn(0)
            wait(pe, staged_gv, 16 * n + 16)
            wait(pe, state_ready, 4 * n)
            for h in range(4):
                o = ps[h % 2 * GLA_DV:(h % 2 + 1) * GLA_DV, 7, (h // 2) * P:(h // 2 + 1) * P]
                nc.tensor.matmul(o, gv_st[:, h * GLA_DV:(h + 1) * GLA_DV], A_T[:, h, :], start=True, stop=False)
                mm = nc.tensor.matmul(o, state[:, h * GLA_DV:(h + 1) * GLA_DV], q_hat[:, :], start=False, stop=True)
            mm.then_inc(o_ready, 1)
            wait(pe, staged_v, 16 * n + 16)
            wait(pe, biased, 8 * n + 8)
            values(0)
            turn(1)
            wait(pe, k_hat_copied, n + 1)
            nc.tensor.matmul(ps[:, 6, 0:2 * P], k_hat_tok[:, :], gv_st[:, :], start=True, stop=True
                             ).then_inc(kv_ready, 1)
            values(1)
            turn(2)
            wait(pe, pt0_ready, 3 * n + 3)
            wait(pe, pt1_ready, 3 * n + 3)
            for h in range(4):
                for kt in range(2):
                    mm = nc.tensor.matmul(ps[h % 2 * HEAD:(h % 2 + 1) * HEAD, 3, (h // 2) * P:(h // 2 + 1) * P],
                                          mv[:, kt, h * HEAD:(h + 1) * HEAD],
                                          PT[:, kt, mem_slot(h) * P:(mem_slot(h) + 1) * P],
                                          start=(kt == 0), stop=(kt == 1))
            mm.then_inc(pv_done, 1)

        def gla_exps(act, n):
            wait(act, gla_diff, 9 * n + 8)
            nc.scalar.activation(gq_lv[:], gq_lv[:], ACT.Abs).then_inc(gla_exp, 1)
            wait(act, gla_exp, 4 * n + 1)
            nc.scalar.activation(gq_lv[:], gq_lv[:], ACT.Exp, scale=-1.0 / GLA_TAU).then_inc(gla_exp, 1)
            wait(act, gla_diff, 9 * n + 9)
            nc.scalar.activation(k_hat[:], k_hat[:], ACT.Exp, scale=-1.0 / GLA_TAU).then_inc(gla_exp, 1)
            wait(act, state_ready, 4 * n)
            wait(act, gla_factor, 4 * n)
            nc.scalar.activation(decay[:], bT[:, blk(n)], ACT.Exp, scale=1.0 / GLA_TAU).then_inc(gla_exp, 1)

        def gla_diffs(dve, n):
            wait(dve, level_ready, 2 * n)
            b = bT[:, blk(n)]
            for l in range(LEVELS):
                s = P >> (l + 1)
                if s:
                    pairs = b.rearrange("p (a c) -> p a c", c=2 * s)
                    nc.vector.tensor_tensor(gq_lv[:, l, :].rearrange("p (a c) -> p a c", c=2 * s), pairs,
                                            pairs[:, :, s - 1:s].to_broadcast([P, P // (2 * s), 2 * s]),
                                            ALU.subtract).then_inc(gla_diff, 1)
                else:
                    nc.vector.tensor_tensor(gq_lv[:, l, :], b, b, ALU.subtract).then_inc(gla_diff, 1)
            wait(dve, k_hat_turned, n)
            nc.vector.tensor_tensor(k_hat[:], b, bT[:, bass.ds(n * P + P - 1, 1)].to_broadcast([P, P]),
                                    ALU.subtract).then_inc(gla_diff, 1)

        def gla_factors(dve, n):
            q, k = gqk[:, 0, blk(n)], gqk[:, 1, blk(n)]
            wait(dve, gla_exp, 4 * n + 2)
            nc.vector.tensor_tensor(gk_lv[:], gq_lv[:], k.unsqueeze(1).to_broadcast([P, LEVELS, P]),
                                    ALU.mult).then_inc(gla_factor, 1)
            nc.vector.tensor_tensor(gq_lv[:], gq_lv[:], q.unsqueeze(1).to_broadcast([P, LEVELS, P]),
                                    ALU.mult).then_inc(gla_factor, 1)
            wait(dve, gla_exp, 4 * n + 4)
            nc.vector.tensor_tensor(k_hat[:], k_hat[:], k, ALU.mult).then_inc(gla_factor, 1)
            wait(dve, o_ready, n)
            nc.vector.tensor_tensor(q_hat[:], decay[:], q, ALU.mult).then_inc(gla_factor, 1)

        def mix_scalar(act, n, first, last):
            band = slice(P, 2 * P) if first else slice(0, 2 * P)

            def exps(g):
                wait(act, shift_ready, 5 * n + 2 * g + 1)
                for j in range(4):
                    p = P_of[g][:, j, band]
                    nc.scalar.activation(p, p, ACT.Exp, bias=shift[:, 4 * g + j:4 * g + j + 1],
                                         accum_out=row_sum[:, 4 * g + j:4 * g + j + 1]).then_inc(probs_ready, 1)
                wait(act, shift_ready, 5 * n + 2 * g + 2)
                nc.scalar.activation(sink_exp[:, 4 * g:4 * g + 4], sink_shift[:, 4 * g:4 * g + 4], ACT.Exp
                                     ).then_inc(probs_ready, 1)

            def pt_copy(u):
                wait(act, turned, 6 * n + 2 * u + 1)
                wait(act, pv_done, 3 * n + u)
                nc.scalar.activation(PT[:, 0, :], ps[:, 4, :], ACT.Copy).then_inc(pt0_ready, 1)

            exps(0)
            exps(1)
            wait(act, shift_ready, 5 * n + 5)
            wait(act, turned, 6 * n)
            for h in range(4):
                nc.scalar.activation(P_of[2][:, h, :], ps[:, h // 2, (h % 2) * MEM:(h % 2 + 1) * MEM], ACT.Exp,
                                     bias=shift[:, 8 + h:9 + h], accum_out=row_sum[:, 8 + h:9 + h]
                                     ).then_inc(probs_ready, 1)
            wait(act, k_hat_turned, n + 1)
            wait(act, kv_ready, n)
            nc.scalar.activation(k_hat_tok[:], ps[:, 6, 0:P], ACT.Copy).then_inc(k_hat_copied, 1)
            pt_copy(0)
            wait(act, o_ready, n + 1)
            nc.scalar.activation(gqk[:, :, blk(n)], ps[:, 7, 0:2 * P].rearrange("p (j t) -> p j t", j=2), ACT.Copy
                                 ).then_inc(o_copied, 1)
            pt_copy(1)
            wait(act, pv_done, 3 * n + 2)
            nc.scalar.activation(hT_hi[:, 0:4, blk(n)], ps[:, 2, :].rearrange("p (j t) -> p j t", j=4), ACT.Copy
                                 ).then_inc(y_hi_ready, 1)
            pt_copy(2)
            if not last:
                gla_exps(act, n + 1)
            wait(act, pv_done, 3 * n + 3)
            nc.scalar.activation(hT_hi[:, 6:8, blk(n)], ps[:, 3, 0:2 * P].rearrange("p (j t) -> p j t", j=2), ACT.Copy
                                 ).then_inc(y_hi_ready, 1)

        def mix_vector(dve, n, first, last):
            band = slice(P, 2 * P) if first else slice(0, 2 * P)

            def bias_max(g):
                wait(dve, scores_ready, 3 * n + g + 1)
                wait(dve, turned, 6 * n - 4 + 2 * g)
                stand_alone(dve, dve_passed)
                for j in range(4):
                    h = 4 * g + j
                    s = ps[:, 2 * g + j // 2, (j % 2) * 2 * P + band.start:(j % 2) * 2 * P + 2 * P]
                    nc.vector.tensor_tensor_reduce(out=P_of[g][:, j, band], in0=s, in1=bias[:, h, band], scale=1.0,
                                                   scalar=sinks[:, h:h + 1], op0=ALU.add, op1=ALU.max,
                                                   accum_out=row_max[:, h:h + 1]).then_inc(biased, 1)
                wait(dve, biased, 8 * n + 4 * g + 4)
                hs = slice(4 * g, 4 * g + 4)
                nc.vector.tensor_scalar(shift[:, hs], row_max[:, hs], -1.0, None, ALU.mult).then_inc(shift_ready, 1)
                nc.vector.tensor_tensor(sink_shift[:, hs], sinks[:, hs], row_max[:, hs], ALU.subtract
                                        ).then_inc(shift_ready, 1)

            def take(l):
                wait(dve, level_ready, 2 * n + l // 4 + 1)
                if l:
                    wait(dve, level_taken, LEVELS * n + l)
                stand_alone(dve, dve_passed)
                nc.vector.copy_predicated(A_T[:], masks[:, l, :].unsqueeze(1).to_broadcast([P, 4, P]),
                                          ps[:, 4:8, l % 4 * P:(l % 4 + 1) * P]
                                          ).then_inc(level_taken, 1)

            def denominators(g):
                hs = slice(4 * g, 4 * g + 4)
                wait(dve, probs_ready, 14 * n + 5 * g + 5)
                nc.vector.tensor_tensor(row_sum[:, hs], row_sum[:, hs], sink_exp[:, hs], ALU.add).then_inc(denom, 1)
                wait(dve, denom, 5 * n + 2 * g + 1)
                wait(dve, scaled, 12 * n - 8 + 4 * g)
                nc.vector.reciprocal(row_inv[:, hs], row_sum[:, hs]).then_inc(denom, 1)

            def pt_copy(u):
                wait(dve, turned, 6 * n + 2 * u + 2)
                wait(dve, pv_done, 3 * n + u)
                nc.vector.tensor_copy(PT[:, 1, :], ps[:, 5, :]).then_inc(pt1_ready, 1)

            def y_lo(tiles, bank, c):
                wait(dve, pv_done, 3 * n + (2, 3)[c])
                wait(dve, y_hi_ready, 2 * n + c + 1)
                w = tiles.stop - tiles.start
                nc.vector.tensor_tensor(hT_lo[:, tiles, blk(n)], ps[:, bank, 0:w * P].rearrange("p (j t) -> p j t", j=w),
                                        hT_hi[:, tiles, blk(n)].bitcast(F32), ALU.subtract).then_inc(y_lo_ready, 1)

            bias_max(0)
            bias_max(1)
            wait(dve, o_ready, n)
            for l in range(4):
                take(l)
                if l == 1:
                    denominators(0)
            wait(dve, scores_ready, 3 * n + 3)
            nc.vector.tensor_reduce(shift[:, 8:12], ps[:, 0:2, :].rearrange("p a (b k) -> p (a b) k", k=MEM), AX.X,
                                    ALU.max, negate=True).then_inc(shift_ready, 1)
            denominators(1)
            for l in range(4, LEVELS):
                take(l)
            wait(dve, probs_ready, 14 * n + 14)
            wait(dve, scaled, 12 * n)
            nc.vector.reciprocal(row_inv[:, 8:12], row_sum[:, 8:12]).then_inc(denom, 1)
            pt_copy(0)
            if not last:
                gla_diffs(dve, n + 1)
            pt_copy(1)
            wait(dve, kv_ready, n + 1)
            wait(dve, o_ready, n + 1)
            for h in range(4):
                r = slice(h * GLA_DK, (h + 1) * GLA_DK)
                at = state[r, h * GLA_DV:(h + 1) * GLA_DV]
                nc.vector.scalar_tensor_tensor(out=at, in0=at, scalar=decay[r, P - 1:P],
                                               in1=ps[r, 6, h * GLA_DV:(h + 1) * GLA_DV], op0=ALU.mult,
                                               op1=ALU.add).then_inc(state_ready, 1)
            y_lo(slice(0, 4), 2, 0)
            pt_copy(2)
            if not last:
                gla_factors(dve, n + 1)
            y_lo(slice(6, 8), 3, 1)

        def stage_qk(sp, n, first):
            sp.dma_start(q_st[:], qT[:, :, blk(n)]).then_inc(staged_q, 16)
            if first:
                sp.dma_start(k_st[:, P:2 * P], kT[:, 0:P]).then_inc(staged_k, 16)
            else:
                sp.dma_start(k_st[:], kT[:, bass.ds(n * P - P, 2 * P)]).then_inc(staged_k, 16)
            sp.dma_start(mq_st[:], mqT[:, :, blk(n)]).then_inc(staged_mq, 16)

        def stage_v(sp, n, first):
            if first:
                sp.dma_start(v_st[:, 1, :], vg[:, 0, 0:P]).then_inc(staged_v, 16)
            else:
                sp.dma_start(v_st[:], vg[:, bass.ds(n - 1, 2), 0:P]).then_inc(staged_v, 16)
            sp.dma_start(gv_st[:].unsqueeze(1), vg[:, bass.ds(n, 1), P:3 * P]).then_inc(staged_gv, 16)

        def mix_sync(sp, n, first, last):
            if not last:
                wait(sp, scores_ready, 3 * n + 3)
                stage_qk(sp, n + 1, False)
                wait(sp, pv_done, 3 * n + 2)
                wait(sp, kv_ready, n + 1)
                stage_v(sp, n + 1, False)

        def mix_pool(pool, n, first, last):
            def scale(u):
                wait(pool, denom, 5 * n + (2, 4, 5)[u])
                stand_alone(pool, pool_passed)
                for j in range(4):
                    p = P_of[u][:, j, :]
                    nc.gpsimd.tensor_scalar(p, p, row_inv[:, 4 * u + j:4 * u + j + 1], 1.0, ALU.mult, ALU.mult
                                            ).then_inc(scaled, 1)
            scale(0)
            scale(1)
            scale(2)

        def mix_start_pool(pool):
            pool.wait_ge(proj_ready, NG)
            pool.wait_ge(proj_taken, NG)
            pool.wait_ge(head_normed, len(normed))
            for t, v in ((A_T, 0.0), (state, 0.0), (Pg0, 0.0), (Pg1, 0.0), (v_st, 0.0)):
                nc.gpsimd.memset(t[:], v).then_inc(mix_set, 1)

        def gla_item(c):
            j, h = c % 2, c // 2
            cols = slice(h * HALF, (h + 1) * HALF)
            return j, cols, gqk[:, j, cols]

        def gla_hi(act, c):
            j, cols, at = gla_item(c)
            act.wait_ge(gla_gated, c + 1)
            nc.scalar.activation(hT_hi[:, 4 + j, cols], at, ACT.Copy).then_inc(gla_hi_ready, 1)

        def gla_norm(dve, c):
            j, cols, at = gla_item(c)
            head_norm(dve, GLA_OUT + c, at, head_gains[:, 4:5], HALF)
            dve.wait_ge(head_normed, GLA_OUT + c + 1)
            nc.vector.tensor_tensor(at, at, ggT[:, j, cols], ALU.mult).then_inc(gla_gated, 1)

        def gla_lo(dve, c):
            j, cols, at = gla_item(c)
            dve.wait_ge(gla_hi_ready, c + 1)
            nc.vector.tensor_tensor(hT_lo[:, 4 + j, cols], at, hT_hi[:, 4 + j, cols].bitcast(F32),
                                    ALU.subtract).then_inc(gla_lo_ready, 1)

        def out_tensor(pe):
            def product(g, tiles):
                m, h = g // 2, g % 2
                s = (NPROJ + m) % 3
                cols = slice(h * HALF, (h + 1) * HALF)
                pe.wait_ge(p_ready[s], (NPROJ + m) // 3 + 1)
                for k in tiles:
                    if k == 4:
                        pe.wait_ge(gla_lo_ready, 2 * h + 2)
                    kc = slice(k * P, (k + 1) * P)
                    mm = split_product(nc, ps[:, g % 4, :], p_hi[:, s, kc], p_lo[:, s, kc],
                                       hT_hi[:, k, cols], hT_lo[:, k, cols], k == 0, k == 5)
                if k == 5:
                    mm.then_inc(proj_ready, 1)

            attention, linear = (0, 1, 2, 3, 6, 7), (4, 5)
            head_sum(pe, GLA_OUT, HALF)
            head_sum(pe, GLA_OUT + 1, HALF)
            pe.wait_ge(y_lo_ready, 2 * NB)
            for g in range(4):
                product(g, attention)
                if g in (1, 2):
                    head_sum(pe, GLA_OUT + g + 1, HALF)
            for g in (0, 2, 1, 3):
                product(g, linear)
            for g in range(4, 2 * KT):
                pe.wait_ge(out_added, out_count(g - 4))
                product(g, attention + linear)

        def out_scalar(act):
            square = lambda c: head_square(act, GLA_OUT + c, gla_item(c)[2], HALF)
            root = lambda c: head_root(act, GLA_OUT + c, HALF)
            square(0)
            square(1)
            unit_scalar(act, NPROJ)
            root(0)
            root(1)
            unit_scalar(act, NPROJ + 1)
            square(2)
            gla_hi(act, 0)
            square(3)
            unit_scalar(act, NPROJ + 2)
            gla_hi(act, 1)
            root(2)
            gla_hi(act, 2)
            root(3)
            gla_hi(act, 3)
            for m in range(KT):
                if m + 3 < KT:
                    unit_scalar(act, NPROJ + m + 3)
                elif m + 3 < KT + 2:
                    weight_hi(act, 1, ("ga", "ua")[m + 3 - KT], 0)
                for h in range(NHALF):
                    norm_square(act, 2, m, h)

        def out_vector(dve):
            unit_vector(dve, NPROJ)
            gla_norm(dve, 0)
            unit_vector(dve, NPROJ + 1)
            gla_lo(dve, 0)
            gla_norm(dve, 1)
            unit_vector(dve, NPROJ + 2)
            gla_lo(dve, 1)
            for c in (2, 3):
                gla_norm(dve, c)
                gla_lo(dve, c)
            for i, g in enumerate(OUT_ORDER):
                m, h = g // 2, g % 2
                dve.wait_ge(proj_ready, NG + i + 1)
                nc.vector.tensor_tensor(part(xT, m, h), ps[:, g % 4, :], part(xT, m, h), ALU.add
                                        ).then_inc(out_added, 1)
                done = [u for u in range(NPROJ + 3, NPROJ + KT) if last_group[u - 3] == NG + i + 1]
                for u in done:
                    unit_vector(dve, u)
                if i in (11, 13):
                    weight_lo(dve, 1, ("ga", "ua")[(i - 11) // 2], 0)

        def x_sync(sp, pieces):
            for c in pieces:
                h, ms = c // 2, slice(4 * (c % 2), 4 * (c % 2) + 4)
                sp.dma_start(xT[:, ms, h * HALF:(h + 1) * HALF],
                             x_in.rearrange("(m p) t -> p m t", p=P)[:, ms, h * HALF:(h + 1) * HALF]
                             ).then_inc(x_landed[c], 16)

        def y_sync(sp):
            for g in range(2 * KT):
                m, h = g // NHALF, g % NHALF
                sp.wait_ge(down_added, Base(NFFN).down - 2 * KT + g + 1)
                sp.dma_start(out[m * P:(m + 1) * P, h * HALF:(h + 1) * HALF], part(xT, m, h)).then_inc(y_stored, 16)
            sp.wait_ge(y_stored, 16 * 2 * KT)

        block = ctx.enter_context(nc.Block())

        @block.sync
        def _(sp):
            x_sync(sp, (0, 1))
            load_slot(sp, 0, "ga", 0)
            load_slot(sp, 0, "ua", 0)
            x_sync(sp, (2, 3))
            load_slot(sp, 0, "gb", 0)
            load_slot(sp, 0, "ub", 0)
            for dst, src in consts:
                sp.dma_start(dst, src).then_inc(const_landed, 16)
            ffn_sync(sp, 0)
            for name in ("ga", "ua"):
                sp.wait_ge(w_ready[SLOT[name]], PAIRS)
            sp.dma_start(memT[:], mem_in.rearrange("(k p) t -> p k t", p=P)).then_inc(mem_landed, 16)
            for name in ("gb", "ub"):
                sp.wait_ge(w_ready[SLOT[name]], PAIRS)
            for u in range(NPROJ):
                unit_sync(sp, u)
            sp.wait_ge(proj_ready, NG)
            sp.wait_ge(bias_stored, 16)
            skewed = bias_dram.rearrange("(h x) -> h x", h=SWA_HEADS)[:, P - 1:P - 1 + P * (ROW - 1)]
            sp.dma_start(bias[:], skewed.rearrange("h (p u) -> p h u", u=ROW - 1)[:, :, 0:2 * P]).then_inc(bias_landed, 16)
            sp.wait_ge(head_normed, len(normed))
            sp.wait_ge(mix_set, 5)
            stage_qk(sp, 0, True)
            stage_v(sp, 0, True)
            each_block(sp, lambda n, first, last: mix_sync(sp, n, first, last))
            sp.wait_ge(biased, 8 * NB)
            sp.wait_ge(turned, 6 * (NB - 1) + 2)
            for u in range(NPROJ, NPROJ + 3):
                unit_sync(sp, u)
            sp.wait_ge(y_lo_ready, 2 * NB)
            load_slot(sp, 1, "ga", 0)
            load_slot(sp, 1, "ua", 0)
            for u in range(NPROJ + 3, NPROJ + KT):
                unit_sync(sp, u)
            for i in range(3):
                sp.wait_ge(p_ready[i], (NPROJ + KT) // 3)
            load_slot(sp, 1, "gb", 0)
            load_slot(sp, 1, "ub", 0)
            sp.wait_ge(proj_ready, NG + 2 * KT)
            ffn_sync(sp, 1)
            y_sync(sp)

        @block.gpsimd
        def _(pool):
            nc.gpsimd.memset(eps[:], EPS).then_inc(const_set, 1)
            nc.gpsimd.memset(ones[:], 1.0).then_inc(const_set, 1)
            nc.gpsimd.memset(rel_bias[:], MASKED).then_inc(const_set, 1)
            pool.wait_ge(bias_row_ready, 1)
            pool.dma_start(bias_dram.rearrange("(h p u) -> h p u", h=SWA_HEADS, p=P),
                           bias_row[:].unsqueeze(1).to_broadcast([SWA_HEADS, P, ROW])).then_inc(bias_stored, 16)
            norm_pool(pool, 0)
            for u in range(3):
                unit_vector(pool, u, nc.gpsimd)
            norm_pool(pool, 1)
            mix_start_pool(pool)
            each_block(pool, lambda n, first, last: mix_pool(pool, n, first, last))
            norm_pool(pool, 2)

        @block.scalar
        def _(act):
            act.dma_start(gains[:], gains_in).then_inc(gains_landed, 16)
            act.wait_ge(const_set, 3)
            act.dma_start(rel_bias[0:N_BUCKETS, :], rel_bias_in).then_inc(rel_bias_landed, 16)
            act.dma_start(bucket_of[:], bucket_of_in).then_inc(rel_bias_landed, 16)
            act.wait_ge(gains_landed, 16)
            for ms in (range(0, KT // 2), range(KT // 2, KT)):
                for m in ms:
                    norm_hi(act, 0, m, 0)
                if ms.start:
                    weight_hi(act, 0, "ga", 0)
                    weight_hi(act, 0, "ua", 0)
                for m in ms:
                    norm_square(act, 0, m, 0)
            for m in range(KT):
                norm_hi(act, 0, m, 1)
            for m in range(KT):
                norm_square(act, 0, m, 1)
            act.wait_ge(const_landed, 16 * NCONST)
            act.wait_ge(masks_ready, 1)
            act.wait_ge(bias_stored, 16)
            ffn_scalar(act, 0)
            for m, h in norm_steps(1):
                norm_hi(act, 1, m, h)
                norm_square(act, 1, m, h)
            proj_scalar(act)
            act.wait_ge(gate_scanned, NB)
            act.wait_ge(mix_set, 5)
            gla_exps(act, 0)
            each_block(act, lambda n, first, last: mix_scalar(act, n, first, last))
            out_scalar(act)
            for m, h in norm_steps(2):
                norm_hi(act, 2, m, h)
            ffn_scalar(act, 1)

        @block.vector
        def _(dve):
            dve.wait_ge(bias_row_summed, 1)
            nc.vector.tensor_copy(bias_row[:], ps[0:SWA_HEADS, BANK_DOWN, 0:ROW]).then_inc(bias_row_ready, 1)
            dve.wait_ge(gains_landed, 16)
            for m in range(KT):
                norm_vector(dve, 0, m, 0)
            weight_lo(dve, 0, "ga", 0)
            weight_lo(dve, 0, "ua", 0)
            for m in range(KT):
                norm_vector(dve, 0, m, 1)
            dve.wait_ge(const_landed, 16 * NCONST)
            nc.vector.tensor_copy(masks[:], masks_f[:]).then_inc(masks_ready, 1)
            for c in (0, 2):
                nc.vector.tensor_scalar(head_gains[:, c:c + 1], head_gains[:, c:c + 1], float(HEAD) ** -0.5, None,
                                        ALU.mult).then_inc(gains_scaled, 1)
            dve.wait_ge(gains_scaled, 2)
            sumsq0_vector(dve)
            ffn_vector(dve, 0)
            for g in range(2 * KT):
                down_add(dve, 0, PAIRS - 1, g)
                if g >= 2:
                    norm_vector(dve, 1, *norm_steps(1)[g - 2])
            for g in (2 * KT - 2, 2 * KT - 1):
                norm_vector(dve, 1, *norm_steps(1)[g])
            proj_vector(dve)
            dve.wait_ge(gate_scanned, NB)
            dve.wait_ge(mix_set, 5)
            gla_diffs(dve, 0)
            gla_factors(dve, 0)
            dve.wait_ge(bias_landed, 16)
            each_block(dve, lambda n, first, last: mix_vector(dve, n, first, last))
            out_vector(dve)
            for m, h in norm_steps(2):
                norm_vector(dve, 2, m, h)
            ffn_vector(dve, 1)
            for g in range(2 * KT):
                down_add(dve, Base(1).down, PAIRS - 1, g)

        @block.tensor
        def _(pe):
            pe.wait_ge(const_set, 3)
            pe.wait_ge(rel_bias_landed, 32)
            nc.tensor.matmul(ps[0:SWA_HEADS, BANK_DOWN, 0:ROW], rel_bias[:, :], bucket_of[:, :], start=True, stop=True
                             ).then_inc(bias_row_summed, 1)
            ffn_tensor(pe, 0)
            pe.wait_ge(const_landed, 16 * NCONST)
            proj_tensor(pe)
            each_block(pe, lambda n, first, last: mix_tensor(pe, n, first, last))
            out_tensor(pe)
            ffn_tensor(pe, 1)


def _columns(w):
    return np.ascontiguousarray(w.reshape(KT, P, -1, P).transpose(2, 1, 0, 3)).reshape(-1, D)


def _bucket_of():
    exact = N_BUCKETS // 2
    hot = np.zeros((N_BUCKETS + 1, ROW), np.float32)
    for u in range(ROW):
        dist = 2 * P - 1 - u
        if not 0 <= dist < P:
            hot[N_BUCKETS, u] = 1
            continue
        large = exact + int(np.float32(np.log(np.float32(max(dist, 1) / exact))) / np.float32(np.log(MAX_DISTANCE / exact))
                            * (N_BUCKETS - exact))
        hot[dist if dist < exact else min(large, N_BUCKETS - 1), u] = 1
    return hot


def _masks():
    i, j = np.arange(P)[None, :], np.arange(P)[:, None]
    out = np.zeros((P, LEVELS, P), np.float32)
    for l in range(LEVELS):
        s = P >> (l + 1)
        out[:, l, :] = (i // (2 * s) == j // (2 * s)) & (i % (2 * s) >= s) & (j % (2 * s) < s) if s else i == j
    return out


def kernel(**inputs):
    import concourse.bacc as _bacc
    from concourse.bass_utils import run_bass_kernel_spmd as _run

    a = {n: np.asarray(v) for n, v in inputs.items()}
    w_in = a["w_in"][0]
    at = {"q": 0, "k": 512, "v": 640, "gq": 768, "gk": 896, "gv": 1024, "gg": 1280, "glr": 1536, "mq": 1552}

    def columns_of(n):
        if n[0] == "q":
            j = int(n[1])
            return np.r_[HEAD * j:HEAD * (j + 1), 4 * HEAD + HEAD * j:4 * HEAD + HEAD * (j + 1)]
        base = n.rstrip("0123")
        start = at[base] + P * int(n[len(base):] or 0)
        return np.arange(start, start + P)

    picked = np.concatenate([columns_of(n) for n in PROJ if n[:2] not in ("mk", "mv")])
    w_out = a["w_out"][0]
    swa_rows = w_out[:SWA_HEADS * HEAD].reshape(2, 4, HEAD, D).transpose(1, 0, 2, 3).reshape(-1, D)
    per_tile = lambda g: g.reshape(-1, KT, P).transpose(2, 0, 1)
    twice = lambda g: np.concatenate([g, g])
    arrays = {
        "x": a["x"][0].T,
        "mem": a["mem"][0].T,
        "w_gate1": _columns(a["ffn1_w_gate"][0]), "w_up1": _columns(a["ffn1_w_up"][0]), "w_down1": a["ffn1_w_down"][0],
        "w_proj": _columns(w_in[:, picked]),
        "w_mem": _columns(a["w_mem_kv"][0]),
        "w_out": _columns(np.concatenate([swa_rows, w_out[SWA_HEADS * HEAD:]])),
        "w_gate2": _columns(a["ffn2_w_gate"][0]), "w_up2": _columns(a["ffn2_w_up"][0]), "w_down2": a["ffn2_w_down"][0],
        "gains": per_tile(np.stack([a["ffn1_norm"][0], a["mix_norm"][0], a["ffn2_norm"][0]])),
        "mem_gain": per_tile(a["mem_norm"][0])[:, 0],
        "head_gains": np.stack([twice(a[n][0]) for n in ("swa_q_norm", "swa_k_norm", "mem_q_norm", "mem_k_norm",
                                                         "gla_out_norm")], axis=1),
        "sinks": a["swa_sinks"][0],
        "rel_bias": a["rel_bias"],
        "bucket_of": _bucket_of(),
        "gate_up": a["gla_w_gate_up"][0],
        "gate_bias": a["gla_b_gate"][0][:, None],
        "masks": _masks(),
        "ident": np.eye(P, dtype=np.float32),
        "head_ones": np.kron(np.eye(2, dtype=np.float32), np.ones((HEAD, HEAD), np.float32)),
    }
    nc = _bacc.Bacc("TRN2", target_bir_lowering=False, num_devices=1)
    feeds, args = {}, []
    for name, v in arrays.items():
        v = np.ascontiguousarray(v)
        feeds[f"in_{name}"] = v
        args.append(nc.dram_tensor(f"in_{name}", v.shape, mybir.dt.from_np(v.dtype), kind="ExternalInput").ap())
    args.append(nc.dram_tensor("out_y", (D, T), F32, kind="ExternalOutput").ap())
    build(nc, *args)
    r = _run(nc, [feeds], core_ids=[0])
    return np.ascontiguousarray(r.results[0]["out_y"].T)[None]
```

```python
from contextlib import ExitStack

import numpy as np

import concourse.bass as bass
from concourse import mybir

F32 = mybir.dt.float32
F32R = mybir.dt.float32r
U8 = mybir.dt.uint8
ALU = mybir.AluOpType
ACT = mybir.ActivationFunctionType
AX = mybir.AxisListType

P = 128
D = 1024
T = 1024
KT = D // P
HALF = 512
NHALF = T // HALF
F = 2816
PAIRS = F // (2 * P)
EPS = 1e-6
MEM = 256
NB = T // P
HEAD = 64
SWA_HEADS = 8
N_BUCKETS = 32
MAX_DISTANCE = 128
ROW = 3 * P
GLA_DK, GLA_DV, GLA_RANK, GLA_TAU = 32, 64, 16, 16.0
LEVELS = 8
MASKED = -1e30
PROJ = ["v", "gv0", "gv1", "gk", "gq", "glr", "mv0", "mv1", "mk0", "mk1", "k",
        "q0", "q1", "q2", "q3", "mq0", "mq1", "gg0", "gg1"]


def split_product(nc, out, w_hi, w_lo, x_hi, x_lo, first, last):
    nc.tensor.matmul(out, w_hi, x_hi, start=first, stop=False)
    nc.tensor.matmul(out, w_hi, x_lo, start=False, stop=False)
    return nc.tensor.matmul(out, w_lo, x_hi, start=False, stop=last)


def build(nc, x_in, mem_in, w_gate1, w_up1, w_down1, w_proj, w_mem, w_out, w_gate2, w_up2, w_down2, gains_in,
          mem_gain_in, head_gains_in, sinks_in, rel_bias_in, bucket_of_in, gate_up_in, gate_bias_in,
          masks_in, ident_in, head_ones_in, out):
    ctx = ExitStack()
    with ctx:
        sb = lambda name, shape, dt=F32: ctx.enter_context(nc.sbuf_tensor(name, shape, dt))
        sem = lambda name: ctx.enter_context(nc.semaphore(name))

        def phase(*tensors):
            with ExitStack() as stack:
                return [stack.enter_context(nc.sbuf_tensor(name, shape, dt)) for name, shape, dt in tensors]

        xT = sb("xT", [P, KT, T])
        pads = lambda i: phase((f"pad_skip{i}", [P, 4, T], F32), (f"gq_pad{i}", [P, 4, 4, P], F32))[1]
        gq_pad = [pads(0)]
        hT_hi = sb("hT_hi", [P, KT, T], F32R)
        gq_pad.append(pads(1))
        hT_lo = sb("hT_lo", [P, KT, T], F32R)
        glu = sb("glu", [P, NHALF, HALF])
        rstd = sb("rstd", [P, T])
        ident = sb("ident", [P, P])
        ones = sb("ones", [P, P])
        head_ones = sb("head_ones", [P, P])
        eps = sb("eps", [P, 1])
        gains = sb("gains", [P, 3, KT])
        mem_gain = sb("mem_gain", [P, KT])
        head_gains = sb("head_gains", [P, 5])
        sinks = sb("sinks", [P, SWA_HEADS])
        gate_bias = sb("gate_bias", [P, 1])
        gate_up_w = sb("gate_up_w", [GLA_RANK, P])
        masks = sb("masks", [P, LEVELS, P], U8)
        rstd_tok = sb("rstd_tok", [P, KT + 2])

        bias_dram = nc.dram_tensor("bias_dram", (SWA_HEADS * P * ROW,), F32, kind="Internal").ap()

        (raw_a, hi_a, lo_a, act_hi, act_lo, hi_d, lo_d, hi_b, lo_b, raw_d, raw_b) = phase(
            ("raw_a", [P, 2, D], F32), ("hi_a", [P, 2, D], F32R), ("lo_a", [P, 2, D], F32R),
            ("act_hi", [P, 3, T], F32R), ("act_lo", [P, 3, T], F32R),
            ("hi_d", [P, 2, D], F32R), ("lo_d", [P, 2, D], F32R), ("hi_b", [P, 2, D], F32R),
            ("lo_b", [P, 2, D], F32R), ("raw_d", [P, 2, D], F32), ("raw_b", [P, 2, D], F32))
        w_raw = [t[:, i, :] for t in (raw_a, raw_d, raw_b) for i in range(2)]
        w_hi = [t[:, i, :] for t in (hi_a, hi_d, hi_b) for i in range(2)]
        w_lo = [t[:, i, :] for t in (lo_a, lo_d, lo_b) for i in range(2)]

        _, rel_bias, bucket_of, bias_row, masks_f = phase(
            ("start_skip", [P, 6, D], F32), ("rel_bias", [N_BUCKETS + 1, SWA_HEADS], F32),
            ("bucket_of", [N_BUCKETS + 1, ROW], F32), ("bias_row", [SWA_HEADS, ROW], F32),
            ("masks_f", [P, LEVELS, P], F32))

        memT, memT_hi, memT_lo = phase(
            ("memT", [P, KT, MEM], F32), ("memT_hi", [P, KT, MEM], F32R), ("memT_lo", [P, KT, MEM], F32R))
        with ExitStack() as mix:
            msb = lambda name, shape, dt=F32: mix.enter_context(nc.sbuf_tensor(name, shape, dt))
            qT = msb("qT", [P, 4, T])
            mqT = msb("mqT", [P, 2, T])
            kT = msb("kT", [P, T])
            mkT = msb("mkT", [P, 2, MEM])
            mv = msb("mv", [P, 2, 2 * P])
            vg = msb("vg", [P, NB, 3 * P])
            gqk = msb("gqk", [P, 2, T])
            bT = msb("bT", [P, T])
            ggT = msb("ggT", [P, 2, T])
            p_hi, p_lo, p_raw = phase(
                ("p_hi", [P, 3, D], F32R), ("p_lo", [P, 3, D], F32R), ("p_raw", [P, 3, D], F32))
            (Pg1, q_st, mq_pad, k_pad, v_st, gv_st, A_T, spare, g_lv, state, k_hat, k_hat_tok, q_hat,
             decay, row_max, shift, sink_shift, sink_exp, row_sum, row_inv) = phase(
                ("Pg1", [P, 4, 2 * P], F32), ("q_st", [P, 4, P], F32),
                ("mq_pad", [P, 4, P], F32), ("k_pad", [P, 2, 2 * P], F32),
                ("v_st", [P, 2, P], F32), ("gv_st", [P, 2 * P], F32),
                ("A_T", [P, 4, P], F32), ("spare", [P, 4, P], F32),
                ("g_lv", [P, LEVELS, P], F32), ("state", [P, 4 * GLA_DV], F32),
                ("k_hat", [P, P], F32), ("k_hat_tok", [P, P], F32), ("q_hat", [P, P], F32),
                ("decay", [P, P], F32),
                ("row_max", [P, 8], F32), ("shift", [P, 12], F32), ("sink_shift", [P, 8], F32),
                ("sink_exp", [P, 8], F32), ("row_sum", [P, 12], F32), ("row_inv", [P, 12], F32))
            _, bias, Pg0 = phase(
                ("mix_skip", [P, 6, D], F32),
                ("bias", [P, SWA_HEADS, 2 * P], F32),
                ("Pg0", [P, 4, 2 * P], F32))
        P_of = [Pg0[:], Pg1[:], rstd[:].rearrange("p (h k) -> p h k", h=4)]
        PT = glu

        ps = ctx.enter_context(nc.psum_tensor("ps", [P, 8, HALF], F32))
        BANK_GATE, BANK_UP, BANK_DOWN, BANK_NORM = 0, 2, 4, 6

        NPROJ = len(PROJ)
        MEM_UNITS = ["mk0", "mk1", "mv0", "mv1"]
        X_UNITS = [n for n in PROJ if n not in MEM_UNITS]
        gains_scaled, masks_ready = sem("gains_scaled"), sem("masks_ready")
        dve_passed, pool_passed = sem("dve_passed"), sem("pool_passed")
        mem_landed, bias_stored, bias_landed = sem("mem_landed"), sem("bias_stored"), sem("bias_landed")
        gains_landed, rel_bias_landed = sem("gains_landed"), sem("rel_bias_landed")
        bias_row_summed, bias_row_ready = sem("bias_row_summed"), sem("bias_row_ready")
        p_landed = [sem(f"p_landed{i}") for i in range(3)]
        p_hi_ready = [sem(f"p_hi_ready{i}") for i in range(3)]
        p_ready = [sem(f"p_ready{i}") for i in range(3)]
        (tok_summed, proj_ready, proj_taken, mem_hi_ready, mem_lo_ready, mem_split, mem_summed, mem_rooted, mem_normed, gate_ready,
         gate_min, gate_log, gate_summed, gate_scanned, head_squared, head_summed, head_rooted, head_normed,
         out_gate_ready, out_added, gla_gated, gla_hi_ready, gla_lo_ready, mix_set, head_inverted) = [sem(n) for n in (
            "tok_summed proj_ready proj_taken mem_hi_ready mem_lo_ready mem_split mem_summed mem_rooted mem_normed gate_ready "
            "gate_min gate_log gate_summed gate_scanned head_squared head_summed head_rooted head_normed "
            "out_gate_ready out_added gla_gated gla_hi_ready gla_lo_ready mix_set head_inverted").split()]
        (staged_q, staged_k, staged_mq, staged_v, staged_gv, scores_ready, biased, shift_ready, probs_ready, denom, scaled,
         turned, pt_ready, pv_done, y_hi_ready, y_lo_ready, level_ready, level_taken, gla_diff, gla_exp,
         gla_factor, pads_ready, k_hat_turned, k_hat_copied, kv_ready, state_ready, o_ready, o_copied) = [sem(n) for n in (
            "staged_q staged_k staged_mq staged_v staged_gv scores_ready biased shift_ready probs_ready denom scaled "
            "turned pt_ready pv_done y_hi_ready y_lo_ready level_ready level_taken gla_diff gla_exp "
            "gla_factor pads_ready k_hat_turned k_hat_copied kv_ready state_ready o_ready o_copied").split()]
        const_landed = sem("const_landed")
        const_set, pads_set = sem("const_set"), sem("pads_set")
        x_landed = [sem(f"x_landed{i}") for i in range(4)]
        consts = [(mem_gain[:], mem_gain_in), (head_gains[:], head_gains_in),
                  (sinks[:], sinks_in.rearrange("(a n) -> a n", a=1).to_broadcast([P, SWA_HEADS])),
                  (gate_bias[:], gate_bias_in), (gate_up_w[:], gate_up_in),
                  (ident[:], ident_in), (masks_f[:], masks_in), (head_ones[:], head_ones_in)]
        NCONST = len(consts)
        h_hi_ready = sem("h_hi_ready")
        h_ready = sem("h_ready")
        squared = sem("squared")
        sumsq_added = sem("sumsq_added")
        sumsq0_added = sem("sumsq0_added")
        norm_summed = sem("norm_summed")
        norm_rooted = sem("norm_rooted")
        rstd_ready = sem("rstd_ready")
        w_landed = [sem(f"w_landed{i}") for i in range(6)]
        w_hi_ready = [sem(f"w_hi_ready{i}") for i in range(6)]
        w_ready = [sem(f"w_ready{i}") for i in range(6)]
        gate_up_ready = sem("gate_up_ready")
        gate_scaled = sem("gate_scaled")
        gate_silu = sem("gate_silu")
        up_scaled = sem("up_scaled")
        glu_ready = sem("glu_ready")
        act_hi_ready = sem("act_hi_ready")
        act_ready = sem("act_ready")
        down_ready = sem("down_ready")
        down_added = sem("down_added")
        y_stored = sem("y_stored")

        SLOT = dict(ga=0, ua=1, da=2, db=3, gb=4, ub=5)

        def wait(eng, s, value):
            if isinstance(value, int) and value <= 0:
                return
            eng.wait_ge(s, value)

        ffn_weights = [(w_gate1, w_up1, w_down1), (w_gate2, w_up2, w_down2)]
        NFFN = 2

        class Base:
            def __init__(self, f):
                self.use = f * PAIRS
                self.gu = f * PAIRS * 4
                self.down = f * PAIRS * 2 * KT

        def load_slot(sp, f, name, k):
            b, s = Base(f), SLOT[name]
            wait(sp, w_ready[s], k + b.use)
            wg, wu, wd = ffn_weights[f]
            tile = 2 * k + (name[1] == "b")
            w = dict(g=wg, u=wu, d=wd)[name[0]]
            sp.dma_start(w_raw[s], w[bass.ds(tile * P, P), :]).then_inc(w_landed[s], 16)

        def each_pair(eng, body):
            body(0, 0, True, False)
            with eng.Fori(1, PAIRS - 2, 2) as i:
                body(i, 1, False, False)
                body(i + 1, 0, False, False)
            body(PAIRS - 2, 1, False, False)
            body(PAIRS - 1, 0, False, True)

        def ffn_sync(sp, f):
            def body(i, par, first, last):
                if not first:
                    for name in ("ga", "ua"):
                        load_slot(sp, f, name, i)
                    for name in ("da", "db"):
                        load_slot(sp, f, name, i - 1)
                    for name in ("gb", "ub"):
                        load_slot(sp, f, name, i)
            each_pair(sp, body)
            for name in ("da", "db"):
                load_slot(sp, f, name, PAIRS - 1)

        def freed(eng, f, name, k):
            b = Base(f)
            if name[0] == "d":
                wait(eng, down_ready, b.down + 2 * KT * k)
            else:
                wait(eng, gate_up_ready, b.gu + 4 * k - (2 if name[1] == "a" else 0))

        def weight_hi(act, f, name, k):
            b, s = Base(f), SLOT[name]
            wait(act, w_landed[s], 16 * (k + b.use) + 16)
            freed(act, f, name, k)
            nc.scalar.activation(w_hi[s], w_raw[s], ACT.Copy).then_inc(w_hi_ready[s], 1)

        def weight_lo(dve, f, name, k):
            b, s = Base(f), SLOT[name]
            wait(dve, w_hi_ready[s], k + b.use + 1)
            nc.vector.tensor_tensor(w_lo[s], w_raw[s], w_hi[s].bitcast(F32),
                                    ALU.subtract).then_inc(w_ready[s], 1)

        def ffn_scalar(act, f):
            b = Base(f)

            def act_slot(par, t):
                return 2 if t else par

            def glu_steps(i, par, t):
                for h in range(NHALF):
                    q = b.gu + 4 * i + 2 * t + h
                    wait(act, gate_scaled, q + 1)
                    nc.scalar.activation(ps[:, BANK_GATE + h, :], ps[:, BANK_GATE + h, :],
                                         ACT.Silu).then_inc(gate_silu, 1)
                    wait(act, glu_ready, q + 1)
                    nc.scalar.activation(act_hi[:, act_slot(par, t), h * HALF:(h + 1) * HALF], glu[:, h, :],
                                         ACT.Copy).then_inc(act_hi_ready, 1)

            def body(i, par, first, last):
                weight_hi(act, f, "gb", i)
                weight_hi(act, f, "ub", i)
                if first:
                    norm_root(act, 2 * f)
                glu_steps(i, par, 0)
                if not last:
                    weight_hi(act, f, "ga", i + 1)
                    weight_hi(act, f, "ua", i + 1)
                weight_hi(act, f, "da", i)
                weight_hi(act, f, "db", i)
                glu_steps(i, par, 1)
                if f == 0 and last:
                    for u in range(3):
                        unit_scalar(act, u)
            each_pair(act, body)

        def ffn_vector(dve, f):
            b = Base(f)

            def glu_steps(i, par, t):
                for h in range(NHALF):
                    q = b.gu + 4 * i + 2 * t + h
                    cols = slice(h * HALF, (h + 1) * HALF)
                    slot = 2 if t else par
                    wait(dve, gate_up_ready, q + 1)
                    nc.vector.tensor_tensor(ps[:, BANK_GATE + h, :], ps[:, BANK_GATE + h, :], rstd[:, cols],
                                            ALU.mult).then_inc(gate_scaled, 1)
                    nc.vector.tensor_tensor(glu[:, h, :], ps[:, BANK_UP + h, :], rstd[:, cols],
                                            ALU.mult).then_inc(up_scaled, 1)
                    wait(dve, up_scaled, q + 1)
                    wait(dve, gate_silu, q + 1)
                    nc.vector.tensor_tensor(glu[:, h, :], ps[:, BANK_GATE + h, :], glu[:, h, :],
                                            ALU.mult).then_inc(glu_ready, 1)
                    wait(dve, act_hi_ready, q + 1)
                    nc.vector.tensor_tensor(act_lo[:, slot, cols], glu[:, h, :],
                                            act_hi[:, slot, cols].bitcast(F32),
                                            ALU.subtract).then_inc(act_ready, 1)

            def body(i, par, first, last):
                weight_lo(dve, f, "gb", i)
                weight_lo(dve, f, "ub", i)
                if first:
                    norm_recip(dve, 2 * f)
                glu_steps(i, par, 0)
                for g in range(2 * KT):
                    if not first:
                        down_add(dve, b.down, i - 1, g)
                    if g == 6 and not last:
                        weight_lo(dve, f, "ga", i + 1)
                    if g == 11 and not last:
                        weight_lo(dve, f, "ua", i + 1)
                weight_lo(dve, f, "da", i)
                weight_lo(dve, f, "db", i)
                glu_steps(i, par, 1)
            each_pair(dve, body)

        def down_add(dve, base, j, g):
            m, h = g // NHALF, g % NHALF
            r = base + 2 * KT * j + g
            dst = xT[:, m, h * HALF:(h + 1) * HALF]
            wait(dve, down_ready, r + 1)
            nc.vector.scalar_tensor_tensor(out=dst, in0=ps[:, BANK_DOWN + g % 4, :], scalar=0.5, in1=dst,
                                           op0=ALU.mult, op1=ALU.add).then_inc(down_added, 1)

        def ffn_tensor(pe, f):
            b = Base(f)

            def gate_up(i, t):
                g, u = (("ga", "ua"), ("gb", "ub"))[t]
                for h in range(NHALF):
                    q = b.gu + 4 * i + 2 * t + h
                    wait(pe, glu_ready, q - 1)
                    for name, bank in ((g, BANK_GATE + h), (u, BANK_UP + h)):
                        s = SLOT[name]
                        if h == 0:
                            wait(pe, w_ready[s], b.use + i + 1)
                        for k in range(KT):
                            if isinstance(i, int) and i == 0 and t == 0 and name[0] == "g":
                                pe.wait_ge(h_ready, split_count(2 * f, k, h))
                            cols, rows = slice(k * P, (k + 1) * P), slice(h * HALF, (h + 1) * HALF)
                            mm = split_product(nc, ps[:, bank, :], w_hi[s][:, cols], w_lo[s][:, cols],
                                               hT_hi[:, k, rows], hT_lo[:, k, rows], k == 0, k == KT - 1)
                    mm.then_inc(gate_up_ready, 1)
                    if isinstance(i, int) and i == 0 and t == 0 and h == 0:
                        norm_sum(pe, 2 * f)

            def down_product(j, par, g, t):
                m, h = g // NHALF, g % NHALF
                s, slot = SLOT[("da", "db")[t]], (par, 2)[t]
                cols, rows = slice(m * P, (m + 1) * P), slice(h * HALF, (h + 1) * HALF)
                mm = split_product(nc, ps[:, BANK_DOWN + g % 4, :], w_hi[s][:, cols], w_lo[s][:, cols],
                                   act_hi[:, slot, rows], act_lo[:, slot, rows], t == 0, t == 1)
                if t == 1:
                    mm.then_inc(down_ready, 1)

            def down(j, par, last=False):
                done = 0
                if last:
                    wait(pe, act_ready, b.gu + 4 * j + 2)
                    wait(pe, down_added, b.down + 2 * KT * j)
                    wait(pe, w_ready[SLOT["da"]], b.use + j + 1)
                    done = 4
                    for g in range(done):
                        down_product(j, par, g, 0)
                wait(pe, act_ready, b.gu + 4 * j + 4)
                for s in (SLOT["da"], SLOT["db"]):
                    wait(pe, w_ready[s], b.use + j + 1)
                for g in range(2 * KT):
                    if g >= 4:
                        pe.wait_ge(down_added, b.down + 2 * KT * j + g - 3)
                    if g >= done:
                        down_product(j, par, g, 0)
                    down_product(j, par, g, 1)

            def body(i, par, first, last):
                gate_up(i, 0)
                if not first:
                    down(i - 1, 1 - par)
                gate_up(i, 1)
            each_pair(pe, body)
            down(PAIRS - 1, 0, last=True)

        def norm_steps(n):
            if n != 1:
                return [(m, h) for h in range(NHALF) for m in range(KT)]
            return [(m, h) for m in range(KT) for h in range(NHALF)]

        def split_count(n, m, h):
            return 2 * KT * n + norm_steps(n).index((m, h)) + 1

        def norm_sum(pe, n):
            if n == 0:
                pe.wait_ge(sumsq0_added, KT)
            for h in range(NHALF):
                pe.wait_ge(sumsq_added, sumsq_count(n))
                nc.tensor.matmul(ps[:, BANK_NORM + h, :], ones[:, :], rstd[:, h * HALF:(h + 1) * HALF],
                                 start=True, stop=True).then_inc(norm_summed, 1)

        def norm_root(act, n):
            for h in range(NHALF):
                bank = ps[:, BANK_NORM + h, :]
                act.wait_ge(norm_summed, NHALF * n + h + 1)
                nc.scalar.activation(bank, bank, ACT.Sqrt, bias=eps[:, 0:1], scale=1.0 / D).then_inc(norm_rooted, 1)

        def norm_recip(dve, n):
            for h in range(NHALF):
                dve.wait_ge(norm_rooted, NHALF * n + h + 1)
                nc.vector.reciprocal(rstd[:, h * HALF:(h + 1) * HALF],
                                     ps[:, BANK_NORM + h, :]).then_inc(rstd_ready, 1)
            dve.wait_ge(rstd_ready, NHALF * (n + 1))

        def part(tensor, m, h):
            return tensor[:, m, h * HALF:(h + 1) * HALF]

        def norm_hi(act, n, m, h):
            if n == 0:
                act.wait_ge(x_landed[2 * h + m // 4], 16)
            elif n == 1:
                act.wait_ge(down_added, Base(1).down - 2 * KT + 2 * m + h + 1)
            else:
                act.wait_ge(out_added, max(out_count(2 * m), out_count(2 * m + 1)))
                act.wait_ge(proj_ready, NG + 2 * KT)
            nc.scalar.activation(part(hT_hi, m, h), part(xT, m, h), ACT.Copy,
                                 scale=gains[:, n, m:m + 1]).then_inc(h_hi_ready, 1)

        def square_steps(n):
            return [(m, h) for m in range(KT) for h in range(NHALF)] if n else norm_steps(0)

        def square_count(n, m, h):
            return 2 * KT * n + square_steps(n).index((m, h)) + 1

        def sumsq_count(n):
            return KT + 2 * KT * n

        def norm_square(act, n, m, h):
            c = square_count(n, m, h)
            if n == 2:
                act.wait_ge(out_added, max(out_count(2 * m), out_count(2 * m + 1)))
            if n == 0 and c - 2 > KT:
                act.wait_ge(sumsq0_added, c - 2 - KT)
            else:
                wait(act, sumsq_added, c - 2 - (KT if n else 0))
                if n == 1 and m == 0:
                    act.wait_ge(sumsq0_added, KT)
            nc.scalar.activation(glu[:, c % 2, :], part(xT, m, h), ACT.Square).then_inc(squared, 1)

        def norm_vector(dve, n, m, h):
            dve.wait_ge(h_hi_ready, split_count(n, m, h))
            nc.vector.scalar_tensor_tensor(out=part(hT_lo, m, h), in0=part(xT, m, h), scalar=gains[:, n, m:m + 1],
                                           in1=part(hT_hi, m, h).bitcast(F32), op0=ALU.mult,
                                           op1=ALU.subtract).then_inc(h_ready, 1)

        def sumsq0_vector(dve):
            acc = rstd[:, HALF:T]
            for m in range(KT):
                dve.wait_ge(squared, KT + m + 1)
                sq = glu[:, (KT + m + 1) % 2, :]
                if m == 0:
                    nc.vector.tensor_copy(acc, sq).then_inc(sumsq0_added, 1)
                else:
                    dve.wait_ge(sumsq0_added, m)
                    nc.vector.tensor_tensor(acc, acc, sq, ALU.add).then_inc(sumsq0_added, 1)

        def norm_pool(pool, n):
            for m, h in square_steps(n):
                if n == 0 and h == 1:
                    continue
                c = square_count(n, m, h)
                acc = rstd[:, h * HALF:(h + 1) * HALF]
                pool.wait_ge(squared, c)
                if m == 0:
                    nc.gpsimd.tensor_scalar(acc, glu[:, c % 2, :], 1.0, 1.0, ALU.mult, ALU.mult).then_inc(sumsq_added, 1)
                else:
                    pool.wait_ge(sumsq_added, c - 1 - (KT if n else 0))
                    nc.gpsimd.tensor_tensor(acc, acc, glu[:, c % 2, :], ALU.add).then_inc(sumsq_added, 1)

        def unit_sync(sp, u):
            wait(sp, p_ready[u % 3], u // 3)
            n = PROJ[u] if u < NPROJ else None
            if n is None:
                src = w_out[(u - NPROJ) * P:(u - NPROJ + 1) * P, :]
            elif n in MEM_UNITS:
                i = MEM_UNITS.index(n)
                src = w_mem[i * P:(i + 1) * P, :]
            else:
                i = X_UNITS.index(n)
                src = w_proj[i * P:(i + 1) * P, :]
            sp.dma_start(p_raw[:, u % 3, :], src).then_inc(p_landed[u % 3], 16)

        def unit_free(u):
            return last_group[u - 3] if u >= 3 else 0

        def unit_scalar(act, u):
            s = u % 3
            act.wait_ge(p_landed[s], 16 * (u // 3 + 1))
            if u < 3:
                act.wait_ge(gate_up_ready, Base(1).gu)
            if u == NPROJ:
                act.wait_ge(scores_ready, 3 * NB)
            if NPROJ < u < NPROJ + 3:
                act.wait_ge(level_ready, LEVELS * NB)
                act.wait_ge(o_ready, NB)
            wait(act, proj_ready, unit_free(u))
            nc.scalar.activation(p_hi[:, s, :], p_raw[:, s, :], ACT.Copy).then_inc(p_hi_ready[s], 1)

        def unit_vector(dve, u, engine=None):
            s = u % 3
            dve.wait_ge(p_hi_ready[s], u // 3 + 1)
            (engine or nc.vector).tensor_tensor(p_lo[:, s, :], p_raw[:, s, :], p_hi[:, s, :].bitcast(F32),
                                    ALU.subtract).then_inc(p_ready[s], 1)

        groups = [("v", t) for t in range(NB)]
        for n in PROJ[3:]:
            if n == "mv0":
                groups += [("mv", 0), ("mv", 1)]
            elif n == "mv1":
                pass
            elif n in ("mk0", "mk1"):
                groups += [(n, 0)]
            else:
                groups += [(n, h) for h in range(NHALF)]
        gi = {g: i for i, g in enumerate(groups)}
        NG = len(groups)

        def units_of(name):
            return {"v": [0, 1, 2], "mv": [6, 7]}.get(name) or [PROJ.index(name)]

        OUT_ORDER = [0, 2, 1, 3] + list(range(4, 2 * KT))

        def out_count(g):
            return OUT_ORDER.index(g) + 1

        last_group = {}
        for i, (n, _) in enumerate(groups):
            for u in units_of(n):
                last_group[u] = i + 1
        for m in range(KT):
            last_group[NPROJ + m] = NG + max(out_count(2 * m), out_count(2 * m + 1))

        normed = [("mk0", 0), ("mk1", 0)] + [(n, h) for n in ("k", "q0", "q1", "q2", "q3", "mq0", "mq1")
                                             for h in range(NHALF)]

        def normed_at(i):
            n, h = normed[i]
            cols = slice(h * HALF, (h + 1) * HALF)
            if n[:2] == "mk":
                return mkT[:, int(n[2]), :], head_gains[:, 3:4]
            if n[:2] == "mq":
                return mqT[:, int(n[2]), cols], head_gains[:, 2:3]
            if n[0] == "q":
                return qT[:, int(n[1]), cols], head_gains[:, 0:1]
            return kT[:, cols], head_gains[:, 1:2]

        def width(i):
            return MEM if normed[i][0][:2] == "mk" else HALF

        GLA_OUT = len(normed)

        def head_buffer(i, w):
            flat = lambda t: t.rearrange("p a q -> p (a q)")
            return {GLA_OUT: flat(spare[:]), GLA_OUT + 1: flat(g_lv[:, 0:4, :])}.get(i, glu[:, i % 2, 0:w])

        def head_bank(i, w):
            return ps[:, {GLA_OUT: 0, GLA_OUT + 1: 3}.get(i, 4 + i % 2), 0:w]

        def head_square(act, i, src, w):
            wait(act, head_summed, i - 1)
            nc.scalar.activation(head_buffer(i, w), src, ACT.Square).then_inc(head_squared, 1)

        def head_sum(pe, i, w):
            pe.wait_ge(head_squared, i + 1)
            wait(pe, head_normed, i - 1)
            nc.tensor.matmul(head_bank(i, w), head_ones[:, :], head_buffer(i, w), start=True,
                             stop=True).then_inc(head_summed, 1)

        def head_root(act, i, w):
            act.wait_ge(head_summed, i + 1)
            nc.scalar.activation(head_bank(i, w), head_bank(i, w), ACT.Sqrt, bias=eps[:, 0:1],
                                 scale=1.0 / HEAD).then_inc(head_rooted, 1)

        def head_norm(dve, i, at, gain, w):
            dve.wait_ge(head_rooted, i + 1)
            bank = head_bank(i, w)
            nc.vector.reciprocal(bank, bank).then_inc(head_inverted, 1)
            dve.wait_ge(head_inverted, i + 1)
            nc.vector.scalar_tensor_tensor(out=at, in0=at, scalar=gain, in1=bank, op0=ALU.mult, op1=ALU.mult
                                           ).then_inc(head_normed, 1)

        DELAY = 2

        def delayed(i):
            if i - DELAY < 0:
                return None
            n, h = groups[i - DELAY]
            if n == "glr":
                return ("gate", h)
            if (n, h) in normed:
                return ("norm", normed.index((n, h)))
            return None

        def proj_tensor(pe):
            for i, (n, h) in enumerate(groups):
                us = units_of(n)
                for u in us:
                    pe.wait_ge(p_ready[u % 3], u // 3 + 1)
                wait(pe, proj_taken, i - 3)
                if n in ("mv", "mk0", "mk1"):
                    pe.wait_ge(mem_split, 2)
                for k in range(KT):
                    kc = slice(k * P, (k + 1) * P)
                    if n == "v":
                        pe.wait_ge(h_ready, split_count(1, k, h // 4))
                        tok = slice(h * P, (h + 1) * P)
                        mm = split_product(nc, ps[:, i % 4, 0:3 * P], hT_hi[:, k, tok], hT_lo[:, k, tok],
                                           p_hi[:, 0:3, kc], p_lo[:, 0:3, kc], k == 0, k == KT - 1)
                    elif n == "mv":
                        tok = slice(h * P, (h + 1) * P)
                        mm = split_product(nc, ps[:, i % 4, 0:2 * P], memT_hi[:, k, tok], memT_lo[:, k, tok],
                                           p_hi[:, 0:2, kc], p_lo[:, 0:2, kc], k == 0, k == KT - 1)
                    elif n in ("mk0", "mk1"):
                        s = us[0] % 3
                        mm = split_product(nc, ps[:, i % 4, 0:MEM], p_hi[:, s, kc], p_lo[:, s, kc],
                                           memT_hi[:, k, :], memT_lo[:, k, :], k == 0, k == KT - 1)
                    else:
                        s = us[0] % 3
                        cols = slice(h * HALF, (h + 1) * HALF)
                        mm = split_product(nc, ps[:, i % 4, :], p_hi[:, s, kc], p_lo[:, s, kc],
                                           hT_hi[:, k, cols], hT_lo[:, k, cols], k == 0, k == KT - 1)
                mm.then_inc(proj_ready, 1)
                if i == 1:
                    pe.wait_ge(sumsq_added, sumsq_count(1))
                    pe.wait_ge(down_added, Base(1).down)
                    for t in range(NB):
                        mm = nc.tensor.matmul(ps[:, 5, t:t + 1], rstd[:, t * P:(t + 1) * P], ones[:, 0:1],
                                              start=True, stop=True)
                    mm.then_inc(tok_summed, 1)
                    norm_sum(pe, 1)
                if i == 5:
                    pe.wait_ge(mem_split, 3)
                    pe.wait_ge(mem_normed, 1)
                    for t in range(2):
                        for k in range(KT):
                            nc.tensor.matmul(ps[:, 5, KT + t:KT + t + 1], memT[:, k, t * P:(t + 1) * P],
                                             ones[:, 0:1], start=(k == 0), stop=(k == KT - 1))
                    for k in range(KT):
                        mm = nc.tensor.matmul(ps[:, 4, 0:MEM], ones[:, :], memT[:, k, :], start=(k == 0),
                                              stop=(k == KT - 1))
                    mm.then_inc(mem_summed, 1)
                small = delayed(i)
                if small and small[0] == "gate":
                    g = small[1]
                    pe.wait_ge(proj_taken, gi[("glr", g)] + 1)
                    pe.wait_ge(mem_normed, 3)
                    nc.tensor.matmul(ps[:, 4 + g, :], gate_up_w[:, :], glu[0:GLA_RANK, g, :], start=True,
                                     stop=True).then_inc(gate_ready, 1)
                elif small:
                    j = small[1]
                    if j < 2:
                        pe.wait_ge(gate_summed, 2)
                    head_sum(pe, j, width(j))

        def mem_split_scalar(act):
            act.wait_ge(mem_landed, 16)
            for k in range(KT):
                nc.scalar.activation(memT_hi[:, k, :], memT[:, k, :], ACT.Copy,
                                     scale=mem_gain[:, k:k + 1]).then_inc(mem_hi_ready, 1)

        def mem_split_vector(dve):
            for k in range(KT):
                dve.wait_ge(mem_hi_ready, k + 1)
                nc.vector.scalar_tensor_tensor(out=memT_lo[:, k, :], in0=memT[:, k, :], scalar=mem_gain[:, k:k + 1],
                                               in1=memT_hi[:, k, :].bitcast(F32), op0=ALU.mult,
                                               op1=ALU.subtract).then_inc(mem_lo_ready, 1)

        def proj_scalar(act):
            mem_split_scalar(act)
            act.wait_ge(tok_summed, 1)
            nc.scalar.activation(ps[:, 5, 0:KT], ps[:, 5, 0:KT], ACT.Sqrt, bias=eps[:, 0:1],
                                 scale=1.0 / D).then_inc(mem_rooted, 1)
            norm_root(act, 1)
            act.wait_ge(mem_lo_ready, KT)
            nc.scalar.activation(memT[:], memT[:], ACT.Square).then_inc(mem_split, 3)
            act.wait_ge(mem_summed, 1)
            nc.scalar.activation(ps[:, 5, KT:KT + 2], ps[:, 5, KT:KT + 2], ACT.Sqrt, bias=eps[:, 0:1],
                                 scale=1.0 / D).then_inc(mem_rooted, 1)
            nc.scalar.activation(ps[:, 4, 0:MEM], ps[:, 4, 0:MEM], ACT.Sqrt, bias=eps[:, 0:1],
                                 scale=1.0 / D).then_inc(mem_rooted, 1)
            for i, (n, h) in enumerate(groups):
                for u in prefetch.get(i, []):
                    unit_scalar(act, u)
                if (n, h) in normed:
                    j = normed.index((n, h))
                    act.wait_ge(proj_taken, i + 1)
                    if j == 0:
                        act.wait_ge(gate_ready, 2)
                    head_square(act, j, normed_at(j)[0], width(j))
                small = delayed(i)
                if small and small[0] == "gate":
                    g = small[1]
                    bank = ps[:, 4 + g, :]
                    act.wait_ge(gate_min, g + 1)
                    nc.scalar.activation(bank, bank, ACT.Abs, bias=gate_bias[:, 0:1]).then_inc(gate_log, 1)
                    act.wait_ge(gate_log, 3 * g + 1)
                    nc.scalar.activation(bank, bank, ACT.Exp, scale=-1.0).then_inc(gate_log, 1)
                    act.wait_ge(gate_log, 3 * g + 2)
                    nc.scalar.activation(bank, bank, ACT.Ln, bias=ones[:, 0:1]).then_inc(gate_log, 1)
                elif small:
                    head_root(act, small[1], width(small[1]))

        def proj_vector(dve):
            mem_split_vector(dve)
            dve.wait_ge(mem_rooted, 1)
            nc.vector.reciprocal(rstd_tok[:, 0:KT], ps[:, 5, 0:KT]).then_inc(mem_normed, 1)
            dve.wait_ge(mem_normed, 1)
            for i, (n, h) in enumerate(groups):
                if i == 3:
                    norm_recip(dve, 1)
                if i == NB - 1:
                    dve.wait_ge(mem_rooted, 3)
                    nc.vector.reciprocal(rstd_tok[:, KT:KT + 2], ps[:, 5, KT:KT + 2]).then_inc(mem_normed, 1)
                    nc.vector.reciprocal(memT[:, 0, :], ps[:, 4, 0:MEM]).then_inc(mem_normed, 1)
                    dve.wait_ge(mem_normed, 3)
                for u in prefetch.get(i, []):
                    unit_vector(dve, u)
                if i == NG - 1:
                    gla_diffs(dve, 0)
                dve.wait_ge(proj_ready, i + 1)
                bank = ps[:, i % 4, :]
                cols = slice(h * HALF, (h + 1) * HALF)
                if n == "v":
                    ins = nc.vector.tensor_scalar(vg[:, h, :], bank[:, 0:3 * P], rstd_tok[:, h:h + 1], None, ALU.mult)
                elif n == "mv":
                    ins = nc.vector.tensor_scalar(mv[:, h, :], bank[:, 0:2 * P], rstd_tok[:, KT + h:KT + h + 1], None,
                                                  ALU.mult)
                elif n in ("mk0", "mk1"):
                    ins = nc.vector.tensor_tensor(mkT[:, int(n[2]), :], bank[:, 0:MEM], memT[:, 0, :], ALU.mult)
                elif n == "gq":
                    ins = nc.vector.scalar_tensor_tensor(out=gqk[:, 0, cols], in0=bank, scalar=float(GLA_DK) ** -0.5,
                                                         in1=rstd[:, cols], op0=ALU.mult, op1=ALU.mult)
                elif n == "glr":
                    ins = nc.vector.tensor_tensor(glu[0:GLA_RANK, h, :], bank[0:GLA_RANK, :],
                                                  rstd[0:GLA_RANK, cols], ALU.mult)
                else:
                    at = {"gk": lambda: gqk[:, 1, cols], "k": lambda: kT[:, cols],
                          "g": lambda: ggT[:, int(n[2]), cols], "m": lambda: mqT[:, int(n[2]), cols],
                          "q": lambda: qT[:, int(n[1]), cols]}
                    dst = at[n if n in at else n[0]]()
                    ins = nc.vector.tensor_tensor(dst, bank, rstd[:, cols], ALU.mult)
                ins.then_inc(proj_taken, 1)
                small = delayed(i)
                if small and small[0] == "gate":
                    g = small[1]
                    c = slice(g * HALF, (g + 1) * HALF)
                    dve.wait_ge(gate_ready, g + 1)
                    nc.vector.tensor_scalar(bT[:, c], ps[:, 4 + g, :], gate_bias[:, 0:1], 0.0, ALU.add,
                                            ALU.min).then_inc(gate_min, 1)
                    dve.wait_ge(gate_log, 3 * g + 3)
                    dve.wait_ge(gate_min, g + 1)
                    nc.vector.tensor_tensor(bT[:, c], bT[:, c], ps[:, 4 + g, :], ALU.subtract).then_inc(gate_summed, 1)
                    dve.wait_ge(gate_summed, g + 1)
                    for t in range(4 * g, 4 * g + 4):
                        blk = bT[:, t * P:(t + 1) * P]
                        nc.vector.tensor_tensor_scan(blk, ones[:, :], blk, 0.0, ALU.mult, ALU.add
                                                     ).then_inc(gate_scanned, 1)
                elif small:
                    at, gain = normed_at(small[1])
                    head_norm(dve, small[1], at, gain, width(small[1]))

        prefetch = {}
        for u in range(3, NPROJ):
            prefetch.setdefault(last_group[u - 3] - 1, []).append(u)

        def stand_alone(eng, passed):
            eng.sem_inc(passed, 1)

        def blk(n):
            return bass.ds(n * P, P)

        def each_block(eng, body):
            body(0, True, False)
            with eng.Fori(1, NB - 1) as n:
                body(n, False, False)
            body(NB - 1, False, True)

        SCORE_BANK = (2, 0, 2)
        TURN_BANK = (0, 4, 4)

        def mix_tensor(pe, n, first, last):
            band = slice(P, 2 * P) if first else slice(0, 2 * P)

            def scores(g):
                for j in range(4):
                    mm = nc.tensor.matmul(ps[:, SCORE_BANK[g] + j // 2, (j % 2) * 2 * P + band.start:(j % 2) * 2 * P + 2 * P],
                                          q_st[:, j, :], k_pad[:, g, band], start=True, stop=True)
                mm.then_inc(scores_ready, 1)

            def mem_scores():
                wait(pe, staged_mq, 32 * n + 32)
                wait(pe, biased, 8 * n + 4)
                for h in range(4):
                    mm = nc.tensor.matmul(ps[:, SCORE_BANK[2] + h // 2, (h % 2) * MEM:(h % 2 + 1) * MEM], mq_pad[:, h, :],
                                          mkT[:, h // 2, :], start=True, stop=True)
                mm.then_inc(scores_ready, 1)

            def levels():
                wait(pe, gla_factor, LF * n + DVE_PADS)
                wait(pe, pads_ready, 3 * n + 3)
                wait(pe, pt_ready, 3 * n)
                wait(pe, state_ready, 4 * n)
                wait(pe, o_copied, n)
                for l in range(LEVELS):
                    if l >= 4:
                        wait(pe, level_taken, LEVELS * n + l - 3)
                    nc.tensor.matmul(ps[:, 4 + l % 4, :], g_lv[:, l, :], gq_pad[l // 4][:, l % 4, :, :],
                                     start=True, stop=True).then_inc(level_ready, 1)

            def turn(u):
                wait(pe, scaled, 12 * n + 4 * u + 4)
                for kt in range(2):
                    for j in range(4):
                        tr = nc.tensor.transpose(ps[:, TURN_BANK[u] + kt, j * P:(j + 1) * P],
                                                 P_of[u][:, j, kt * P:(kt + 1) * P], ident[:, :])
                tr.then_inc(turned, 1)

            def values(g):
                wait(pe, pt_ready, 3 * n + g + 1)
                for kt in range(2):
                    mm = nc.tensor.matmul(ps[g * HEAD:(g + 1) * HEAD, 2, :], v_st[:, kt, g * HEAD:(g + 1) * HEAD],
                                          PT[:, kt, :], start=(kt == 0), stop=(kt == 1))
                mm.then_inc(pv_done, 1)

            wait(pe, staged_q, 16 * n + 16)
            wait(pe, staged_k, 32 * n + 32)
            if not first:
                wait(pe, y_hi_ready, 2 * n - 1)
                wait(pe, y_lo_ready, 2 * n - 1)
            scores(0)
            wait(pe, y_hi_ready, 2 * n)
            wait(pe, y_lo_ready, 2 * n)
            scores(1)
            mem_scores()
            levels()
            wait(pe, biased, 8 * n + 8)
            turn(0)
            wait(pe, gla_factor, LF * n + LF - 1)
            wait(pe, level_taken, LEVELS * n + 7)
            nc.tensor.transpose(ps[:, 6, 0:P], k_hat[:, :], ident[:, :]).then_inc(k_hat_turned, 1)
            turn(1)
            wait(pe, staged_v, 16 * n + 16)
            wait(pe, probs_ready, 14 * n + 14)
            values(0)
            wait(pe, staged_gv, 16 * n + 16)
            wait(pe, k_hat_copied, n + 1)
            nc.tensor.matmul(ps[:, 6, 0:2 * P], k_hat_tok[:, :], gv_st[:, :], start=True, stop=True
                             ).then_inc(kv_ready, 1)
            if last:
                head_sum(pe, GLA_OUT, HALF)
                head_sum(pe, GLA_OUT + 1, HALF)
            values(1)
            turn(2)
            wait(pe, level_taken, LEVELS * n + 8)
            wait(pe, gla_factor, LF * n + LF)
            for h in range(4):
                o = ps[h % 2 * GLA_DV:(h % 2 + 1) * GLA_DV, 7, (h // 2) * P:(h // 2 + 1) * P]
                nc.tensor.matmul(o, gv_st[:, h * GLA_DV:(h + 1) * GLA_DV], A_T[:, h, :], start=True, stop=False)
                mm = nc.tensor.matmul(o, state[:, h * GLA_DV:(h + 1) * GLA_DV], q_hat[:, :], start=False, stop=True)
            mm.then_inc(o_ready, 1)
            wait(pe, pt_ready, 3 * n + 3)
            for h in range(4):
                for kt in range(2):
                    mm = nc.tensor.matmul(ps[h % 2 * HEAD:(h % 2 + 1) * HEAD, 1, (h // 2) * P:(h // 2 + 1) * P],
                                          mv[:, kt, h * HEAD:(h + 1) * HEAD], PT[:, kt, h * P:(h + 1) * P],
                                          start=(kt == 0), stop=(kt == 1))
            mm.then_inc(pv_done, 1)

        def gla_exps(act, n):
            wait(act, gla_diff, 10 * n + 10)
            nc.scalar.activation(g_lv[:], g_lv[:], ACT.Exp, scale=1.0 / GLA_TAU).then_inc(gla_exp, 1)

        def gla_edge_exps(act, n):
            wait(act, gla_diff, 10 * n + 9)
            nc.scalar.activation(k_hat[:], k_hat[:], ACT.Exp, scale=-1.0 / GLA_TAU).then_inc(gla_exp, 1)
            wait(act, state_ready, 4 * n)
            wait(act, gla_factor, LF * n)
            nc.scalar.activation(decay[:], bT[:, blk(n)], ACT.Exp, scale=1.0 / GLA_TAU).then_inc(gla_exp, 1)

        def gla_diffs(dve, n):
            wait(dve, level_ready, LEVELS * n)
            b = bT[:, blk(n)]
            for l in range(LEVELS):
                s = P >> (l + 1)
                if s:
                    pairs = b.rearrange("p (a c) -> p a c", c=2 * s)
                    nc.vector.tensor_tensor(g_lv[:, l, :].rearrange("p (a c) -> p a c", c=2 * s), pairs,
                                            pairs[:, :, s - 1:s].to_broadcast([P, P // (2 * s), 2 * s]),
                                            ALU.subtract).then_inc(gla_diff, 1)
                else:
                    nc.vector.tensor_tensor(g_lv[:, l, :], b, b, ALU.subtract).then_inc(gla_diff, 1)
            wait(dve, k_hat_turned, n)
            nc.vector.tensor_tensor(k_hat[:], b, bT[:, bass.ds(n * P + P - 1, 1)].to_broadcast([P, P]),
                                    ALU.subtract).then_inc(gla_diff, 1)
            wait(dve, gla_diff, 10 * n + 9)
            nc.vector.scalar_tensor_tensor(out=g_lv[:], in0=g_lv[:], scalar=-1.0, in1=g_lv[:], op0=ALU.mult,
                                           op1=ALU.min).then_inc(gla_diff, 1)

        DVE_PADS = 6
        LF = DVE_PADS + 2

        def pad_levels(engine, n, part, h, done):
            r = slice(h * GLA_DK, (h + 1) * GLA_DK)
            engine.tensor_tensor(gq_pad[part][r, :, h, :], g_lv[r, 4 * part:4 * part + 4, :],
                                 gqk[r, 0, blk(n)].unsqueeze(1).to_broadcast([GLA_DK, 4, P]), ALU.mult).then_inc(done, 1)

        def gla_pads(dve, n, part):
            wait(dve, gla_exp, 3 * n + 1)
            for h in (range(2) if part else range(4)):
                pad_levels(nc.vector, n, part, h, gla_factor)

        def gla_edge_factors(dve, n):
            q, k = gqk[:, 0, blk(n)], gqk[:, 1, blk(n)]
            wait(dve, gla_exp, 3 * n + 3)
            nc.vector.tensor_tensor(k_hat[:], k_hat[:], k, ALU.mult).then_inc(gla_factor, 1)
            wait(dve, o_ready, n)
            nc.vector.tensor_tensor(q_hat[:], decay[:], q, ALU.mult).then_inc(gla_factor, 1)

        def gla_pads_pool(pool, n):
            wait(pool, gla_exp, 3 * n + 1)
            wait(pool, level_ready, LEVELS * n)
            for h in (2, 3):
                pad_levels(nc.gpsimd, n, 1, h, pads_ready)
            wait(pool, pads_ready, 3 * n + 2)
            wait(pool, gla_factor, LF * n + DVE_PADS)
            nc.gpsimd.tensor_tensor(g_lv[:], g_lv[:], gqk[:, 1, blk(n)].unsqueeze(1).to_broadcast([P, LEVELS, P]),
                                    ALU.mult).then_inc(pads_ready, 1)

        def mix_scalar(act, n, first, last):
            band = slice(P, 2 * P) if first else slice(0, 2 * P)

            def exps(g):
                wait(act, shift_ready, 5 * n + 2 * g + 1)
                for j in range(4):
                    p = P_of[g][:, j, band]
                    nc.scalar.activation(p, p, ACT.Exp, bias=shift[:, 4 * g + j:4 * g + j + 1],
                                         accum_out=row_sum[:, 4 * g + j:4 * g + j + 1]).then_inc(probs_ready, 1)
                wait(act, shift_ready, 5 * n + 2 * g + 2)
                nc.scalar.activation(sink_exp[:, 4 * g:4 * g + 4], sink_shift[:, 4 * g:4 * g + 4], ACT.Exp
                                     ).then_inc(probs_ready, 1)

            def pt_copy(u):
                wait(act, turned, 3 * n + u + 1)
                wait(act, pv_done, 3 * n + u)
                bank = TURN_BANK[u]
                nc.scalar.activation(PT[:], ps[:, bank:bank + 2, :], ACT.Copy).then_inc(pt_ready, 1)

            exps(0)
            exps(1)
            wait(act, shift_ready, 5 * n + 5)
            wait(act, turned, 3 * n)
            for h in range(4):
                nc.scalar.activation(P_of[2][:, h, :], ps[:, SCORE_BANK[2] + h // 2, (h % 2) * MEM:(h % 2 + 1) * MEM], ACT.Exp,
                                     bias=shift[:, 8 + h:9 + h], accum_out=row_sum[:, 8 + h:9 + h]
                                     ).then_inc(probs_ready, 1)
            pt_copy(0)
            if last:
                wait(act, level_ready, LEVELS * NB)
                for c in range(2):
                    head_square(act, GLA_OUT + c, gla_item(c)[2], HALF)
            wait(act, k_hat_turned, n + 1)
            wait(act, kv_ready, n)
            nc.scalar.activation(k_hat_tok[:], ps[:, 6, 0:P], ACT.Copy).then_inc(k_hat_copied, 1)
            pt_copy(1)
            if not last:
                gla_exps(act, n + 1)
            else:
                for c in range(2):
                    head_root(act, GLA_OUT + c, HALF)
            wait(act, pv_done, 3 * n + 2)
            nc.scalar.activation(hT_hi[:, 0:4, blk(n)], ps[:, 2, :].rearrange("p (j t) -> p j t", j=4), ACT.Copy
                                 ).then_inc(y_hi_ready, 1)
            pt_copy(2)
            if last:
                unit_scalar(act, NPROJ)
            wait(act, o_ready, n + 1)
            nc.scalar.activation(gqk[:, :, blk(n)], ps[:, 7, 0:2 * P].rearrange("p (j t) -> p j t", j=2), ACT.Copy
                                 ).then_inc(o_copied, 1)
            wait(act, pv_done, 3 * n + 3)
            nc.scalar.activation(hT_hi[:, 6:8, blk(n)], ps[:, 1, 0:2 * P].rearrange("p (j t) -> p j t", j=2), ACT.Copy
                                 ).then_inc(y_hi_ready, 1)
            if not last:
                gla_edge_exps(act, n + 1)

        def mix_vector(dve, n, first, last):
            band = slice(P, 2 * P) if first else slice(0, 2 * P)

            def bias_max(g):
                wait(dve, scores_ready, 3 * n + g + 1)
                if not first:
                    wait(dve, turned, 3 * n - 2 + g)
                stand_alone(dve, dve_passed)
                for j in range(4):
                    h = 4 * g + j
                    s = ps[:, SCORE_BANK[g] + j // 2, (j % 2) * 2 * P + band.start:(j % 2) * 2 * P + 2 * P]
                    nc.vector.tensor_tensor_reduce(out=P_of[g][:, j, band], in0=s, in1=bias[:, h, band], scale=1.0,
                                                   scalar=sinks[:, h:h + 1], op0=ALU.add, op1=ALU.max,
                                                   accum_out=row_max[:, h:h + 1]).then_inc(biased, 1)
                wait(dve, biased, 8 * n + 4 * g + 4)
                hs = slice(4 * g, 4 * g + 4)
                nc.vector.tensor_scalar(shift[:, hs], row_max[:, hs], -1.0, None, ALU.mult).then_inc(shift_ready, 1)
                nc.vector.tensor_tensor(sink_shift[:, hs], sinks[:, hs], row_max[:, hs], ALU.subtract
                                        ).then_inc(shift_ready, 1)

            def take(l):
                wait(dve, level_ready, LEVELS * n + l + 1)
                if l:
                    wait(dve, level_taken, LEVELS * n + l)
                stand_alone(dve, dve_passed)
                nc.vector.copy_predicated(A_T[:], masks[:, l, :].unsqueeze(1).to_broadcast([P, 4, P]),
                                          ps[:, 4 + l % 4, :].rearrange("p (h q) -> p h q", h=4)
                                          ).then_inc(level_taken, 1)

            def denominators(g):
                hs = slice(4 * g, 4 * g + 4)
                wait(dve, probs_ready, 14 * n + 5 * g + 5)
                nc.vector.tensor_tensor(row_sum[:, hs], row_sum[:, hs], sink_exp[:, hs], ALU.add).then_inc(denom, 1)
                wait(dve, denom, 5 * n + 2 * g + 1)
                if not first:
                    wait(dve, scaled, 12 * n - 8 + 4 * g)
                nc.vector.reciprocal(row_inv[:, hs], row_sum[:, hs]).then_inc(denom, 1)

            def y_lo(tiles, bank, c):
                wait(dve, pv_done, 3 * n + (2, 3)[c])
                wait(dve, y_hi_ready, 2 * n + c + 1)
                w = tiles.stop - tiles.start
                nc.vector.tensor_tensor(hT_lo[:, tiles, blk(n)], ps[:, bank, 0:w * P].rearrange("p (j t) -> p j t", j=w),
                                        hT_hi[:, tiles, blk(n)].bitcast(F32), ALU.subtract).then_inc(y_lo_ready, 1)

            bias_max(0)
            bias_max(1)
            if first:
                dve.wait_ge(pads_set, 2)
                gla_pads(dve, 0, 0)
                gla_pads(dve, 0, 1)
                gla_edge_factors(dve, 0)
                dve.wait_ge(mix_set, 7)
            wait(dve, scores_ready, 3 * n + 3)
            nc.vector.tensor_reduce(shift[:, 8:12], ps[:, 2:4, :].rearrange("p a (b k) -> p (a b) k", k=MEM), AX.X,
                                    ALU.max, negate=True).then_inc(shift_ready, 1)
            denominators(0)
            denominators(1)
            wait(dve, o_ready, n)
            for l in range(LEVELS):
                take(l)
                if l == 3:
                    wait(dve, probs_ready, 14 * n + 14)
                    wait(dve, scaled, 12 * n)
                    nc.vector.reciprocal(row_inv[:, 8:12], row_sum[:, 8:12]).then_inc(denom, 1)
            if not last:
                gla_diffs(dve, n + 1)
                gla_pads(dve, n + 1, 0)
            else:
                gla_norm(dve, 0)
            y_lo(slice(0, 4), 2, 0)
            if not last:
                gla_pads(dve, n + 1, 1)
            else:
                wait(dve, head_summed, GLA_OUT + 2)
                unit_vector(dve, NPROJ)
            wait(dve, kv_ready, n + 1)
            wait(dve, o_ready, n + 1)
            for h in range(4):
                r = slice(h * GLA_DK, (h + 1) * GLA_DK)
                at = state[r, h * GLA_DV:(h + 1) * GLA_DV]
                nc.vector.scalar_tensor_tensor(out=at, in0=at, scalar=decay[r, P - 1:P],
                                               in1=ps[r, 6, h * GLA_DV:(h + 1) * GLA_DV], op0=ALU.mult,
                                               op1=ALU.add).then_inc(state_ready, 1)
            y_lo(slice(6, 8), 1, 1)
            if not last:
                gla_edge_factors(dve, n + 1)
            else:
                gla_norm(dve, 1)

        def stage_qk(sp, n, first):
            sp.dma_start(q_st[:], qT[:, :, blk(n)]).then_inc(staged_q, 16)
            for g in range(2):
                r = slice(g * HEAD, (g + 1) * HEAD)
                if first:
                    sp.dma_start(k_pad[r, g, P:2 * P], kT[r, 0:P]).then_inc(staged_k, 16)
                else:
                    sp.dma_start(k_pad[r, g, :], kT[r, bass.ds(n * P - P, 2 * P)]).then_inc(staged_k, 16)
            for g in range(2):
                r = slice(g * HEAD, (g + 1) * HEAD)
                sp.dma_start(mq_pad[r, :, :].rearrange("p (t g) c -> p t g c", g=2)[:, :, g, :], mqT[r, :, blk(n)]
                             ).then_inc(staged_mq, 16)

        def stage_v(sp, n, first):
            if first:
                sp.dma_start(v_st[:, 1, :], vg[:, 0, 0:P]).then_inc(staged_v, 16)
            else:
                sp.dma_start(v_st[:], vg[:, bass.ds(n - 1, 2), 0:P]).then_inc(staged_v, 16)

        def stage_gv(sp, n):
            sp.dma_start(gv_st[:].unsqueeze(1), vg[:, bass.ds(n, 1), P:3 * P]).then_inc(staged_gv, 16)

        def mix_sync(sp, n, first, last):
            if not last:
                wait(sp, scores_ready, 3 * n + 3)
                stage_qk(sp, n + 1, False)
                wait(sp, pv_done, 3 * n + 2)
                stage_v(sp, n + 1, False)
                wait(sp, o_ready, n + 1)
                stage_gv(sp, n + 1)

        def mix_pool(pool, n, first, last):
            wait(pool, pads_ready, 3 * n + 3)

            def scale(u):
                wait(pool, denom, 5 * n + (2, 4, 5)[u])
                stand_alone(pool, pool_passed)
                for j in range(4):
                    p = P_of[u][:, j, :]
                    nc.gpsimd.tensor_scalar(p, p, row_inv[:, 4 * u + j:4 * u + j + 1], 1.0, ALU.mult, ALU.mult
                                            ).then_inc(scaled, 1)
            scale(0)
            scale(1)
            scale(2)
            if not last:
                wait(pool, scaled, 12 * n + 12)
                gla_pads_pool(pool, n + 1)

        def mix_start_pool(pool):
            pool.wait_ge(proj_ready, NG - 2)
            pool.wait_ge(p_ready[2], NPROJ // 3)
            for t in (k_pad[:], mq_pad[:], v_st[:, 0, :], state[:], Pg0[:, :, 0:P]):
                nc.gpsimd.memset(t, 0.0).then_inc(mix_set, 1)
            pool.wait_ge(proj_ready, NG)
            for t in gq_pad:
                nc.gpsimd.memset(t[:], 0.0).then_inc(pads_set, 1)
            for t in (A_T[:], Pg1[:, :, 0:P]):
                nc.gpsimd.memset(t, 0.0).then_inc(mix_set, 1)
            pool.wait_ge(mix_set, 7)

        def gla_item(c):
            j, h = c % 2, c // 2
            cols = slice(h * HALF, (h + 1) * HALF)
            return j, cols, gqk[:, j, cols]

        def gla_hi(act, c):
            j, cols, at = gla_item(c)
            act.wait_ge(gla_gated, c + 1)
            nc.scalar.activation(hT_hi[:, 4 + j, cols], at, ACT.Copy).then_inc(gla_hi_ready, 1)

        def gla_norm(dve, c):
            j, cols, at = gla_item(c)
            head_norm(dve, GLA_OUT + c, at, head_gains[:, 4:5], HALF)
            dve.wait_ge(head_normed, GLA_OUT + c + 1)
            dve.wait_ge(out_gate_ready, 1)
            nc.vector.tensor_tensor(at, at, ggT[:, j, cols], ALU.mult).then_inc(gla_gated, 1)

        def gla_lo(dve, c):
            j, cols, at = gla_item(c)
            dve.wait_ge(gla_hi_ready, c + 1)
            nc.vector.tensor_tensor(hT_lo[:, 4 + j, cols], at, hT_hi[:, 4 + j, cols].bitcast(F32),
                                    ALU.subtract).then_inc(gla_lo_ready, 1)

        def out_tensor(pe):
            def product(g, tiles):
                m, h = g // 2, g % 2
                s = (NPROJ + m) % 3
                cols = slice(h * HALF, (h + 1) * HALF)
                pe.wait_ge(p_ready[s], (NPROJ + m) // 3 + 1)
                for k in tiles:
                    if k == 6:
                        pe.wait_ge(y_lo_ready, 2 * NB)
                    if k == 4:
                        pe.wait_ge(gla_lo_ready, 2 * h + 2)
                    kc = slice(k * P, (k + 1) * P)
                    mm = split_product(nc, ps[:, g % 4, :], p_hi[:, s, kc], p_lo[:, s, kc],
                                       hT_hi[:, k, cols], hT_lo[:, k, cols], k == 0, k == 5)
                if k == 5:
                    mm.then_inc(proj_ready, 1)

            attention, linear = (0, 1, 2, 3, 6, 7), (4, 5)
            pe.wait_ge(y_lo_ready, 2 * NB)
            pe.wait_ge(head_normed, GLA_OUT + 1)
            for g in range(4):
                if g == 3:
                    pe.wait_ge(head_normed, GLA_OUT + 2)
                product(g, attention)
                if g in (1, 2):
                    head_sum(pe, GLA_OUT + g + 1, HALF)
            for g in (0, 2, 1, 3):
                product(g, linear)
            for g in range(4, 2 * KT):
                pe.wait_ge(out_added, out_count(g - 4))
                product(g, attention + linear)

        def out_scalar(act):
            square = lambda c: head_square(act, GLA_OUT + c, gla_item(c)[2], HALF)
            root = lambda c: head_root(act, GLA_OUT + c, HALF)
            act.wait_ge(o_copied, NB)
            square(2)
            square(3)
            gla_hi(act, 0)
            unit_scalar(act, NPROJ + 1)
            root(2)
            gla_hi(act, 1)
            unit_scalar(act, NPROJ + 2)
            root(3)
            gla_hi(act, 2)
            gla_hi(act, 3)
            for m in range(KT):
                if m + 3 < KT:
                    unit_scalar(act, NPROJ + m + 3)
                elif m + 3 < KT + 2:
                    weight_hi(act, 1, ("ga", "ua")[m + 3 - KT], 0)
                if m == KT - 1:
                    for k in range(KT):
                        norm_hi(act, 2, k, 0)
                for h in range(NHALF):
                    norm_square(act, 2, m, h)

        def out_vector(dve):
            dve.wait_ge(y_lo_ready, 2 * NB)
            unit_vector(dve, NPROJ + 1)
            gla_lo(dve, 0)
            gla_lo(dve, 1)
            gla_norm(dve, 2)
            unit_vector(dve, NPROJ + 2)
            gla_lo(dve, 2)
            gla_norm(dve, 3)
            gla_lo(dve, 3)
            for i, g in enumerate(OUT_ORDER):
                m, h = g // 2, g % 2
                dve.wait_ge(proj_ready, NG + i + 1)
                nc.vector.tensor_tensor(part(xT, m, h), ps[:, g % 4, :], part(xT, m, h), ALU.add
                                        ).then_inc(out_added, 1)
                done = [u for u in range(NPROJ + 3, NPROJ + KT) if last_group[u - 3] == NG + i + 1]
                for u in done:
                    unit_vector(dve, u)
                if i in (11, 13):
                    weight_lo(dve, 1, ("ga", "ua")[(i - 11) // 2], 0)

        def x_sync(sp, pieces):
            for c in pieces:
                h, ms = c // 2, slice(4 * (c % 2), 4 * (c % 2) + 4)
                sp.dma_start(xT[:, ms, h * HALF:(h + 1) * HALF],
                             x_in.rearrange("(m p) t -> p m t", p=P)[:, ms, h * HALF:(h + 1) * HALF]
                             ).then_inc(x_landed[c], 16)

        def y_sync(sp):
            for g in range(2 * KT):
                m, h = g // NHALF, g % NHALF
                sp.wait_ge(down_added, Base(NFFN).down - 2 * KT + g + 1)
                sp.dma_start(out[m * P:(m + 1) * P, h * HALF:(h + 1) * HALF], part(xT, m, h)).then_inc(y_stored, 16)
            sp.wait_ge(y_stored, 16 * 2 * KT)

        block = ctx.enter_context(nc.Block())

        @block.sync
        def _(sp):
            x_sync(sp, (0, 1))
            load_slot(sp, 0, "ga", 0)
            load_slot(sp, 0, "ua", 0)
            x_sync(sp, (2, 3))
            load_slot(sp, 0, "gb", 0)
            load_slot(sp, 0, "ub", 0)
            for dst, src in consts:
                sp.dma_start(dst, src).then_inc(const_landed, 16)
            ffn_sync(sp, 0)
            for name in ("ga", "ua"):
                sp.wait_ge(w_ready[SLOT[name]], PAIRS)
            sp.dma_start(memT[:], mem_in.rearrange("(k p) t -> p k t", p=P)).then_inc(mem_landed, 16)
            for name in ("gb", "ub"):
                sp.wait_ge(w_ready[SLOT[name]], PAIRS)
            for u in range(NPROJ):
                unit_sync(sp, u)
            for i in range(2):
                sp.wait_ge(p_ready[i], (NPROJ - 1 - i) // 3 + 1)
            sp.wait_ge(bias_stored, 16)
            skewed = bias_dram.rearrange("(h x) -> h x", h=SWA_HEADS)[:, P - 1:P - 1 + P * (ROW - 1)]
            sp.dma_start(bias[:], skewed.rearrange("h (p u) -> p h u", u=ROW - 1)[:, :, 0:2 * P]).then_inc(bias_landed, 16)
            sp.wait_ge(head_normed, len(normed))
            sp.wait_ge(mix_set, 5)
            stage_qk(sp, 0, True)
            stage_v(sp, 0, True)
            stage_gv(sp, 0)
            each_block(sp, lambda n, first, last: mix_sync(sp, n, first, last))
            sp.wait_ge(biased, 8 * NB)
            unit_sync(sp, NPROJ)
            sp.wait_ge(turned, 3 * (NB - 1) + 1)
            unit_sync(sp, NPROJ + 1)
            unit_sync(sp, NPROJ + 2)
            sp.wait_ge(y_lo_ready, 2 * NB)
            load_slot(sp, 1, "ga", 0)
            load_slot(sp, 1, "ua", 0)
            for u in range(NPROJ + 3, NPROJ + KT):
                unit_sync(sp, u)
            for i in range(3):
                sp.wait_ge(p_ready[i], (NPROJ + KT) // 3)
            load_slot(sp, 1, "gb", 0)
            load_slot(sp, 1, "ub", 0)
            sp.wait_ge(proj_ready, NG + 2 * KT)
            ffn_sync(sp, 1)
            y_sync(sp)

        @block.gpsimd
        def _(pool):
            nc.gpsimd.memset(eps[:], EPS).then_inc(const_set, 1)
            nc.gpsimd.memset(ones[:], 1.0).then_inc(const_set, 1)
            nc.gpsimd.memset(rel_bias[:], MASKED).then_inc(const_set, 1)
            norm_pool(pool, 0)
            pool.wait_ge(bias_row_ready, 1)
            pool.dma_start(bias_dram.rearrange("(h p u) -> h p u", h=SWA_HEADS, p=P),
                           bias_row[:].unsqueeze(1).to_broadcast([SWA_HEADS, P, ROW])).then_inc(bias_stored, 16)
            for u in range(3):
                unit_vector(pool, u, nc.gpsimd)
            norm_pool(pool, 1)
            mix_start_pool(pool)
            gla_pads_pool(pool, 0)
            each_block(pool, lambda n, first, last: mix_pool(pool, n, first, last))
            norm_pool(pool, 2)

        @block.scalar
        def _(act):
            act.dma_start(gains[:], gains_in).then_inc(gains_landed, 16)
            act.wait_ge(const_set, 3)
            act.dma_start(rel_bias[0:N_BUCKETS, :], rel_bias_in).then_inc(rel_bias_landed, 16)
            act.dma_start(bucket_of[:], bucket_of_in).then_inc(rel_bias_landed, 16)
            act.wait_ge(gains_landed, 16)
            for m in range(KT // 2):
                norm_hi(act, 0, m, 0)
            norm_square(act, 0, 0, 0)
            norm_square(act, 0, 1, 0)
            for m in range(KT // 2, KT):
                norm_hi(act, 0, m, 0)
            weight_hi(act, 0, "ga", 0)
            weight_hi(act, 0, "ua", 0)
            for m in range(2, KT):
                norm_square(act, 0, m, 0)
                norm_hi(act, 0, m - 2, 1)
            norm_hi(act, 0, KT - 2, 1)
            norm_hi(act, 0, KT - 1, 1)
            for m in range(KT):
                norm_square(act, 0, m, 1)
            act.wait_ge(const_landed, 16 * NCONST)
            act.wait_ge(masks_ready, 1)
            act.wait_ge(bias_stored, 16)
            ffn_scalar(act, 0)
            for m, h in norm_steps(1):
                norm_hi(act, 1, m, h)
                norm_square(act, 1, m, h)
            proj_scalar(act)
            gla_exps(act, 0)
            gla_edge_exps(act, 0)
            act.wait_ge(proj_taken, NG)
            nc.scalar.activation(ggT[:], ggT[:], ACT.Silu).then_inc(out_gate_ready, 1)
            each_block(act, lambda n, first, last: mix_scalar(act, n, first, last))
            out_scalar(act)
            for m in range(KT):
                norm_hi(act, 2, m, 1)
            ffn_scalar(act, 1)

        @block.vector
        def _(dve):
            dve.wait_ge(gains_landed, 16)
            for m in range(KT):
                norm_vector(dve, 0, m, 0)
                if m == KT // 2:
                    dve.wait_ge(bias_row_summed, 1)
                    nc.vector.tensor_copy(bias_row[:], ps[0:SWA_HEADS, BANK_DOWN, 0:ROW]).then_inc(bias_row_ready, 1)
            weight_lo(dve, 0, "ga", 0)
            weight_lo(dve, 0, "ua", 0)
            for m in range(KT):
                norm_vector(dve, 0, m, 1)
            dve.wait_ge(const_landed, 16 * NCONST)
            nc.vector.tensor_copy(masks[:], masks_f[:]).then_inc(masks_ready, 1)
            for c in (0, 2):
                nc.vector.tensor_scalar(head_gains[:, c:c + 1], head_gains[:, c:c + 1], float(HEAD) ** -0.5, None,
                                        ALU.mult).then_inc(gains_scaled, 1)
            dve.wait_ge(gains_scaled, 2)
            sumsq0_vector(dve)
            ffn_vector(dve, 0)
            for g in range(2 * KT):
                down_add(dve, 0, PAIRS - 1, g)
                if g >= 2:
                    norm_vector(dve, 1, *norm_steps(1)[g - 2])
            for g in (2 * KT - 2, 2 * KT - 1):
                norm_vector(dve, 1, *norm_steps(1)[g])
            proj_vector(dve)
            dve.wait_ge(gate_scanned, NB)
            dve.wait_ge(bias_landed, 16)
            each_block(dve, lambda n, first, last: mix_vector(dve, n, first, last))
            out_vector(dve)
            for m, h in norm_steps(2):
                norm_vector(dve, 2, m, h)
            ffn_vector(dve, 1)
            for g in range(2 * KT):
                down_add(dve, Base(1).down, PAIRS - 1, g)

        @block.tensor
        def _(pe):
            pe.wait_ge(const_set, 3)
            pe.wait_ge(rel_bias_landed, 32)
            nc.tensor.matmul(ps[0:SWA_HEADS, BANK_DOWN, 0:ROW], rel_bias[:, :], bucket_of[:, :], start=True, stop=True
                             ).then_inc(bias_row_summed, 1)
            ffn_tensor(pe, 0)
            pe.wait_ge(const_landed, 16 * NCONST)
            proj_tensor(pe)
            pe.wait_ge(proj_taken, NG)
            each_block(pe, lambda n, first, last: mix_tensor(pe, n, first, last))
            out_tensor(pe)
            ffn_tensor(pe, 1)


def _columns(w):
    return np.ascontiguousarray(w.reshape(KT, P, -1, P).transpose(2, 1, 0, 3)).reshape(-1, D)


def _bucket_of():
    exact = N_BUCKETS // 2
    hot = np.zeros((N_BUCKETS + 1, ROW), np.float32)
    for u in range(ROW):
        dist = 2 * P - 1 - u
        if not 0 <= dist < P:
            hot[N_BUCKETS, u] = 1
            continue
        large = exact + int(np.float32(np.log(np.float32(max(dist, 1) / exact))) / np.float32(np.log(MAX_DISTANCE / exact))
                            * (N_BUCKETS - exact))
        hot[dist if dist < exact else min(large, N_BUCKETS - 1), u] = 1
    return hot


def _masks():
    i, j = np.arange(P)[None, :], np.arange(P)[:, None]
    out = np.zeros((P, LEVELS, P), np.float32)
    for l in range(LEVELS):
        s = P >> (l + 1)
        out[:, l, :] = (i // (2 * s) == j // (2 * s)) & (i % (2 * s) >= s) & (j % (2 * s) < s) if s else i == j
    return out


def kernel(**inputs):
    import concourse.bacc as _bacc
    from concourse.bass_utils import run_bass_kernel_spmd as _run

    a = {n: np.asarray(v) for n, v in inputs.items()}
    w_in = a["w_in"][0]
    at = {"q": 0, "k": 512, "v": 640, "gq": 768, "gk": 896, "gv": 1024, "gg": 1280, "glr": 1536, "mq": 1552}

    def columns_of(n):
        if n[0] == "q":
            j = int(n[1])
            return np.r_[HEAD * j:HEAD * (j + 1), 4 * HEAD + HEAD * j:4 * HEAD + HEAD * (j + 1)]
        base = n.rstrip("0123")
        start = at[base] + P * int(n[len(base):] or 0)
        return np.arange(start, start + P)

    picked = np.concatenate([columns_of(n) for n in PROJ if n[:2] not in ("mk", "mv")])
    w_out = a["w_out"][0]
    swa_rows = w_out[:SWA_HEADS * HEAD].reshape(2, 4, HEAD, D).transpose(1, 0, 2, 3).reshape(-1, D)
    per_tile = lambda g: g.reshape(-1, KT, P).transpose(2, 0, 1)
    twice = lambda g: np.concatenate([g, g])
    arrays = {
        "x": a["x"][0].T,
        "mem": a["mem"][0].T,
        "w_gate1": _columns(a["ffn1_w_gate"][0]), "w_up1": _columns(a["ffn1_w_up"][0]), "w_down1": a["ffn1_w_down"][0],
        "w_proj": _columns(w_in[:, picked]),
        "w_mem": _columns(a["w_mem_kv"][0]),
        "w_out": _columns(np.concatenate([swa_rows, w_out[SWA_HEADS * HEAD:]])),
        "w_gate2": _columns(a["ffn2_w_gate"][0]), "w_up2": _columns(a["ffn2_w_up"][0]), "w_down2": a["ffn2_w_down"][0],
        "gains": per_tile(np.stack([a["ffn1_norm"][0], a["mix_norm"][0], a["ffn2_norm"][0]])),
        "mem_gain": per_tile(a["mem_norm"][0])[:, 0],
        "head_gains": np.stack([twice(a[n][0]) for n in ("swa_q_norm", "swa_k_norm", "mem_q_norm", "mem_k_norm",
                                                         "gla_out_norm")], axis=1),
        "sinks": a["swa_sinks"][0],
        "rel_bias": a["rel_bias"],
        "bucket_of": _bucket_of(),
        "gate_up": a["gla_w_gate_up"][0],
        "gate_bias": a["gla_b_gate"][0][:, None],
        "masks": _masks(),
        "ident": np.eye(P, dtype=np.float32),
        "head_ones": np.kron(np.eye(2, dtype=np.float32), np.ones((HEAD, HEAD), np.float32)),
    }
    nc = _bacc.Bacc("TRN2", target_bir_lowering=False, num_devices=1)
    feeds, args = {}, []
    for name, v in arrays.items():
        v = np.ascontiguousarray(v)
        feeds[f"in_{name}"] = v
        args.append(nc.dram_tensor(f"in_{name}", v.shape, mybir.dt.from_np(v.dtype), kind="ExternalInput").ap())
    args.append(nc.dram_tensor("out_y", (D, T), F32, kind="ExternalOutput").ap())
    build(nc, *args)
    r = _run(nc, [feeds], core_ids=[0])
    return np.ascontiguousarray(r.results[0]["out_y"].T)[None]
```
